# Optimizing a Trainium2 kernel written in Bass

```python
import math
import jax, jax.numpy as jnp
from jax import lax
import numpy as np

D_MODEL = 2048
BATCH = 1
SEQ = 256
DEPTH = 1

CHUNK = 64
N_MIXERS = 4
CONV_KERNEL = 31
LN_EPS = 1e-5
RWKV_HEAD_DIM = 64
RWKV_HEADS = D_MODEL // RWKV_HEAD_DIM
DECAY_LORA = 96
AAA_LORA = 96
GATE_LORA = 256
GN_EPS = 64e-5
SHORT_KERNEL = 3
FOX_HEAD_DIM = 128
FOX_HEADS = D_MODEL // FOX_HEAD_DIM
Q_BLOCK = 128
D_FF = 4 * D_MODEL
RMS_EPS = 1e-6


def _n_layers_of(m):
    return (DEPTH - m + N_MIXERS - 1) // N_MIXERS

def rmsnorm(x, g):
    xf = x.astype(jnp.float32)
    y = xf * lax.rsqrt(jnp.mean(xf * xf, axis=-1, keepdims=True) + RMS_EPS)
    return (y * g.astype(jnp.float32)).astype(x.dtype)

def layernorm(x, g, b):
    xf = x.astype(jnp.float32)
    mu = jnp.mean(xf, axis=-1, keepdims=True)
    var = jnp.mean(jnp.square(xf - mu), axis=-1, keepdims=True)
    y = (xf - mu) * lax.rsqrt(var + LN_EPS)
    return (y * g.astype(jnp.float32) + b.astype(jnp.float32)).astype(x.dtype)

def causal_dwconv(x, w):
    K = w.shape[0]
    return lax.conv_general_dilated(
        x, w[:, None, :].astype(x.dtype), window_strides=(1,), padding=[(K - 1, 0)],
        dimension_numbers=('NWC', 'WIO', 'NWC'), feature_group_count=x.shape[-1])

def conformer_conv(h, w_in, b_in, dw, dw_b, ln_g, ln_b, w_out, b_out):
    u = h @ w_in + b_in
    val, gate = jnp.split(u, 2, axis=-1)
    u = val * jax.nn.sigmoid(gate)
    u = causal_dwconv(u, dw) + dw_b
    u = jax.nn.silu(layernorm(u, ln_g, ln_b))
    return u @ w_out + b_out

def rwkv7_time_mix(h, mu, w_rkv, w0, w1, w2, a0, a1, a2, g1, g2, k_k, k_a, r_k, gn_g, gn_b, w_o):
    B, T, D = h.shape
    H, N = RWKV_HEADS, RWKV_HEAD_DIM
    f32 = jnp.float32
    xx = jnp.pad(h, ((0, 0), (1, 0), (0, 0)))[:, :T] - h
    xr, xw, xk, xv, xa, xg = (h + xx * mu[i] for i in range(6))
    r = xr @ w_rkv[0]
    k = xk @ w_rkv[1]
    v = xv @ w_rkv[2]
    w = -jax.nn.softplus(-(w0 + jnp.tanh(xw @ w1) @ w2).astype(f32)) - 0.5
    a = jax.nn.sigmoid(a0 + (xa @ a1) @ a2)
    g = jax.nn.sigmoid(xg @ g1) @ g2
    kk = (k * k_k).astype(f32).reshape(B, T, H, N)
    kk = kk / jnp.maximum(jnp.sqrt(jnp.sum(kk * kk, axis=-1, keepdims=True)), 1e-12)
    k = k * (1 + (a - 1) * k_a)

    def heads(t):
        return t.astype(f32).reshape(B, T, H, N)

    r_h, k_h, v_h, a_h = heads(r), heads(k), heads(v), heads(a)
    decay = jnp.exp(-jnp.exp(w)).reshape(B, T, H, N)

    def to_chunks(t):
        return t.transpose(1, 0, 2, 3).reshape(T // CHUNK, CHUNK, B, H, N)

    xs = tuple(to_chunks(t) for t in (r_h, decay, k_h, v_h, -kk, kk * a_h))

    def frame_step(S, inp):
        r_t, w_t, k_t, v_t, a_t, b_t = inp
        sa = jnp.einsum('bhij,bhj->bhi', S, a_t)
        S = S * w_t[:, :, None, :] + sa[..., None] * b_t[:, :, None, :] + v_t[..., None] * k_t[:, :, None, :]
        y = jnp.einsum('bhij,bhj->bhi', S, r_t)
        return S, y

    def chunk_step(S, chunk):
        return lax.scan(frame_step, S, chunk)

    S0 = jnp.zeros((B, H, N, N), f32)
    _, y = lax.scan(chunk_step, S0, xs)
    y = y.reshape(T, B, H, N).transpose(1, 0, 2, 3)
    mean = jnp.mean(y, axis=-1, keepdims=True)
    var = jnp.mean(jnp.square(y - mean), axis=-1, keepdims=True)
    y = ((y - mean) * lax.rsqrt(var + GN_EPS)).reshape(B, T, D) * gn_g.astype(f32) + gn_b.astype(f32)
    bonus = (jnp.sum(r_h * k_h * r_k.astype(f32), axis=-1, keepdims=True) * v_h).reshape(B, T, D)
    y = (y + bonus).astype(h.dtype)
    return (y * g) @ w_o

def short_conv(h, w_in, conv_w, w_out):
    u = h @ w_in
    gate_b, gate_c, hv = jnp.split(u, 3, axis=-1)
    z = causal_dwconv(gate_c * hv, conv_w)
    return (gate_b * z) @ w_out

def fox_attention(h, w_qkvf, b_f, w_o):
    B, T, D = h.shape
    H, Dh = FOX_HEADS, FOX_HEAD_DIM
    f32 = jnp.float32
    u = h @ w_qkvf

    def heads(t):
        return t.reshape(B, T, H, Dh).transpose(0, 2, 1, 3)

    q, k, v = heads(u[..., :D]), heads(u[..., D:2 * D]), heads(u[..., 2 * D:3 * D])
    log_f = jax.nn.log_sigmoid((u[..., 3 * D:] + b_f).astype(f32))
    c = jnp.cumsum(log_f, axis=1).transpose(0, 2, 1)
    scale = 1.0 / math.sqrt(Dh)
    outs = []
    for blk in range(T // Q_BLOCK):
        q0 = blk * Q_BLOCK
        q1 = q0 + Q_BLOCK
        s = jnp.einsum('bhqd,bhkd->bhqk', q[:, :, q0:q1], k[:, :, :q1]).astype(f32) * scale
        s = s + c[:, :, q0:q1, None] - c[:, :, None, :q1]
        mask = (q0 + jnp.arange(Q_BLOCK))[:, None] >= jnp.arange(q1)[None, :]
        s = jnp.where(mask, s, -jnp.inf)
        p = jax.nn.softmax(s, axis=-1).astype(v.dtype)
        outs.append(jnp.einsum('bhqk,bhkd->bhqd', p, v[:, :, :q1]))
    o = jnp.concatenate(outs, axis=2).transpose(0, 2, 1, 3).reshape(B, T, D)
    return o @ w_o

def sq_relu_mlp(h, w1, w2):
    return jnp.square(jax.nn.relu(h @ w1)) @ w2

def first_inputs(seed: int = 0) -> dict:
    key = jax.random.key(seed)
    ks = iter(jax.random.split(key, 48))
    D = D_MODEL
    nA, nB, nC, nD = (_n_layers_of(m) for m in range(N_MIXERS))
    H, N = RWKV_HEADS, RWKV_HEAD_DIM

    def nrm(shape, scale):
        return jax.random.normal(next(ks), shape, jnp.float32) * scale

    def gain(shape):
        return 1.0 + nrm(shape, 0.02)

    inp = {}
    inp["x"] = nrm((BATCH, SEQ, D), 1.0)
    inp["norm1_g"] = gain((DEPTH, D))
    inp["norm2_g"] = gain((DEPTH, D))
    inp["mlp_w1"] = nrm((DEPTH, D, D_FF), D ** -0.5)
    inp["mlp_w2"] = nrm((DEPTH, D_FF, D), D_FF ** -0.5)
    inp["cc_w_in"] = nrm((nA, D, 2 * D), D ** -0.5)
    inp["cc_b_in"] = nrm((nA, 2 * D), 0.02)
    inp["cc_dw"] = nrm((nA, CONV_KERNEL, D), CONV_KERNEL ** -0.5)
    inp["cc_dw_b"] = nrm((nA, D), 0.02)
    inp["cc_ln_g"] = gain((nA, D))
    inp["cc_ln_b"] = nrm((nA, D), 0.02)
    inp["cc_w_out"] = nrm((nA, D, D), D ** -0.5)
    inp["cc_b_out"] = nrm((nA, D), 0.02)
    inp["rw_mu"] = jax.random.uniform(next(ks), (nB, 6, D), jnp.float32)
    inp["rw_w_rkv"] = nrm((nB, 3, D, D), D ** -0.5)
    inp["rw_w0"] = jax.random.uniform(next(ks), (nB, D), jnp.float32, -6.0, -1.0)
    inp["rw_w1"] = nrm((nB, D, DECAY_LORA), D ** -0.5)
    inp["rw_w2"] = nrm((nB, DECAY_LORA, D), 0.5 * DECAY_LORA ** -0.5)
    inp["rw_a0"] = nrm((nB, D), 0.02)
    inp["rw_a1"] = nrm((nB, D, AAA_LORA), D ** -0.5)
    inp["rw_a2"] = nrm((nB, AAA_LORA, D), AAA_LORA ** -0.5)
    inp["rw_g1"] = nrm((nB, D, GATE_LORA), D ** -0.5)
    inp["rw_g2"] = nrm((nB, GATE_LORA, D), GATE_LORA ** -0.5)
    inp["rw_k_k"] = 0.85 + nrm((nB, D), 0.1)
    inp["rw_k_a"] = 1.0 + nrm((nB, D), 0.1)
    inp["rw_r_k"] = nrm((nB, H, N), 0.1)
    inp["rw_gn_g"] = gain((nB, D))
    inp["rw_gn_b"] = nrm((nB, D), 0.02)
    inp["rw_w_o"] = nrm((nB, D, D), D ** -0.5)
    inp["sc_w_in"] = nrm((nC, D, 3 * D), D ** -0.5)
    inp["sc_conv_w"] = nrm((nC, SHORT_KERNEL, D), SHORT_KERNEL ** -0.5)
    inp["sc_w_out"] = nrm((nC, D, D), D ** -0.5)
    w_qkv = nrm((nD, D, 3 * D), D ** -0.5)
    w_f = nrm((nD, D, FOX_HEADS), 0.1 * D ** -0.5)
    inp["fx_w_qkvf"] = jnp.concatenate([w_qkv, w_f], axis=-1)
    inp["fx_b_f"] = jax.random.uniform(next(ks), (nD, FOX_HEADS), jnp.float32, 1.0, 5.0)
    inp["fx_w_o"] = nrm((nD, D, D), D ** -0.5)
    inp["final_g"] = gain((D,))
    return inp

def first_block(x, norm1_g, norm2_g, mlp_w1, mlp_w2,
              cc_w_in, cc_b_in, cc_dw, cc_dw_b, cc_ln_g, cc_ln_b, cc_w_out, cc_b_out,
              rw_mu, rw_w_rkv, rw_w0, rw_w1, rw_w2, rw_a0, rw_a1, rw_a2, rw_g1, rw_g2,
              rw_k_k, rw_k_a, rw_r_k, rw_gn_g, rw_gn_b, rw_w_o,
              sc_w_in, sc_conv_w, sc_w_out,
              fx_w_qkvf, fx_b_f, fx_w_o, final_g):
    for i in range(DEPTH):
        m, j = i % N_MIXERS, i // N_MIXERS
        h = rmsnorm(x, norm1_g[i])
        if m == 0:
            y = conformer_conv(h, cc_w_in[j], cc_b_in[j], cc_dw[j], cc_dw_b[j],
                               cc_ln_g[j], cc_ln_b[j], cc_w_out[j], cc_b_out[j])
        elif m == 1:
            y = rwkv7_time_mix(h, rw_mu[j], rw_w_rkv[j], rw_w0[j], rw_w1[j], rw_w2[j],
                               rw_a0[j], rw_a1[j], rw_a2[j], rw_g1[j], rw_g2[j],
                               rw_k_k[j], rw_k_a[j], rw_r_k[j], rw_gn_g[j], rw_gn_b[j], rw_w_o[j])
        elif m == 2:
            y = short_conv(h, sc_w_in[j], sc_conv_w[j], sc_w_out[j])
        else:
            y = fox_attention(h, fx_w_qkvf[j], fx_b_f[j], fx_w_o[j])
        x = x + y
        x = x + sq_relu_mlp(rmsnorm(x, norm2_g[i]), mlp_w1[i], mlp_w2[i])
    return rmsnorm(x, final_g)


D_MIX = D_MODEL
D_POOL = D_MIX // 2
POOL_WINDOWS = (2, 4, 8, 16)
N_POOL_GROUPS = len(POOL_WINDOWS)
POOL_GROUP = D_POOL // N_POOL_GROUPS
D_ATTN = D_MIX - D_POOL
N_HEADS = 8
HEAD_DIM = D_ATTN // N_HEADS
IDX_HEADS = 16
IDX_DIM = 64
INDEXER_SCALE = (IDX_HEADS * IDX_DIM) ** -0.5
MAX_TOPK = 256
N_BUCKETS = 32
MAX_DISTANCE = 128
PEER_HEADS = 8
PEER_KEYS = 128
N_EXPERTS = PEER_KEYS * PEER_KEYS
PEER_QDIM = 256
PEER_HALF = PEER_QDIM // 2
PEER_TOPK = 16
PEER_CHUNK = 128
ALPHA = (2 * DEPTH) ** 0.25
BETA = (8 * DEPTH) ** -0.25
NEG_INF = -1e30

SPLIT_SIZES = (D_POOL, D_ATTN, D_ATTN, D_ATTN, IDX_HEADS * IDX_DIM, IDX_DIM, IDX_HEADS)
D_IN = sum(SPLIT_SIZES)


def layer_norm(x, g, b):
    xf = x.astype(jnp.float32)
    mu = jnp.mean(xf, axis=-1, keepdims=True)
    var = jnp.mean(jnp.square(xf - mu), axis=-1, keepdims=True)
    y = (xf - mu) * lax.rsqrt(var + LN_EPS)
    return (y * g.astype(jnp.float32) + b.astype(jnp.float32)).astype(x.dtype)

def split_columns(proj):
    parts, start = [], 0
    for size in SPLIT_SIZES:
        parts.append(proj[..., start:start + size])
        start += size
    return parts

def pool_mixer(v, pool_w, pool_scale):
    B, S, _ = v.shape
    vg = v.reshape(B, S, N_POOL_GROUPS, POOL_GROUP)
    c = jnp.cumsum(vg.astype(jnp.float32), axis=1)
    c = jnp.pad(c, ((0, 0), (1, 0), (0, 0), (0, 0)))
    pos = jnp.arange(S)
    means = []
    for g, w in enumerate(POOL_WINDOWS):
        cg = c[:, :, g]
        hi = cg[:, 1:]
        lo = cg[:, jnp.maximum(pos + 1 - w, 0)]
        cnt = jnp.minimum(pos + 1, w).astype(jnp.float32)[None, :, None]
        means.append((hi - lo) / cnt)
    pooled = jnp.stack(means, axis=2).astype(v.dtype) - vg
    mixed = jnp.einsum('bsgc,gcd->bsgd', pooled, pool_w)
    return mixed.reshape(B, S, D_POOL) * pool_scale

def t5_bucket(dist):
    max_exact = N_BUCKETS // 2
    d = jnp.maximum(dist, 1).astype(jnp.float32)
    large = max_exact + (jnp.log(d / max_exact) / math.log(MAX_DISTANCE / max_exact)
                         * (N_BUCKETS - max_exact)).astype(jnp.int32)
    large = jnp.minimum(large, N_BUCKETS - 1)
    return jnp.where(dist < max_exact, dist, large)

def sparse_attention(q, k, v, q_idx, k_idx, w_idx, rel_bias):
    B, S = q.shape[:2]
    top_k = min(MAX_TOPK, S // 4)
    n_blocks = S // Q_BLOCK
    b_ix = jnp.arange(B)[:, None, None]
    key_pos = jnp.arange(S)

    def block(i):
        start = i * Q_BLOCK
        qi = lax.dynamic_slice_in_dim(q_idx, start, Q_BLOCK, axis=1)
        wi = lax.dynamic_slice_in_dim(w_idx, start, Q_BLOCK, axis=1)
        qa = lax.dynamic_slice_in_dim(q, start, Q_BLOCK, axis=1)
        q_pos = start + jnp.arange(Q_BLOCK)
        rel = jax.nn.relu(jnp.einsum('bqhd,bsd->bqhs', qi, k_idx))
        score = jnp.einsum('bqh,bqhs->bqs', wi, rel).astype(jnp.float32) * INDEXER_SCALE
        causal = key_pos[None, :] <= q_pos[:, None]
        score = jnp.where(causal[None], score, NEG_INF)
        _, sel = lax.top_k(score, top_k)
        k_sel = k[b_ix, sel]
        v_sel = v[b_ix, sel]
        logits = jnp.einsum('bqhd,bqkhd->bhqk', qa, k_sel).astype(jnp.float32) * HEAD_DIM ** -0.5
        dist = q_pos[None, :, None] - sel
        bias = rel_bias[t5_bucket(jnp.maximum(dist, 0))]
        logits = logits + jnp.transpose(bias, (0, 3, 1, 2)).astype(jnp.float32)
        logits = jnp.where((dist >= 0)[:, None], logits, NEG_INF)
        p = jax.nn.softmax(logits, axis=-1).astype(v.dtype)
        return jnp.einsum('bhqk,bqkhd->bqhd', p, v_sel)

    out = lax.map(block, jnp.arange(n_blocks))
    return jnp.transpose(out, (1, 0, 2, 3, 4)).reshape(B, S, N_HEADS * HEAD_DIM)

def peer_ffn(x, wq, sub_keys, u, v):
    B, S, D = x.shape
    xt = x.reshape(-1, PEER_CHUNK, D)

    def chunk(xc):
        qh = (xc @ wq).reshape(PEER_CHUNK, PEER_HEADS, 2, PEER_HALF)
        s1 = jnp.einsum('thd,kd->thk', qh[:, :, 0], sub_keys[0]).astype(jnp.float32)
        s2 = jnp.einsum('thd,kd->thk', qh[:, :, 1], sub_keys[1]).astype(jnp.float32)
        v1, i1 = lax.top_k(s1, PEER_TOPK)
        v2, i2 = lax.top_k(s2, PEER_TOPK)
        cand = (v1[..., :, None] + v2[..., None, :]).reshape(PEER_CHUNK, PEER_HEADS, PEER_TOPK * PEER_TOPK)
        cidx = (i1[..., :, None] * PEER_KEYS + i2[..., None, :]).reshape(PEER_CHUNK, PEER_HEADS, PEER_TOPK * PEER_TOPK)
        best, pos = lax.top_k(cand, PEER_TOPK)
        expert = jnp.take_along_axis(cidx, pos, axis=-1)
        gate = jax.nn.softmax(best, axis=-1)
        u_sel = u[expert]
        v_sel = v[expert]
        act = jax.nn.gelu(jnp.einsum('td,thkd->thk', xc, u_sel).astype(jnp.float32), approximate=False)
        return jnp.einsum('thk,thkd->td', (gate * act).astype(x.dtype), v_sel)

    return lax.map(chunk, xt).reshape(B, S, D)

def second_inputs(seed: int = 0) -> dict:
    key = jax.random.key(seed)
    ks = jax.random.split(key, 16)
    f32 = jnp.float32
    L = DEPTH
    x = jax.random.normal(ks[0], (BATCH, SEQ, D_MODEL), f32)
    w_in = jax.random.normal(ks[1], (L, D_MODEL, D_IN), f32) * D_MODEL ** -0.5
    pool_w = jax.random.normal(ks[2], (L, N_POOL_GROUPS, POOL_GROUP, POOL_GROUP), f32) * POOL_GROUP ** -0.5
    pool_scale = 1.0 + 0.1 * jax.random.normal(ks[3], (L, D_POOL), f32)
    rel_bias = 0.5 * jax.random.normal(ks[4], (N_BUCKETS, N_HEADS), f32)
    w_out = jax.random.normal(ks[5], (L, D_MIX, D_MODEL), f32) * (D_MIX ** -0.5 * BETA)
    ln1_g = 1.0 + 0.05 * jax.random.normal(ks[6], (L, D_MODEL), f32)
    ln1_b = 0.02 * jax.random.normal(ks[7], (L, D_MODEL), f32)
    peer_wq = jax.random.normal(ks[8], (L, D_MODEL, PEER_HEADS * PEER_QDIM), f32) * D_MODEL ** -0.5
    peer_subkeys = jax.random.normal(ks[9], (L, 2, PEER_KEYS, PEER_HALF), f32) * PEER_HALF ** -0.5
    peer_u = jax.random.normal(ks[10], (L, N_EXPERTS, D_MODEL), f32) * D_MODEL ** -0.5
    peer_v = jax.random.normal(ks[11], (L, N_EXPERTS, D_MODEL), f32) * (BETA * PEER_HEADS ** -0.5)
    ln2_g = 1.0 + 0.05 * jax.random.normal(ks[12], (L, D_MODEL), f32)
    ln2_b = 0.02 * jax.random.normal(ks[13], (L, D_MODEL), f32)
    return {"x": x, "w_in": w_in, "pool_w": pool_w, "pool_scale": pool_scale,
            "rel_bias": rel_bias, "w_out": w_out, "ln1_g": ln1_g, "ln1_b": ln1_b,
            "peer_wq": peer_wq, "peer_subkeys": peer_subkeys, "peer_u": peer_u,
            "peer_v": peer_v, "ln2_g": ln2_g, "ln2_b": ln2_b}

def second_block(x, w_in, pool_w, pool_scale, rel_bias, w_out, ln1_g, ln1_b,
              peer_wq, peer_subkeys, peer_u, peer_v, ln2_g, ln2_b):
    B, S, _ = x.shape
    h = x
    for l in range(DEPTH):
        proj = h @ w_in[l]
        p_pool, p_q, p_k, p_v, p_qi, p_ki, p_wi = split_columns(proj)
        out_pool = pool_mixer(p_pool, pool_w[l], pool_scale[l])
        out_attn = sparse_attention(
            p_q.reshape(B, S, N_HEADS, HEAD_DIM),
            p_k.reshape(B, S, N_HEADS, HEAD_DIM),
            p_v.reshape(B, S, N_HEADS, HEAD_DIM),
            p_qi.reshape(B, S, IDX_HEADS, IDX_DIM), p_ki, p_wi, rel_bias)
        mix = jnp.concatenate([out_pool, out_attn], axis=-1) @ w_out[l]
        h = layer_norm(ALPHA * h + mix, ln1_g[l], ln1_b[l])
        ffn = peer_ffn(h, peer_wq[l], peer_subkeys[l], peer_u[l], peer_v[l])
        h = layer_norm(ALPHA * h + ffn, ln2_g[l], ln2_b[l])
    return h


def setup_inputs(seed=0):
    out = dict(first_inputs(seed))
    for name, value in second_inputs(seed + 1).items():
        if name != "x":
            out[name + "_2"] = value
    return out


def reference(
    x, norm1_g, norm2_g, mlp_w1, mlp_w2, cc_w_in, cc_b_in, cc_dw, cc_dw_b, cc_ln_g, cc_ln_b,
    cc_w_out, cc_b_out, rw_mu, rw_w_rkv, rw_w0, rw_w1, rw_w2, rw_a0, rw_a1, rw_a2, rw_g1, rw_g2,
    rw_k_k, rw_k_a, rw_r_k, rw_gn_g, rw_gn_b, rw_w_o, sc_w_in, sc_conv_w, sc_w_out, fx_w_qkvf,
    fx_b_f, fx_w_o, final_g, w_in_2, pool_w_2, pool_scale_2, rel_bias_2, w_out_2, ln1_g_2,
    ln1_b_2, peer_wq_2, peer_subkeys_2, peer_u_2, peer_v_2, ln2_g_2, ln2_b_2,
):
    x = first_block(
        x, norm1_g, norm2_g, mlp_w1, mlp_w2, cc_w_in, cc_b_in, cc_dw, cc_dw_b, cc_ln_g, cc_ln_b,
        cc_w_out, cc_b_out, rw_mu, rw_w_rkv, rw_w0, rw_w1, rw_w2, rw_a0, rw_a1, rw_a2, rw_g1,
        rw_g2, rw_k_k, rw_k_a, rw_r_k, rw_gn_g, rw_gn_b, rw_w_o, sc_w_in, sc_conv_w, sc_w_out,
        fx_w_qkvf, fx_b_f, fx_w_o, final_g,
    )
    return second_block(
        x, w_in_2, pool_w_2, pool_scale_2, rel_bias_2, w_out_2, ln1_g_2, ln1_b_2, peer_wq_2,
        peer_subkeys_2, peer_u_2, peer_v_2, ln2_g_2, ln2_b_2,
    )


_drawn_inputs = setup_inputs


def setup_inputs(seed=0):
    import zlib

    import numpy as np

    out = dict(_drawn_inputs(seed))
    spreads = {}
    factors = {'norm1_g': 3.041,
     'cc_b_in': 3.117,
     'cc_ln_g': 2.944,
     'cc_ln_b': 3.298,
     'ln2_b_2': 2.79,
     'norm2_g': 3.358,
     'cc_dw_b': 3.354,
     'cc_b_out': 3.996}
    for name, (base, spread) in spreads.items():
        noise = np.random.default_rng([zlib.crc32(name.encode()), seed]).standard_normal(out[name].shape)
        drawn = base * np.exp(spread * noise) if base else spread * noise
        out[name] = __import__('jax').numpy.asarray(drawn.astype(out[name].dtype))
    for name, factor in factors.items():
        out[name] = (out[name] * factor).astype(out[name].dtype)
    return out
```

```python
from contextlib import ExitStack

import concourse.bass as bass
from concourse import mybir

F32 = mybir.dt.float32
F32R = mybir.dt.float32r
U32 = mybir.dt.uint32
ACT = mybir.ActivationFunctionType
ALU = mybir.AluOpType
AX = mybir.AxisListType.X

P = 128
TOK = 256
NT = TOK // P
D = 2048
KT = D // P
D_FF = 4 * D
TAPS = 31
PAD = TAPS - 1
LN_EPS, RMS_EPS = 1e-5, 1e-6
ALPHA = 2 ** 0.25
HEADS = 8
IDX_HEADS = 16
IDX_DIM = 64
IDX_SCALE = (IDX_HEADS * IDX_DIM) ** -0.5
TOPK = 64
NEG = -1e30
TAKEN = -3e38
WINDOWS = (2, 4, 8, 16)
BUCKETS = 32
PEER_HEADS = 8
PEER_TOPK = 16
KEYS = 128
SLOTS = PEER_HEADS * PEER_TOPK
RING = 8

G_IN, G_OUT, G_MLP, G_PROJ, G_MIX, G_QRY, G_END = 0, 8, 12, 44, 54, 58, 62
SUBS = 8

C_ID, C_ONE, C_CAUSAL, C_CNT, C_HOT, C_IOTA, C_END = 0, 128, 256, 768, 1792, 2176, 2192
V_N1, V_N2, V_FIN, V_BV, V_BG, V_DWB, V_LNG, V_LNB, V_BOUT, V_L1G, V_L1B, V_PSC, V_END = (
    0, 16, 32, 48, 64, 80, 96, 112, 128, 144, 160, 176, 184)


def build(nc, a, out):
    with ExitStack() as ctx:
        def sem(name):
            return ctx.enter_context(nc.semaphore(name))

        

        def at(name, offset, shape, dtype=F32):
            return nc.alloc_sbuf_tensor_at(name, [shape[0], *shape[1:]], dtype, offset=offset)

        KB = 1024
        base = (nc.sbuf_base + 63) // 64 * 64
        o_x, o_t, o_ah, o_al = base, base + 16 * KB, base + 32 * KB, base + 48 * KB
        o_raw, o_hi, o_lo = base + 64 * KB, base + 96 * KB, base + 112 * KB
        o_z = base + 128 * KB
        o_c = o_z + 64 * KB

        X = at("X", o_x, [P, KT, TOK])
        T = at("T", o_t, [P, KT, TOK])
        A_hi = at("A_hi", o_ah, [P, KT, TOK], F32R)
        A_lo = at("A_lo", o_al, [P, KT, TOK], F32R)
        raw = at("raw", o_raw, [P, 4, 4, 512])
        w_hi = at("w_hi", o_hi, [P, 4, 2, 512], F32R)
        w_lo = at("w_lo", o_lo, [P, 4, 2, 512], F32R)

        cst = at("cst", o_c, [P, C_END])
        o = o_c + C_END * 4
        VT = at("VT", o, [P, V_END]); o += V_END * 4
        dwT = at("dwT", o, [P, KT, 32]); o += KT * 32 * 4
        mean_sb = at("mean_sb", o, [P, TOK]); o += TOK * 4
        root = at("root", o, [P, TOK]); o += TOK * 4
        rstd = at("rstd", o, [P, TOK]); o += TOK * 4
        rb = at("rb", o, [BUCKETS, HEADS]); o += 64
        assert o <= nc.sbuf_usable_end, (o, nc.sbuf_usable_end)
        ident = cst[:, C_ID:C_ID + P]
        ones = cst[:, C_ONE:C_ONE + P]

        xnat = at("xnat", o_z, [P, NT, D])
        dwn = at("dwn", o_z + 16 * KB, [32, D])
        vrow = at("vrow", o_z + 24 * KB, [P, 2, P])
        rbB = at("rbB", o_z + 26 * KB, [BUCKETS, HEADS, P])
        brow = at("brow", o_z + 32 * KB, [P, HEADS, 384])
        Z = at("Z", o_z, [P, KT, TOK])
        B_hi = at("B_hi", o_z + 16 * KB, [P, KT, TOK], F32R)
        B_lo = at("B_lo", o_z + 32 * KB, [P, KT, TOK], F32R)
        upad = at("upad", o_z + 48 * KB, [P, 2, PAD + TOK])
        sig = at("sig", o_z + 51 * KB, [P, 2, TOK])
        relu = at("relu", o_z + 48 * KB, [P, 4, TOK])
        sq = at("sq", o_z + 52 * KB, [P, 4, TOK])
        proj = at("proj", o_z, [P, 40, TOK])
        wt = at("wt", o_z + 48 * KB, [P, KT, 144])
        BT = at("BT", o_z + 40 * KB, [P, HEADS, TOK])
        kidx = at("kidx", o_z + 58 * KB, [P, TOK])
        widx = at("widx", o_z + 59 * KB, [P, NT, IDX_HEADS])
        score = at("score", o_z + 59 * KB + 256, [P, TOK])
        work = at("work", o_z + 60 * KB + 256, [P, TOK])
        keep = at("keep", o_z + 61 * KB + 256, [P, NT, TOK])
        top8 = at("top8", o_z + 63 * KB + 256, [P, 8])
        stat = at("stat", o_z + 63 * KB + 512, [P, 2, HEADS])
        L = at("L", o_z + 48 * KB, [P, HEADS, TOK])
        poolw = at("poolw", o_t, [P, 4, 2, 256])
        pbuf = at("pbuf", o_t + 8 * KB, [P, 2, 2, 16 + TOK])
        ridx = at("ridx", o_t + 13 * KB, [P, 2, TOK])
        pT = at("pT", o_t, [P, 2 * HEADS, P])
        vnat = at("vnat", o_t + 8 * KB, [P, NT, HEADS * P])
        qh = at("qh", o_z, [P, KT, TOK])
        hnat = at("hnat", o_z + 16 * KB, [P, NT, D])
        s_sc = at("s_sc", o_z + 32 * KB, [P, KT, KEYS])
        s_wk = at("s_wk", o_z + 40 * KB, [P, KT, KEYS])
        cand = at("cand", o_z + 48 * KB, [P, PEER_HEADS, 256])
        cwork = at("cwork", o_z + 40 * KB, [P, PEER_HEADS, 256])
        onehot = at("onehot", o_z + 32 * KB, [P, SLOTS, PEER_TOPK])
        o = o_z + 56 * KB
        subk = at("subk", o, [P, 2, P]); o += KB
        subT = at("subT", o, [P, 2, KEYS]); o += KB
        val16 = at("val16", o, [P, KT, 16]); o += KB
        pos16 = at("pos16", o, [P, KT, 16], U32); o += KB
        posf = at("posf", o, [P, KT, 16]); o += KB
        best = at("best", o, [P, SLOTS]); o += 512
        bpos = at("bpos", o, [P, SLOTS], U32); o += 512
        o = o_t
        bij = at("bij", o, [P, 2, SLOTS], U32); o += KB
        bijf = at("bijf", o, [P, 2, SLOTS]); o += KB
        eij = at("eij", o, [P, 2, SLOTS]); o += KB
        eidf = at("eidf", o, [P, NT, SLOTS]); o += KB
        eid = at("eid", o, [P, NT, SLOTS], U32); o += KB
        gate = at("gate", o, [P, NT, SLOTS]); o += KB
        gsum = at("gsum", o, [P, NT, 2, PEER_HEADS]); o += 128
        dots = at("dots", o, [P, NT, SLOTS]); o += KB
        gelu = at("gelu", o, [P, NT, SLOTS]); o += KB
        coef = at("coef", o, [P, NT, SLOTS]); o += KB
        ering = at("ering", o, [P, 2, RING], U32); o += 64
        dring = at("dring", o, [P, RING]); o += 32
        fstat = at("fstat", o, [P, NT, 8]); o += 64
        assert o <= o_t + 16 * KB
        rows = at("rows", o_raw, [P, RING, D])
        mixed = at("mixed", o_ah, [P, NT, D])
        gb = at("gb", o_al, [P, 2, D])
        y = at("y", o_x, [P, NT, D])

        def psum(name):
            return ctx.enter_context(nc.psum_tensor(name, [P, 512], F32))

        bank = [psum(f"bank{m}") for m in range(4)]
        misc = [psum(f"misc{m}") for m in range(4)]
        scratch = nc.dram_tensor("bias_rows", [HEADS * P * 384], F32).ap()

        def sems(*names):
            return [sem(n) for n in names]

        raw_in = sems(*[f"raw_in{c}" for c in range(4)])
        hi_done, lo_done = sems("hi_done", "lo_done")
        sub_used = sem("sub_used")
        bank_done = sems(*[f"bank_done{m}" for m in range(4)])
        bank_free = sems(*[f"bank_free{m}" for m in range(4)])
        act_pass, pool_pass = sems("act_pass", "pool_pass")
        cst_in, x_in, vec_in, dw_in, rb_in = sems("cst_in", "x_in", "vec_in", "dw_in", "rb_in")
        vt_ps, vt_ok, x_ps, x_ok = sems("vt_ps", "vt_ok", "x_ps", "x_ok")
        rbB_ok, brow_ps, brow_ok, brow_out = sems("rbB_ok", "brow_ps", "brow_ok", "brow_out")
        conv_step, dve_step, act_step = sems("conv_step", "dve_step", "act_step")
        rsq_ok, hidh_ok, hid_ok = sems("rsq_ok", "hidh_ok", "hid_ok")
        NORMS = ("rms1", "lnc", "rms2", "rms3", "ln1")
        n_mean, n_meansb, n_cent, n_sq, n_var, n_eps, n_root, n_rstd, n_out, n_hi, n_op = (
            {n: sem(f"{n}_{what}") for n in NORMS if n[0] == "l" or what not in ("meansb", "cent", "var")}
            for what in ("mean", "meansb", "cent", "sq", "var", "eps", "root", "rstd", "out", "hi", "op"))
        silu_ok, pads_ok = sems("silu_ok", "pads_ok")
        wt_in, poolw_in, BT_in, tail_ps, tail_ok = sems("wt_in", "poolw_in", "BT_in", "tail_ps", "tail_ok")
        pooled_ok, pool_ps, pm_ok, pm_hi, mix_op = sems("pooled_ok", "pool_ps", "pm_ok", "pm_hi", "mix_op")
        idx_ps, idx_rel, idx_acc = sems("idx_ps", "idx_rel", "idx_acc")
        v_ps, v_ok, lg_ps, lg_ok, cen_ok, exp_ok, prob_ok = sems(
            "v_ps", "v_ok", "lg_ps", "lg_ok", "cen_ok", "exp_ok", "prob_ok")
        pT_ps, pT_ok, att_ps, att_hi, att_lo = sems("pT_ps", "pT_ok", "att_ps", "att_hi", "att_lo")
        subk_in, subT_ps, subT_ok, hn_ps, hn_ok = sems("subk_in", "subT_ps", "subT_ok", "hn_ps", "hn_ok")
        key_ps, key_ok, top_ok, gcen_ok, gexp_ok, eid_ok = sems(
            "key_ps", "key_ok", "top_ok", "gcen_ok", "gexp_ok", "eid_ok")
        row_in = sems(*[f"row_in{j}" for j in range(RING)])
        row_used, ering_ok, dots_ok, gelu_ok, coef_ok = sems("row_used", "ering_ok", "dots_ok", "gelu_ok", "coef_ok")
        gb_in, var_ok, rt_ok, y_ok, y_out = sems("gb_in", "var_ok", "rt_ok", "y_ok", "y_out")

        class Steps:

            def __init__(self, engine, semaphore):
                self.engine, self.semaphore, self.count = engine, semaphore, 0

            def __call__(self, instruction, hold=True):
                instruction.then_inc(self.semaphore, 1)
                self.count += 1
                if hold:
                    self.engine.wait_ge(self.semaphore, self.count)

        w_conv = a["cc_w_in"][0].rearrange("(k p) (h g n) -> g p k h n", p=P, h=2, n=256)
        w_co = a["cc_w_out"][0].rearrange("(k p) (g n) -> g p k n", p=P, n=512)
        w_1 = a["mlp_w1"][0].rearrange("(k p) (q g n) -> q g p k n", p=P, q=4, n=512)
        w_2 = a["mlp_w2"][0].rearrange("(q k p) (g n) -> q g p k n", p=P, q=4, n=512)
        w_pr = a["w_in_2"][0][:, 0:5120].rearrange("(k p) (g n) -> g p k n", p=P, n=512)
        w_mx = a["w_out_2"][0].rearrange("(k p) (g n) -> g p k n", p=P, n=512)
        w_qr = a["peer_wq"][0].rearrange("(k p) (g n) -> g p k n", p=P, n=512)

        block = ctx.enter_context(nc.Block())

        @block.sync
        def _(sp):
            def conv_chunk(c, g):
                for half in range(2):
                    sp.dma_start(raw[:, c, :, 256 * half:256 * half + 256],
                                 w_conv[bass.ds(g, 1), :, 4 * c:4 * c + 4, half, :]
                                 .rearrange("o p k n -> (o p) k n")).then_inc(raw_in[c], 16)

            def chunk(c, view, g, G):
                sp.wait_ge(lo_done, G * SUBS + (2 * c + 2 - SUBS))
                sp.dma_start(raw[:, c, :, :], view[bass.ds(g, 1), :, 4 * c:4 * c + 4, :]
                             .rearrange("o p k n -> (o p) k n")).then_inc(raw_in[c], 16)

            sp.dma_start(cst[:], a["table"]).then_inc(cst_in, 16)
            sp.dma_start(xnat[:], a["x"][0].rearrange("(t p) d -> p t d", p=P)).then_inc(x_in, 16)
            for c in range(4):
                conv_chunk(c, 0)
            with sp.Fori(1, G_OUT) as g:
                for c in range(4):
                    sp.wait_ge(lo_done, g * SUBS + (2 * c + 2 - SUBS))
                    conv_chunk(c, g)
            with sp.Fori(0, 4) as g:
                for c in range(4):
                    chunk(c, w_co, g, g + G_OUT)
            with sp.Fori(0, 4) as q:
                for part, view in enumerate((w_1, w_2)):
                    with sp.Fori(0, 4) as g:
                        for c in range(4):
                            chunk(c, view[bass.ds(q, 1)].rearrange("o g p k n -> (o g) p k n"), g,
                                  q * 8 + g + (G_MLP + 4 * part))
            for view, G0, n in ((w_pr, G_PROJ, 10), (w_mx, G_MIX, 4), (w_qr, G_QRY, 4)):
                with sp.Fori(0, n) as g:
                    for c in range(4):
                        chunk(c, view, g, g + G0)
            sp.wait_ge(bank_done[3], G_END)
            for i, name in enumerate(("ln2_g", "ln2_b")):
                sp.dma_start(gb[:, i, :], a[name].broadcast_to([P, D])).then_inc(gb_in, 16)
            for t in range(NT):
                sp.wait_ge(y_ok, t + 1)
                sp.dma_start(out[0, t * P:(t + 1) * P, :], y[:, t, :]).then_inc(y_out, 16)
            sp.wait_ge(y_out, 16 * NT)

        @block.gpsimd
        def _(pool):
            with pool.Fori(0, G_END) as G:
                for s in range(SUBS):
                    pool.wait_ge(hi_done, G * SUBS + (s + 1))
                    nc.gpsimd.tensor_tensor(w_lo[:, s % 4], raw[:, s // 2, 2 * (s % 2):2 * (s % 2) + 2, :],
                                            w_hi[:, s % 4].bitcast(F32), ALU.subtract).then_inc(lo_done, 1)

            def gather(table, t, first):
                with pool.Fori(0, SLOTS // (2 * RING)) as r:
                    for half in range(2):
                        nc.gpsimd.tensor_copy(ering[:, half, :], eid[:, t, bass.ds((2 * r + half) * RING, RING)]
                                              ).then_inc(ering_ok, 1)
                        pool.wait_ge(ering_ok, 2 * r + (half + 1 + first))
                        for j in range(RING):
                            pool.wait_ge(row_used, (2 * r + (half + first)) * RING + (j + 1))
                            pool.sem_inc(pool_pass, 1)
                            pool.indirect_dma_start(rows[:, j, :], None, table,
                                                    bass.IndirectOffsetOnAxis(ering[:, half, j:j + 1], 0)
                                                    ).then_inc(row_in[j], 16)

            rounds = SLOTS // RING
            for t in range(NT):
                pool.wait_ge(eid_ok, t + 1)
                gather(a["peer_u"][0], t, t * rounds)
            for t in range(NT):
                gather(a["peer_v"][0], t, (NT + t) * rounds)

        @block.tensor
        def _(pe):
            def groups(hi, lo, G0, n, ready, base=0, step=1, order=(0, 1, 2, 3)):
                with pe.Fori(0, n) as g:
                    G = g + G0
                    for s in range(SUBS):
                        pe.wait_ge(ready, base + step * (s + 1))
                        pe.wait_ge(lo_done, G * SUBS + (s + 1))
                        for m in range(4):
                            if s == 0:
                                pe.wait_ge(bank_free[m], G + 1)
                            for k in range(2):
                                wh = w_hi[:, s % 4, k, order[m] * P:(order[m] + 1) * P]
                                wl = w_lo[:, s % 4, k, order[m] * P:(order[m] + 1) * P]
                                dst, kt = bank[m][:, 0:TOK], 2 * s + k
                                nc.tensor.matmul(dst, wh, hi[:, kt, :], start=(kt == 0), stop=False)
                                nc.tensor.matmul(dst, wh, lo[:, kt, :], start=False, stop=False)
                                last = nc.tensor.matmul(dst, wl, hi[:, kt, :], start=False, stop=(kt == KT - 1))
                            if s == SUBS - 1:
                                last.then_inc(bank_done[m], 1)
                        if s < SUBS - 1:
                            last.then_inc(sub_used, 1)

            def column_means(dst, src, ready, per, done):
                for k in range(KT):
                    if k % 4 == 0:
                        pe.wait_ge(ready, per * (k // 4 + 1))
                    last = nc.tensor.matmul(dst[:, 0:TOK], ones, src[:, k, :], start=(k == 0), stop=(k == KT - 1))
                last.then_inc(done, 1)

            for m in range(4):
                pe.sem_inc(bank_free[m], 1)
            pe.wait_ge(cst_in, 16)
            pe.wait_ge(x_in, 16)
            for r in range(KT // 2):
                if r >= 4:
                    pe.wait_ge(x_ok, r - 3)
                for i in range(4):
                    k, t = 2 * r + i // 2, i % 2
                    last = nc.tensor.transpose(misc[r % 4][:, i * P:(i + 1) * P], xnat[:, t, k * P:(k + 1) * P], ident)
                last.then_inc(x_ps, 1)
            pe.wait_ge(vec_in, 16 * 11)
            nc.tensor.transpose(bank[0][:, 0:P], vrow[:, 0, :], ident)
            nc.tensor.transpose(bank[0][:, P:V_END], vrow[0:V_END - P, 1, :], ident[0:V_END - P, 0:V_END - P]
                                ).then_inc(vt_ps, 1)
            pe.wait_ge(dw_in, 16)
            pe.wait_ge(pads_ok, 1)
            for k in range(KT):
                last = nc.tensor.transpose(bank[1][:, 32 * k:32 * k + 32], dwn[:, k * P:(k + 1) * P], ident[0:32, 0:32])
            last.then_inc(vt_ps, 1)
            column_means(misc[0], T, n_sq["rms1"], 1, n_mean["rms1"])
            pe.wait_ge(rbB_ok, 1)
            for h in range(HEADS):
                if h >= 2:
                    pe.wait_ge(brow_ok, h - 1)
                nc.tensor.matmul(misc[2 + h % 2][:, 0:384], rbB[:, h, :], cst[0:BUCKETS, C_HOT:C_HOT + 384],
                                 start=True, stop=True).then_inc(brow_ps, 1)
            pe.wait_ge(vt_ok, 2)
            groups(A_hi, A_lo, G_IN, 8, n_op["rms1"], order=(2, 3, 0, 1))

            pe.wait_ge(conv_step, 8 * 2 * TAPS)
            column_means(misc[0], Z, conv_step, 0, n_mean["lnc"])
            column_means(misc[1], T, n_sq["lnc"], 1, n_var["lnc"])
            groups(B_hi, B_lo, G_OUT, 4, n_op["lnc"])

            column_means(misc[0], T, n_sq["rms2"], 1, n_mean["rms2"])
            with pe.Fori(0, 4) as q:
                groups(A_hi, A_lo, q * 8 + G_MLP, 4, n_op["rms2"])
                groups(B_hi, B_lo, q * 8 + (G_MLP + 4), 4, hid_ok, base=q * KT, step=2)

            column_means(misc[0], T, n_sq["rms3"], 1, n_mean["rms3"])
            groups(A_hi, A_lo, G_PROJ, 10, n_op["rms3"])
            pe.wait_ge(wt_in, 48)
            for k in range(KT):
                nc.tensor.matmul(misc[0][:, 0:TOK], wt[:, k, 0:P], X[:, k, :], start=(k == 0), stop=(k == KT - 1))
            for t in range(NT):
                for k in range(KT):
                    last = nc.tensor.matmul(misc[1][:, t * 16:t * 16 + 16], X[:, k, t * P:(t + 1) * P],
                                            wt[:, k, P:P + 16], start=(k == 0), stop=(k == KT - 1))
            last.then_inc(tail_ps, 1)

            pe.wait_ge(poolw_in, 16)
            pe.wait_ge(tail_ok, 2)
            for g in range(4):
                pe.wait_ge(pooled_ok, g + 1)
                for o in range(2):
                    r = 2 * g + o
                    if r >= 4:
                        pe.wait_ge(pm_ok, r - 3)
                    for c in range(2):
                        last = nc.tensor.matmul(misc[r % 4][:, 0:TOK], poolw[:, g, c, o * P:(o + 1) * P],
                                                proj[:, 2 * g + c, :], start=(c == 0), stop=(c == 1))
                    last.then_inc(pool_ps, 1)

            pe.wait_ge(pm_ok, 8)
            for n in range(NT * IDX_HEADS):
                b, h = divmod(n, IDX_HEADS)
                lo64 = IDX_DIM * (h % 2)
                if n >= 4:
                    pe.wait_ge(idx_rel, n - 3)
                nc.tensor.matmul(misc[n % 4][:, 0:P * (b + 1)],
                                 proj[lo64:lo64 + IDX_DIM, 32 + h // 2, b * P:(b + 1) * P],
                                 kidx[lo64:lo64 + IDX_DIM, 0:P * (b + 1)], start=True, stop=True).then_inc(idx_ps, 1)
            pe.wait_ge(idx_rel, NT * IDX_HEADS)
            for r in range(4):
                for i in range(4):
                    b, h = r // 2, 4 * (r % 2) + i
                    last = nc.tensor.transpose(misc[r][:, i * P:(i + 1) * P], proj[:, 24 + h, b * P:(b + 1) * P], ident)
                last.then_inc(v_ps, 1)
            pe.wait_ge(v_ok, 4)
            for b in range(NT):
                nk = P * (b + 1)
                for h in range(HEADS):
                    n = HEADS * b + h
                    if h >= 4:
                        pe.wait_ge(lg_ok, n - 3)
                    nc.tensor.matmul(misc[h % 4][:, 0:nk], proj[:, 8 + h, b * P:(b + 1) * P], proj[:, 16 + h, 0:nk],
                                     start=True, stop=True).then_inc(lg_ps, 1)
                pe.wait_ge(lg_ok, HEADS * (b + 1))
                pe.wait_ge(prob_ok, b + 1)
                done = 2 * b
                for r in range(2 * (b + 1)):
                    for i in range(4):
                        h, kb = divmod(4 * r + i, b + 1)
                        last = nc.tensor.transpose(misc[r % 4][:, i * P:(i + 1) * P], L[:, h, kb * P:(kb + 1) * P], ident)
                    last.then_inc(pT_ps, 1)
                pe.wait_ge(pT_ok, done + 2 * (b + 1))
                for i in range(2):
                    for h in range(4 * i, 4 * i + 4):
                        for kb in range(b + 1):
                            last = nc.tensor.matmul(misc[i][:, (h % 4) * P:(h % 4 + 1) * P],
                                                    vnat[:, kb, h * P:(h + 1) * P], pT[:, h * (b + 1) + kb, :],
                                                    start=(kb == 0), stop=(kb == b))
                    last.then_inc(att_ps, 1)
                pe.wait_ge(att_lo, 2 * (b + 1))

            groups(A_hi, A_lo, G_MIX, 4, mix_op)

            pe.wait_ge(bank_free[3], G_QRY + 1)
            column_means(misc[0], X, bank_free[3], 0, n_mean["ln1"])
            column_means(misc[1], T, n_sq["ln1"], 1, n_var["ln1"])
            pe.wait_ge(n_op["ln1"], 8)
            for r in range(8):
                if r >= 4:
                    pe.wait_ge(hn_ok, r - 3)
                for i in range(4):
                    t, k = r // 4, 4 * (r % 4) + i
                    last = nc.tensor.transpose(misc[r % 4][:, i * P:(i + 1) * P], X[:, k, t * P:(t + 1) * P], ident)
                last.then_inc(hn_ps, 1)
            pe.wait_ge(subk_in, 16)
            pe.wait_ge(hn_ok, 5)
            for i in range(2):
                last = nc.tensor.transpose(misc[0][:, i * P:(i + 1) * P], subk[:, i, :], ident)
            last.then_inc(subT_ps, 1)
            groups(A_hi, A_lo, G_QRY, 4, n_op["ln1"])
            pe.wait_ge(bank_free[3], G_END + 1)
            pe.wait_ge(subT_ok, 1)
            pe.wait_ge(hn_ok, 8)
            for t in range(NT):
                for r in range(4):
                    if t:
                        pe.wait_ge(key_ok, 4 * (t - 1) + r + 1)
                    for i in range(4):
                        hh = 4 * r + i
                        last = nc.tensor.matmul(misc[r][:, i * P:(i + 1) * P], qh[:, hh, t * P:(t + 1) * P],
                                                subT[:, hh % 2, :], start=True, stop=True)
                    last.then_inc(key_ps, 1)

        @block.scalar
        def _(act):
            step = Steps(act, act_step)

            def round_sub(G, s, raw_count):
                act.wait_ge(raw_in[s // 2], raw_count)
                if s >= 4:
                    act.wait_ge(sub_used, G * 7 + (s - 3))
                elif s == 3:
                    if not (isinstance(G, int) and G == 0):
                        act.wait_ge(bank_done[3], G)
                elif not (isinstance(G, int) and G == 0):
                    act.wait_ge(sub_used, G * 7 + (s - 2))
                nc.scalar.copy(w_hi[:, s % 4], raw[:, s // 2, 2 * (s % 2):2 * (s % 2) + 2, :]).then_inc(hi_done, 1)

            def ahead(G, now, then, last=False):
                for s in range(3, SUBS):
                    round_sub(G, s, now)
                if not last:
                    for s in range(3):
                        round_sub(G + 1, s, then)

            def landed(G):
                return (G + 9) * 16

            def squares(n, src, waits):
                for s, v in waits:
                    act.wait_ge(s, v)
                for p in range(4):
                    if n[0] == "l":
                        act.wait_ge(n_cent[n], p + 1)
                    nc.scalar.activation(T[:, 4 * p:4 * p + 4, :], src[:, 4 * p:4 * p + 4, :], ACT.Square
                                         ).then_inc(n_sq[n], 1)

            def take_root(n):
                act.wait_ge(n_eps[n], 1)
                nc.scalar.activation(root[:], rstd[:], ACT.Sqrt).then_inc(n_root[n], 1)

            def round_operand(n, src, dst, ready, per):
                for p in range(4):
                    act.wait_ge(ready, per * (p + 1))
                    nc.scalar.copy(dst[:, 4 * p:4 * p + 4, :], src[:, 4 * p:4 * p + 4, :]).then_inc(n_hi[n], 1)

            VEC = (("norm1_g", V_N1), ("norm2_g", V_N2), ("final_g", V_FIN), ("cc_b_in", V_BV), ("cc_dw_b", V_DWB),
                   ("cc_ln_g", V_LNG), ("cc_ln_b", V_LNB), ("cc_b_out", V_BOUT), ("ln1_g", V_L1G),
                   ("ln1_b", V_L1B), ("pool_scale", V_PSC))
            for name, col in VEC:
                v = a[name].rearrange("(r c) -> r c", c=P) if name == "final_g" else a[name][0].rearrange("(r c) -> r c", c=P)
                act.dma_start(vrow[col % P:col % P + v.shape[0], col // P, :], v).then_inc(
                    vec_in, 16)
            act.dma_start(rb[:], a["rel_bias"]).then_inc(rb_in, 16)
            act.wait_ge(pads_ok, 1)
            act.dma_start(dwn[0:TAPS, :], a["cc_dw"][0]).then_inc(dw_in, 16)

            squares("rms1", X, [(x_ok, 8)])
            act.wait_ge(vt_ps, 2)
            nc.scalar.copy(VT[:], bank[0][:, 0:V_END]).then_inc(vt_ok, 1)
            nc.scalar.copy(dwT[:], bank[1][:].rearrange("p (k j) -> p k j", j=32)).then_inc(vt_ok, 1)
            for s in range(3):
                round_sub(0, s, 32)
            take_root("rms1")
            round_operand("rms1", T, A_hi, n_out["rms1"], 4)
            for h in range(HEADS):
                act.wait_ge(brow_ps, h + 1)
                nc.scalar.copy(brow[:, h, :], misc[2 + h % 2][:, 0:384]).then_inc(brow_ok, 1)
            act.wait_ge(brow_ok, HEADS)
            act.dma_start(scratch.rearrange("(h p x) -> p h x", p=P, x=384), brow[:]).then_inc(brow_out, 16)

            def conv_group(g):
                ahead(g, (g + 1) * 32, (g + 2) * 32)
                gates(g)

            def gates(g):
                for i in range(2):
                    act.wait_ge(bank_done[i], g + 1)
                    act.wait_ge(bank_free[2 + i], g + 1)
                    act.sem_inc(act_pass, 1)
                    nc.scalar.activation(sig[:, i, :], bank[i][:, 0:TOK], ACT.Sigmoid,
                                         bias=VT[:, bass.ds(V_BG + i + 2 * g, 1)]).then_inc(bank_free[i], 1)

            conv_group(0)
            with act.Fori(1, 7) as g:
                conv_group(g)
            ahead(7, 8 * 32, landed(8))
            gates(7)

            act.wait_ge(n_mean["lnc"], 1)
            nc.scalar.copy(mean_sb[:], misc[0][:, 0:TOK]).then_inc(n_meansb["lnc"], 1)
            squares("lnc", Z, [])
            take_root("lnc")
            for p in range(4):
                act.wait_ge(n_out["lnc"], p + 1)
                for k in range(4 * p, 4 * p + 4):
                    nc.scalar.activation(T[:, k, :], Z[:, k, :], ACT.Silu, bias=VT[:, V_LNB + k:V_LNB + k + 1],
                                         scale=VT[:, V_LNG + k:V_LNG + k + 1]).then_inc(silu_ok, 1)
                act.wait_ge(silu_ok, 4 * (p + 1))
                nc.scalar.copy(B_hi[:, 4 * p:4 * p + 4, :], T[:, 4 * p:4 * p + 4, :]).then_inc(n_hi["lnc"], 1)
            with act.Fori(G_OUT, G_MLP) as G:
                ahead(G, landed(G), landed(G + 1))

            def all_read(G):
                return [(bank_free[m], G + 2) for m in range(4)]

            squares("rms2", X, all_read(G_MLP - 1))
            take_root("rms2")
            round_operand("rms2", T, A_hi, n_out["rms2"], 4)
            with act.Fori(0, 4) as q:
                for g in range(4):
                    G = q * 8 + (G_MLP + g)
                    ahead(G, landed(G), landed(G + 1))
                    for m in range(4):
                        act.wait_ge(bank_done[m], G + 1)
                        act.wait_ge(rsq_ok, q * 16 + (4 * g + m + 1))
                        nc.scalar.activation(relu[:, m, :], bank[m][:, 0:TOK], ACT.Relu).then_inc(bank_free[m], 1)
                    for m in range(4):
                        act.wait_ge(bank_free[m], G + 2)
                        nc.scalar.activation(B_hi[:, 4 * g + m, :], relu[:, m, :], ACT.Square).then_inc(hidh_ok, 1)
                    act.wait_ge(hidh_ok, q * 16 + (4 * g + 4))
                with act.Fori(0, 4) as g:
                    G = q * 8 + g + (G_MLP + 4)
                    ahead(G, landed(G), landed(G + 1))

            squares("rms3", X, all_read(G_PROJ - 1))
            take_root("rms3")
            round_operand("rms3", X, A_hi, n_out["rms3"], 4)
            act.wait_ge(n_op["rms3"], 8)
            act.wait_ge(brow_out, 16)
            w2 = a["w_in_2"][0].rearrange("(k p) n -> p k n", p=P)
            for to, lo, n in ((0, 5120, 64), (64, 5120, 64), (128, 5184, 16)):
                act.dma_start(wt[:, :, to:to + n], w2[:, :, lo:lo + n]).then_inc(wt_in, 16)
            act.dma_start(poolw[:], a["pool_w"][0].rearrange("g (c p) n -> p g c n", p=P)).then_inc(poolw_in, 16)
            for h in range(HEADS):
                first = h * P * 384 + P - 1
                act.dma_start(BT[:, h, :], scratch[first:first + P * 383].rearrange("(p x) -> p x", x=383)[:, 0:TOK]
                              ).then_inc(BT_in, 16)
            with act.Fori(G_PROJ, G_MIX) as G:
                ahead(G, landed(G), landed(G + 1))

            act.wait_ge(tail_ps, 1)
            act.wait_ge(bank_free[3], G_MIX + 1)
            nc.scalar.copy(kidx[:], misc[0][:, 0:TOK]).then_inc(tail_ok, 1)
            nc.scalar.mul(widx[:], misc[1][:, 0:32].rearrange("p (t h) -> p t h", t=NT), IDX_SCALE).then_inc(tail_ok, 1)
            for g in range(4):
                act.wait_ge(pool_ps, 2 * g + 2)
                for o in range(2):
                    nc.scalar.mul(proj[:, 2 * g + o, :], misc[(2 * g + o) % 4][:, 0:TOK],
                                  VT[:, V_PSC + 2 * g + o:V_PSC + 2 * g + o + 1]).then_inc(pm_ok, 1)
                act.wait_ge(pm_ok, 2 * g + 2)
                nc.scalar.copy(A_hi[:, 2 * g:2 * g + 2, :], proj[:, 2 * g:2 * g + 2, :]).then_inc(pm_hi, 1)
            for n in range(NT * IDX_HEADS):
                act.wait_ge(idx_ps, n + 1)
                if n >= 2:
                    act.wait_ge(idx_acc, n - 1)
                nk = P * (n // IDX_HEADS + 1)
                nc.scalar.activation(ridx[:, n % 2, 0:nk], misc[n % 4][:, 0:nk], ACT.Relu).then_inc(idx_rel, 1)
            act.wait_ge(idx_acc, NT * IDX_HEADS)
            for r in range(4):
                act.wait_ge(v_ps, r + 1)
                nc.scalar.copy(vnat[:, r // 2, 512 * (r % 2):512 * (r % 2) + 512], misc[r][:]).then_inc(v_ok, 1)
            for b in range(NT):
                nk = P * (b + 1)
                act.wait_ge(cen_ok, b + 1)
                nc.scalar.activation(L[:, :, 0:nk], L[:, :, 0:nk], ACT.Exp).then_inc(exp_ok, 1)
                for r in range(2 * (b + 1)):
                    act.wait_ge(pT_ps, 2 * b + r + 1)
                    nc.scalar.copy(pT[:, 4 * r:4 * r + 4, :], misc[r % 4][:].rearrange("p (i q) -> p i q", i=4)
                                   ).then_inc(pT_ok, 1)
                for i in range(2):
                    act.wait_ge(att_ps, 2 * b + i + 1)
                    nc.scalar.copy(A_hi[:, 8 + 4 * i:12 + 4 * i, b * P:(b + 1) * P],
                                   misc[i][:].rearrange("p (i q) -> p i q", i=4)).then_inc(att_hi, 1)

            with act.Fori(G_MIX, G_QRY) as G:
                ahead(G, landed(G), landed(G + 1))
            act.wait_ge(n_mean["ln1"], 1)
            nc.scalar.copy(mean_sb[:], misc[0][:, 0:TOK]).then_inc(n_meansb["ln1"], 1)
            squares("ln1", X, [])
            take_root("ln1")
            round_operand("ln1", X, A_hi, n_out["ln1"], 4)
            act.dma_start(subk[:], a["peer_subkeys"][0].rearrange("i k d -> k i d")).then_inc(subk_in, 16)
            act.wait_ge(subT_ps, 1)
            nc.scalar.copy(subT[:], misc[0][:, 0:2 * P].rearrange("p (i k) -> p i k", i=2)).then_inc(subT_ok, 1)
            with act.Fori(G_QRY, G_END - 1) as G:
                ahead(G, landed(G), landed(G + 1))
            ahead(G_END - 1, landed(G_END - 1), None, last=True)

            for t in range(NT):
                if t:
                    act.wait_ge(top_ok, t)
                for r in range(4):
                    act.wait_ge(key_ps, 4 * t + r + 1)
                    nc.scalar.copy(s_sc[:, 4 * r:4 * r + 4, :], misc[r][:].rearrange("p (i k) -> p i k", i=4)
                                   ).then_inc(key_ok, 1)
                act.wait_ge(gcen_ok, t + 1)
                nc.scalar.activation(gate[:, t, :], gate[:, t, :], ACT.Exp).then_inc(gexp_ok, 1)
            for t in range(NT):
                act.wait_ge(dots_ok, SLOTS // RING * (t + 1))
                nc.scalar.activation(gelu[:, t, :], dots[:, t, :], ACT.Gelu).then_inc(gelu_ok, 1)
            for t in range(NT):
                act.wait_ge(var_ok, t + 1)
                nc.scalar.activation(fstat[:, t, 3:4], fstat[:, t, 2:3], ACT.Sqrt).then_inc(rt_ok, 1)

        @block.vector
        def _(dve):
            step = Steps(dve, dve_step)
            V = nc.vector

            def over_tiles(tile, n):
                return tile.unsqueeze(1).broadcast_to([P, n, tile.shape[1]])

            def reciprocal_root(n, ps, eps, done):
                dve.wait_ge(done, 1)
                V.tensor_scalar(rstd[:], ps[:, 0:TOK], eps, None, ALU.add).then_inc(n_eps[n], 1)
                dve.wait_ge(n_root[n], 1)
                V.reciprocal(rstd[:], root[:]).then_inc(n_rstd[n], 1)
                dve.wait_ge(n_rstd[n], 1)

            def low_parts(n, src, hi, lo):
                for p in range(4):
                    dve.wait_ge(n_hi[n], p + 1)
                    V.tensor_tensor(lo[:, 4 * p:4 * p + 4, :], src[:, 4 * p:4 * p + 4, :],
                                    hi[:, 4 * p:4 * p + 4, :].bitcast(F32), ALU.subtract).then_inc(n_op[n], 2)

            def rms(n, dst, gain):
                reciprocal_root(n, misc[0], RMS_EPS, n_mean[n])
                for k in range(KT):
                    V.scalar_tensor_tensor(dst[:, k, :], X[:, k, :], VT[:, gain + k:gain + k + 1], rstd[:],
                                           ALU.mult, ALU.mult).then_inc(n_out[n], 1)
                low_parts(n, dst, A_hi, A_lo)

            def centre(n, src):
                dve.wait_ge(n_meansb[n], 1)
                for p in range(4):
                    V.tensor_tensor(src[:, 4 * p:4 * p + 4, :], src[:, 4 * p:4 * p + 4, :],
                                    over_tiles(mean_sb[:], 4), ALU.subtract).then_inc(n_cent[n], 1)

            dve.sem_inc(rsq_ok, 4)
            dve.sem_inc(row_used, RING)
            V.memset(dwn[:], 0.0).then_inc(pads_ok, 1)
            step(V.memset(upad[:, :, 0:PAD], 0.0), hold=False)
            for r in range(8):
                dve.wait_ge(x_ps, r + 1)
                V.tensor_copy(X[:, 2 * r:2 * r + 2, :], misc[r % 4][:].rearrange("p (k t) -> p k t", k=2)
                              ).then_inc(x_ok, 1)
            dve.wait_ge(rb_in, 16)
            V.tensor_copy(rbB[:], rb[:].unsqueeze(2).broadcast_to([BUCKETS, HEADS, P])).then_inc(rbB_ok, 1)
            dve.wait_ge(vt_ok, 2)
            rms("rms1", T, V_N1)

            with dve.Fori(0, 8) as g:
                for i in range(2):
                    dve.wait_ge(bank_done[2 + i], g + 1)
                    dve.wait_ge(bank_free[i], g + 2)
                    V.scalar_tensor_tensor(upad[:, i, PAD:PAD + TOK], bank[2 + i][:, 0:TOK],
                                           VT[:, bass.ds(V_BV + i + 2 * g, 1)], sig[:, i, :], ALU.add, ALU.mult
                                           ).then_inc(bank_free[2 + i], 1)
                for n in range(2 * TAPS):
                    j, i = divmod(n, 2)
                    z = Z[:, bass.ds(2 * g + i, 1), :].rearrange("p o t -> p (o t)")
                    w = dwT[:, bass.ds(2 * g + i, 1), j:j + 1].rearrange("p o j -> p (o j)")
                    if n < 2:
                        dve.wait_ge(bank_free[2 + i], g + 2)
                        V.tensor_scalar(z, upad[:, i, 0:TOK], w, VT[:, bass.ds(V_DWB + i + 2 * g, 1)],
                                        ALU.mult, ALU.add).then_inc(conv_step, 1)
                    else:
                        dve.wait_ge(conv_step, g * (2 * TAPS) + (n - 1))
                        V.scalar_tensor_tensor(z, upad[:, i, j:j + TOK], w, z, ALU.mult, ALU.add
                                               ).then_inc(conv_step, 1)
                dve.wait_ge(conv_step, g * (2 * TAPS) + 2 * TAPS)

            centre("lnc", Z)
            reciprocal_root("lnc", misc[1], LN_EPS, n_var["lnc"])
            for p in range(4):
                V.tensor_tensor(Z[:, 4 * p:4 * p + 4, :], Z[:, 4 * p:4 * p + 4, :], over_tiles(rstd[:], 4),
                                ALU.mult).then_inc(n_out["lnc"], 1)
            dve.wait_ge(brow_out, 16)
            low_parts("lnc", T, B_hi, B_lo)
            with dve.Fori(0, 4) as g:
                for m in range(4):
                    dve.wait_ge(bank_done[m], g + (G_OUT + 1))
                    xk = X[:, bass.ds(4 * g + m, 1), :].rearrange("p o t -> p (o t)")
                    V.scalar_tensor_tensor(xk, bank[m][:, 0:TOK], VT[:, bass.ds(V_BOUT + m + 4 * g, 1)], xk,
                                           ALU.add, ALU.add).then_inc(bank_free[m], 1)

            rms("rms2", T, V_N2)
            with dve.Fori(0, 4) as q:
                for g in range(4):
                    G = q * 8 + (G_MLP + g)
                    for m in range(4):
                        dve.wait_ge(bank_free[m], G + 2)
                        V.tensor_tensor(sq[:, m, :], relu[:, m, :], relu[:, m, :], ALU.mult).then_inc(rsq_ok, 1)
                    for m in range(4):
                        dve.wait_ge(rsq_ok, q * 16 + (4 * g + m + 5))
                        dve.wait_ge(hidh_ok, q * 16 + (4 * g + m + 1))
                        V.tensor_tensor(B_lo[:, 4 * g + m, :], sq[:, m, :], B_hi[:, 4 * g + m, :].bitcast(F32),
                                        ALU.subtract).then_inc(hid_ok, 1)
                    dve.wait_ge(hid_ok, q * 16 + (4 * g + 4))
                for g in range(4):
                    G = q * 8 + (G_MLP + 4 + g)
                    for m in range(4):
                        dve.wait_ge(bank_done[m], G + 1)
                        V.tensor_tensor(X[:, 4 * g + m, :], bank[m][:, 0:TOK], X[:, 4 * g + m, :], ALU.add
                                        ).then_inc(bank_free[m], 1)

            rms("rms3", X, V_FIN)
            with dve.Fori(0, 10) as g:
                for m in range(4):
                    dve.wait_ge(bank_done[m], g + (G_PROJ + 1))
                    V.tensor_scalar(proj[:, bass.ds(4 * g + m, 1), :].rearrange("p o t -> p (o t)"),
                                    bank[m][:, 0:TOK], 1.0, None, ALU.mult).then_inc(bank_free[m], 1)

            step(V.memset(pbuf[:], 0.0))
            for g, w in enumerate(WINDOWS):
                v = proj[:, 2 * g:2 * g + 2, :]
                src, d = 0, 1
                step(V.tensor_copy(pbuf[:, 0, :, 16:16 + TOK], v))
                while d < w:
                    step(V.tensor_tensor(pbuf[:, 1 - src, :, 16:16 + TOK], pbuf[:, src, :, 16:16 + TOK],
                                         pbuf[:, src, :, 16 - d:16 - d + TOK], ALU.add))
                    src, d = 1 - src, 2 * d
                step(V.tensor_tensor(pbuf[:, src, :, 16:16 + TOK], pbuf[:, src, :, 16:16 + TOK],
                                     over_tiles(cst[:, C_CNT + g * TOK:C_CNT + (g + 1) * TOK], 2), ALU.mult))
                V.tensor_tensor(v, pbuf[:, src, :, 16:16 + TOK], v, ALU.subtract).then_inc(pooled_ok, 1)
                dve.wait_ge(pooled_ok, g + 1)
            for g in range(4):
                dve.wait_ge(pm_hi, g + 1)
                V.tensor_tensor(A_lo[:, 2 * g:2 * g + 2, :], proj[:, 2 * g:2 * g + 2, :],
                                A_hi[:, 2 * g:2 * g + 2, :].bitcast(F32), ALU.subtract).then_inc(mix_op, 1)

            dve.wait_ge(tail_ok, 2)
            for b in range(NT):
                nk = P * (b + 1)
                causal = cst[:, C_CAUSAL + b * TOK:C_CAUSAL + b * TOK + nk]
                for h in range(IDX_HEADS):
                    n = IDX_HEADS * b + h
                    dve.wait_ge(idx_rel, n + 1)
                    if h:
                        dve.wait_ge(idx_acc, n)
                    V.scalar_tensor_tensor(score[:, 0:nk], ridx[:, n % 2, 0:nk], widx[:, b, h:h + 1],
                                           score[:, 0:nk] if h else causal, ALU.mult, ALU.add).then_inc(idx_acc, 1)
                dve.wait_ge(idx_acc, IDX_HEADS * (b + 1))
                src = score
                for _ in range(TOPK // 8):
                    step(V.max(top8[:], src[:, 0:nk]))
                    step(V.match_replace(work[:, 0:nk], top8[:], src[:, 0:nk], TAKEN))
                    src = work
                step(V.tensor_scalar(keep[:, b, 0:nk], work[:, 0:nk], TAKEN / 2, NEG, ALU.is_gt, ALU.mult))
                step(V.tensor_tensor(keep[:, b, 0:nk], keep[:, b, 0:nk], causal, ALU.add))

            dve.wait_ge(BT_in, 16 * HEADS)
            for b in range(NT):
                nk = P * (b + 1)
                l = L[:, :, 0:nk]
                for h in range(HEADS):
                    dve.wait_ge(lg_ps, HEADS * b + h + 1)
                    V.scalar_tensor_tensor(L[:, h, 0:nk], misc[h % 4][:, 0:nk], P ** -0.5,
                                           BT[:, h, TOK - nk:TOK], ALU.mult, ALU.add).then_inc(lg_ok, 1)
                dve.wait_ge(lg_ok, HEADS * (b + 1))
                step(V.tensor_tensor(l, l, over_tiles(keep[:, b, 0:nk], HEADS), ALU.add))
                step(V.tensor_reduce(stat[:, 0, :], l, AX, ALU.max))
                V.tensor_tensor(l, l, stat[:, 0, :].unsqueeze(2).broadcast_to([P, HEADS, nk]), ALU.subtract
                                ).then_inc(cen_ok, 1)
                dve.wait_ge(exp_ok, b + 1)
                step(V.tensor_reduce(stat[:, 1, :], l, AX, ALU.add))
                step(V.reciprocal(stat[:, 1, :], stat[:, 1, :]))
                V.tensor_tensor(l, l, stat[:, 1, :].unsqueeze(2).broadcast_to([P, HEADS, nk]), ALU.mult
                                ).then_inc(prob_ok, 1)
                for i in range(2):
                    dve.wait_ge(att_hi, 2 * b + i + 1)
                    hs = slice(8 + 4 * i, 12 + 4 * i)
                    V.tensor_tensor(A_lo[:, hs, b * P:(b + 1) * P], misc[i][:].rearrange("p (i q) -> p i q", i=4),
                                    A_hi[:, hs, b * P:(b + 1) * P].bitcast(F32), ALU.subtract).then_inc(att_lo, 1)
            dve.wait_ge(att_lo, 2 * NT)
            dve.sem_inc(mix_op, 4)

            with dve.Fori(0, 4) as g:
                for m in range(4):
                    dve.wait_ge(bank_done[m], g + (G_MIX + 1))
                    xk = X[:, bass.ds(4 * g + m, 1), :].rearrange("p o t -> p (o t)")
                    V.scalar_tensor_tensor(xk, xk, ALPHA, bank[m][:, 0:TOK], ALU.mult, ALU.add
                                           ).then_inc(bank_free[m], 1)
            centre("ln1", X)
            reciprocal_root("ln1", misc[1], LN_EPS, n_var["ln1"])
            for p in range(4):
                step(V.tensor_tensor(X[:, 4 * p:4 * p + 4, :], X[:, 4 * p:4 * p + 4, :], over_tiles(rstd[:], 4),
                                     ALU.mult), hold=False)
            for k in range(KT):
                if k % 4 == 0:
                    dve.wait_ge(dve_step, step.count - 3 + k // 4)
                V.tensor_scalar(X[:, k, :], X[:, k, :], VT[:, V_L1G + k:V_L1G + k + 1],
                                VT[:, V_L1B + k:V_L1B + k + 1], ALU.mult, ALU.add).then_inc(n_out["ln1"], 1)
            low_parts("ln1", X, A_hi, A_lo)
            for r in range(8):
                dve.wait_ge(hn_ps, r + 1)
                V.tensor_copy(hnat[:, r // 4, 512 * (r % 4):512 * (r % 4) + 512], misc[r % 4][:]).then_inc(hn_ok, 1)
            with dve.Fori(0, 4) as g:
                for m in range(4):
                    dve.wait_ge(bank_done[m], g + (G_QRY + 1))
                    V.tensor_scalar(qh[:, bass.ds(4 * g + m, 1), :].rearrange("p o t -> p (o t)"),
                                    bank[m][:, 0:TOK], 1.0, None, ALU.mult).then_inc(bank_free[m], 1)

            def top16(vals, where, src, wk, n):
                for i in range(n):
                    step(V.max(vals(i)[:, 0:8], src(i)), hold=i == n - 1)
                for i in range(n):
                    step(V.max_index(where(i)[:, 0:8], vals(i)[:, 0:8], src(i)), hold=False)
                    step(V.match_replace(wk(i), vals(i)[:, 0:8], src(i), TAKEN), hold=i == n - 1)
                for i in range(n):
                    step(V.max(vals(i)[:, 8:16], wk(i)), hold=i == n - 1)
                for i in range(n):
                    step(V.max_index(where(i)[:, 8:16], vals(i)[:, 8:16], wk(i)), hold=i == n - 1)

            for t in range(NT):
                dve.wait_ge(key_ok, 4 * (t + 1))
                top16(lambda i: val16[:, i, :], lambda i: pos16[:, i, :], lambda i: s_sc[:, i, :],
                      lambda i: s_wk[:, i, :], KT)
                step(V.tensor_copy(posf[:], pos16[:]), hold=False)
                v = val16[:].rearrange("p (h s) i -> p h s i", s=2)
                four = [P, PEER_HEADS, 16, 16]
                step(V.tensor_tensor(cand[:].rearrange("p h (i j) -> p h i j", i=16),
                                     v[:, :, 0, :].unsqueeze(3).broadcast_to(four),
                                     v[:, :, 1, :].unsqueeze(2).broadcast_to(four), ALU.add))
                top16(lambda h: best[:, 16 * h:16 * h + 16], lambda h: bpos[:, 16 * h:16 * h + 16],
                      lambda h: cand[:, h, :], lambda h: cwork[:, h, :], PEER_HEADS)
                step(V.tensor_scalar(bij[:, 0, :], bpos[:], 4, None, ALU.logical_shift_right), hold=False)
                step(V.tensor_scalar(bij[:, 1, :], bpos[:], 15, None, ALU.bitwise_and))
                step(V.tensor_copy(bijf[:], bij[:]))
                pf = posf[:].rearrange("p (h s) i -> p h s i", s=2)
                oh4 = onehot[:].rearrange("p (h k) i -> p h k i", h=PEER_HEADS)
                for s in range(2):
                    step(V.tensor_tensor(onehot[:], bijf[:, s, :].unsqueeze(2).broadcast_to([P, SLOTS, 16]),
                                         cst[:, C_IOTA:C_IOTA + 16].unsqueeze(1).broadcast_to([P, SLOTS, 16]),
                                         ALU.is_equal))
                    step(V.tensor_tensor(oh4, oh4, pf[:, :, s, :].unsqueeze(2).broadcast_to(four), ALU.mult))
                    step(V.tensor_reduce(eij[:, s, :], onehot[:], AX, ALU.add))
                step(V.scalar_tensor_tensor(eidf[:, t, :], eij[:, 0, :], float(KEYS), eij[:, 1, :],
                                            ALU.mult, ALU.add))
                V.tensor_copy(eid[:, t, :], eidf[:, t, :]).then_inc(eid_ok, 1)
                dve.sem_inc(top_ok, 1)
                b3 = best[:].rearrange("p (h k) -> p h k", k=16)
                g3 = gate[:, t, :].rearrange("p (h k) -> p h k", k=16)
                V.tensor_tensor(g3, b3, b3[:, :, 0:1].broadcast_to([P, PEER_HEADS, 16]), ALU.subtract
                                ).then_inc(gcen_ok, 1)
                dve.wait_ge(gexp_ok, t + 1)
                step(V.tensor_reduce(gsum[:, t, 0, :], g3, AX, ALU.add))
                step(V.reciprocal(gsum[:, t, 1, :], gsum[:, t, 0, :]))
                step(V.tensor_tensor(g3, g3, gsum[:, t, 1, :].unsqueeze(2).broadcast_to([P, PEER_HEADS, 16]),
                                     ALU.mult))

            rounds = SLOTS // RING
            for t in range(NT):
                with dve.Fori(0, rounds) as r:
                    N = r + t * rounds
                    for j in range(RING):
                        dve.wait_ge(row_in[j], 16 * N + 16)
                        V.tensor_tensor_reduce(out=rows[:, j, :], in0=rows[:, j, :], in1=hnat[:, t, :], scale=1.0,
                                               scalar=0.0, op0=ALU.mult, op1=ALU.add, accum_out=dring[:, j:j + 1]
                                               ).then_inc(row_used, 1)
                    dve.wait_ge(row_used, N * RING + 2 * RING)
                    V.tensor_scalar(dots[:, t, bass.ds(r * RING, RING)], dring[:], 1.0, None, ALU.mult
                                    ).then_inc(dots_ok, 1)
                    dve.wait_ge(dots_ok, N + 1)
            step(V.memset(mixed[:], 0.0), hold=False)
            for t in range(NT):
                dve.wait_ge(gelu_ok, t + 1)
                step(V.tensor_tensor(coef[:, t, :], gelu[:, t, :], gate[:, t, :], ALU.mult))
            dve.wait_ge(gb_in, 32)
            for t in range(NT):
                with dve.Fori(0, rounds) as r:
                    N = r + (NT + t) * rounds
                    for j in range(RING):
                        dve.wait_ge(row_in[j], 16 * N + 16)
                        dve.wait_ge(row_used, N * RING + (RING + j))
                        V.scalar_tensor_tensor(mixed[:, t, :], rows[:, j, :], coef[:, t, bass.ds(r * RING + j, 1)],
                                               mixed[:, t, :], ALU.mult, ALU.add).then_inc(row_used, 1)
                dve.wait_ge(row_used, (NT + t + 1) * rounds * RING + RING)
                f = fstat[:, t, :]
                step(V.scalar_tensor_tensor(y[:, t, :], hnat[:, t, :], ALPHA, mixed[:, t, :], ALU.mult, ALU.add,
                                            accum_out=f[:, 0:1]))
                step(V.tensor_scalar(f[:, 1:2], f[:, 0:1], 1.0 / D, None, ALU.mult))
                step(V.tensor_scalar(y[:, t, :], y[:, t, :], f[:, 1:2], None, ALU.subtract))
                step(V.tensor_tensor_reduce(out=mixed[:, t, :], in0=y[:, t, :], in1=y[:, t, :], scale=1.0, scalar=0.0,
                                            op0=ALU.mult, op1=ALU.add, accum_out=f[:, 4:5]))
                V.tensor_scalar(f[:, 2:3], f[:, 4:5], 1.0 / D, LN_EPS, ALU.mult, ALU.add).then_inc(var_ok, 1)
                dve.wait_ge(rt_ok, t + 1)
                step(V.reciprocal(f[:, 5:6], f[:, 3:4]))
                step(V.scalar_tensor_tensor(y[:, t, :], y[:, t, :], f[:, 5:6], gb[:, 0, :], ALU.mult, ALU.mult))
                V.tensor_tensor(y[:, t, :], y[:, t, :], gb[:, 1, :], ALU.add).then_inc(y_ok, 1)


def shape_table():
    import numpy as np

    t = np.zeros((P, C_END), np.float32)
    p, s = np.arange(P)[:, None], np.arange(TOK)[None, :]
    t[:, C_ID:C_ID + P] = np.eye(P)
    t[:, C_ONE:C_ONE + P] = 1.0 / D
    for b in range(NT):
        t[:, C_CAUSAL + b * TOK:C_CAUSAL + (b + 1) * TOK] = np.where(s <= p + b * P, 0.0, NEG)
    for g, w in enumerate(WINDOWS):
        t[:, C_CNT + g * TOK:C_CNT + (g + 1) * TOK] = 1.0 / np.minimum(s + 1, w)
    dist = np.maximum(TOK - 1 - np.arange(384), 0)
    exact = BUCKETS // 2
    far = exact + (np.log(np.maximum(dist, 1) / exact) / np.log(128 / exact) * (BUCKETS - exact)).astype(np.int32)
    bucket = np.where(dist < exact, dist, np.minimum(far, BUCKETS - 1))
    t[0:BUCKETS, C_HOT:C_HOT + 384] = bucket[None, :] == np.arange(BUCKETS)[:, None]
    t[:, C_IOTA:C_IOTA + 16] = np.arange(16)
    return t


_INS = {"x": "x", "norm1_g": "norm1_g", "norm2_g": "norm2_g", "mlp_w1": "mlp_w1", "mlp_w2": "mlp_w2",
        "cc_w_in": "cc_w_in", "cc_b_in": "cc_b_in", "cc_dw": "cc_dw", "cc_dw_b": "cc_dw_b", "cc_ln_g": "cc_ln_g",
        "cc_ln_b": "cc_ln_b", "cc_w_out": "cc_w_out", "cc_b_out": "cc_b_out", "final_g": "final_g",
        "w_in_2": "w_in_2", "pool_w_2": "pool_w", "pool_scale_2": "pool_scale", "rel_bias_2": "rel_bias",
        "w_out_2": "w_out_2", "ln1_g_2": "ln1_g", "ln1_b_2": "ln1_b", "peer_wq_2": "peer_wq",
        "peer_subkeys_2": "peer_subkeys", "peer_u_2": "peer_u", "peer_v_2": "peer_v", "ln2_g_2": "ln2_g",
        "ln2_b_2": "ln2_b"}


def kernel(**inputs):
    import numpy as _np
    import concourse.bacc as _bacc
    from concourse import mybir as _mybir
    from concourse.bass_utils import run_bass_kernel_spmd as _run

    nc = _bacc.Bacc("TRN2", target_bir_lowering=False, num_devices=1)
    arrays, args = {}, {}
    for name, short in _INS.items():
        arr = _np.ascontiguousarray(inputs[name])
        arrays[f"in_{name}"] = arr
        args[short] = nc.dram_tensor(f"in_{name}", arr.shape, _mybir.dt.from_np(arr.dtype), kind="ExternalInput").ap()
    table = shape_table()
    arrays["in_table"] = table
    args["table"] = nc.dram_tensor("in_table", table.shape, F32, kind="ExternalInput").ap()
    out = nc.dram_tensor("out_0", (1, TOK, D), F32, kind="ExternalOutput").ap()
    build(nc, args, out)
    r = _run(nc, [arrays], core_ids=[0])
    return r.results[0]["out_0"]
```

```python
from contextlib import ExitStack

import concourse.bass as bass
from concourse import mybir

F32 = mybir.dt.float32
F32R = mybir.dt.float32r
U32 = mybir.dt.uint32
ACT = mybir.ActivationFunctionType
ALU = mybir.AluOpType
AX = mybir.AxisListType.X

P = 128
TOK = 256
NT = TOK // P
D = 2048
KT = D // P
D_FF = 4 * D
TAPS = 31
PAD = TAPS - 1
LN_EPS, RMS_EPS = 1e-5, 1e-6
ALPHA = 2 ** 0.25
HEADS = 8
IDX_HEADS = 16
IDX_DIM = 64
IDX_SCALE = (IDX_HEADS * IDX_DIM) ** -0.5
TOPK = 64
NEG = -1e30
TAKEN = -3e38
WINDOWS = (2, 4, 8, 16)
BUCKETS = 32
PEER_HEADS = 8
PEER_TOPK = 16
KEYS = 128
SLOTS = PEER_HEADS * PEER_TOPK
RING = 8

G_IN, G_OUT, G_MLP, G_PROJ, G_MIX, G_QRY, G_END = 0, 8, 12, 44, 54, 58, 62
SUBS = 8

C_ID, C_ONE, C_CAUSAL, C_CNT, C_HOT, C_IOTA, C_END = 0, 128, 256, 768, 1792, 2176, 2192
V_N1, V_N2, V_FIN, V_BV, V_BG, V_DWB, V_LNG, V_LNB, V_BOUT, V_L1G, V_L1B, V_PSC, V_END = (
    0, 16, 32, 48, 64, 80, 96, 112, 128, 144, 160, 176, 184)

PROJ_ORDER = (8, 9, 0, 1, 4, 5, 2, 3, 6, 7)


def build(nc, a, out):
    with ExitStack() as ctx:
        def sem(name):
            return ctx.enter_context(nc.semaphore(name))

        def at(name, offset, shape, dtype=F32):
            return nc.alloc_sbuf_tensor_at(name, [shape[0], *shape[1:]], dtype, offset=offset)

        KB = 1024
        base = (nc.sbuf_base + 63) // 64 * 64
        o_x, o_t, o_ah, o_al = base, base + 16 * KB, base + 32 * KB, base + 48 * KB
        o_raw, o_hi, o_lo = base + 64 * KB, base + 96 * KB, base + 112 * KB
        o_z = base + 128 * KB
        o_c = o_z + 64 * KB

        X = at("X", o_x, [P, KT, TOK])
        T = at("T", o_t, [P, KT, TOK])
        A_hi = at("A_hi", o_ah, [P, KT, TOK], F32R)
        A_lo = at("A_lo", o_al, [P, KT, TOK], F32R)
        raw = at("raw", o_raw, [P, 4, 4, 512])
        w_hi = at("w_hi", o_hi, [P, 4, 2, 512], F32R)
        w_lo = at("w_lo", o_lo, [P, 4, 2, 512], F32R)

        cst = at("cst", o_c, [P, C_END])
        o = o_c + C_END * 4
        VT = at("VT", o, [P, V_END]); o += V_END * 4
        dwT = at("dwT", o, [P, KT, 32]); o += KT * 32 * 4
        mean_sb = at("mean_sb", o, [P, TOK]); o += TOK * 4
        root = at("root", o, [P, TOK]); o += TOK * 4
        rstd = at("rstd", o, [P, TOK]); o += TOK * 4
        rb = at("rb", o, [BUCKETS, HEADS]); o += 64
        assert o <= nc.sbuf_usable_end, (o, nc.sbuf_usable_end)
        ident = cst[:, C_ID:C_ID + P]
        ones = cst[:, C_ONE:C_ONE + P]

        xnat = at("xnat", o_z + 16 * KB, [P, NT, D])
        xsc = at("xsc", o_z + 32 * KB, [P, NT, D])
        dwn = at("dwn", o_x, [32, D])
        vrow = at("vrow", o_x + 8 * KB, [P, 2, P])
        rbB = at("rbB", o_z + 44 * KB, [BUCKETS, HEADS, P])
        xstat = at("xstat", o_x + 13 * KB, [P, NT, 8])
        brow = at("brow", o_z + 32 * KB, [P, HEADS, 384])
        Z = at("Z", o_z, [P, KT, TOK])
        B_hi = at("B_hi", o_z + 16 * KB, [P, KT, TOK], F32R)
        B_lo = at("B_lo", o_z + 32 * KB, [P, KT, TOK], F32R)
        upad = at("upad", o_z + 48 * KB, [P, 2, PAD + TOK])
        sig = at("sig", o_z + 51 * KB, [P, 2, TOK])
        relu = at("relu", o_z + 48 * KB, [P, 4, TOK])
        sq = at("sq", o_z + 52 * KB, [P, 4, TOK])
        tile_sum = at("tile_sum", o_z + 56 * KB, [P, TOK])
        rstd2 = at("rstd2", o_z + 57 * KB, [P, TOK])
        xsq = at("xsq", o_z + 58 * KB, [P, 4, TOK])
        proj = at("proj", o_z, [P, 40, TOK])
        wt = at("wt", o_z + 48 * KB, [P, KT, 144])
        BT = at("BT", o_z + 40 * KB, [P, HEADS, TOK])
        kidx = at("kidx", o_z + 58 * KB, [P, TOK])
        widx = at("widx", o_z + 59 * KB, [P, NT, IDX_HEADS])
        score = at("score", o_z + 59 * KB + 256, [P, TOK])
        work = at("work", o_z + 60 * KB + 256, [P, TOK])
        keep = at("keep", o_z + 61 * KB + 256, [P, NT, TOK])
        top8 = at("top8", o_z + 63 * KB + 256, [P, 8])
        stat = at("stat", o_z + 63 * KB + 512, [P, 2, HEADS])
        mix_sum = at("mix_sum", o_z + 56 * KB, [P, TOK])
        L = (at("L0", o_z + 32 * KB, [P, HEADS, P]), at("L1", o_z + 48 * KB, [P, HEADS, TOK]))
        pT = (at("pT0", o_z + 36 * KB, [P, HEADS, P]), at("pT1", o_t, [P, 2 * HEADS, P]))
        poolw = at("poolw", o_t, [P, 4, 2, 256])
        pbuf = at("pbuf", o_t + 8 * KB, [P, 2, 2, 16 + TOK])
        vnat = at("vnat", o_t + 8 * KB, [P, NT, HEADS * P])
        qh = at("qh", o_z, [P, KT, TOK])
        hnat = at("hnat", o_z + 16 * KB, [P, NT, D])
        s_sc = (at("s_sc0", o_z + 32 * KB, [P, KT, KEYS]), at("s_sc1", o_z + 40 * KB, [P, KT, KEYS]))
        o = o_z + 48 * KB
        s_wk = at("s_wk", o, [P, 4, KEYS]); o += 2 * KB
        cand = at("cand", o, [P, 2, 256]); o += 2 * KB
        cwork = at("cwork", o, [P, 2, 256]); o += 2 * KB
        onehot = at("onehot", o, [P, 2, 32, PEER_TOPK]); o += 4 * KB
        subk = at("subk", o, [P, 2, P]); o += KB
        subT = at("subT", o, [P, 2, KEYS]); o += KB
        val16 = at("val16", o, [P, 4, 16]); o += 256
        pos16 = at("pos16", o, [P, 4, 16], U32); o += 256
        posf = at("posf", o, [P, 4, 16]); o += 256
        best = at("best", o, [P, 32]); o += 128
        bpos = at("bpos", o, [P, 32], U32); o += 128
        bij = at("bij", o, [P, 2, 32], U32); o += 256
        bijf = at("bijf", o, [P, 2, 32]); o += 256
        eij = at("eij", o, [P, 2, 32]); o += 256
        assert o <= o_z + 64 * KB
        o = o_t
        eidf = at("eidf", o, [P, NT, SLOTS]); o += KB
        eid = at("eid", o, [P, NT, SLOTS], U32); o += KB
        gate = at("gate", o, [P, NT, SLOTS]); o += KB
        gsum = at("gsum", o, [P, NT, PEER_HEADS]); o += 64
        dots = at("dots", o, [P, NT, SLOTS]); o += KB
        gelu = at("gelu", o, [P, NT, SLOTS]); o += KB
        coef = at("coef", o, [P, NT, SLOTS]); o += KB
        ering = at("ering", o, [P, 2, RING], U32); o += 64
        dring = at("dring", o, [P, RING]); o += 32
        bn = at("bn", o, [P, NT, 4, 6]); o += 192
        fstat = at("fstat", o, [P, NT, 8]); o += 64
        assert o <= o_t + 16 * KB
        rows = at("rows", o_raw, [P, RING, D])
        mixed = at("mixed", o_ah, [P, NT, D])
        gb = at("gb", o_al, [P, 2, D])
        y = at("y", o_x, [P, NT, D])

        def psum(name):
            return ctx.enter_context(nc.psum_tensor(name, [P, 512], F32))

        bank = [psum(f"bank{m}") for m in range(4)]
        misc = [psum(f"misc{m}") for m in range(4)]
        scratch = nc.dram_tensor("bias_rows", [HEADS * P * 384], F32).ap()

        def sems(*names):
            return [sem(n) for n in names]

        raw_in = sems(*[f"raw_in{c}" for c in range(4)])
        hi_done, lo_done = sems("hi_done", "lo_done")
        sub_used = sem("sub_used")
        bank_done = sems(*[f"bank_done{m}" for m in range(4)])
        bank_free = sems(*[f"bank_free{m}" for m in range(4)])
        act_pass, pool_pass = sems("act_pass", "pool_pass")
        cst_in, cst2_in, vec_in, dw_in, rb_in = sems("cst_in", "cst2_in", "vec_in", "dw_in", "rb_in")
        x_in = sems(*[f"x_in{c}" for c in range(4)])
        xsq_ok, xeps_ok, xroot_ok, xsc_ok, xT_ps = sems("xsq_ok", "xeps_ok", "xroot_ok", "xsc_ok", "xT_ps")
        xadd_ok, ssq_ok, sum_ok, proj_ok = sems("xadd_ok", "ssq_ok", "sum_ok", "proj_ok")
        part_ok = sem("part_ok")
        vt_ps, vt_ok, x_ps, x_ok = sems("vt_ps", "vt_ok", "x_ps", "x_ok")
        rbB_ok, brow_ps, brow_ok, brow_out = sems("rbB_ok", "brow_ps", "brow_ok", "brow_out")
        conv_step, dve_step, act_step = sems("conv_step", "dve_step", "act_step")
        rsq_ok, hidh_ok, hid_ok = sems("rsq_ok", "hidh_ok", "hid_ok")
        NORMS = ("rms1", "lnc", "rms2", "rms3", "ln1")
        n_mean, n_meansb, n_cent, n_sq, n_var, n_eps, n_root, n_rstd, n_out, n_hi, n_op = (
            {n: sem(f"{n}_{what}") for n in NORMS if n[0] == "l" or what not in ("meansb", "cent", "var")}
            for what in ("mean", "meansb", "cent", "sq", "var", "eps", "root", "rstd", "out", "hi", "op"))
        silu_ok, pads_ok = sems("silu_ok", "pads_ok")
        wt_in, poolw_in, BT_in, tail_ps, tail_ok = sems("wt_in", "poolw_in", "BT_in", "tail_ps", "tail_ok")
        pooled_ok, pool_ps, pm_ok, pm_hi, mix_op = sems("pooled_ok", "pool_ps", "pm_ok", "pm_hi", "mix_op")
        idx_ps, idx_rel, idx_acc = sems("idx_ps", "idx_rel", "idx_acc")
        v_ps, v_ok, lg_ps, lg_ok, cen_ok, exp_ok, prob_ok = sems(
            "v_ps", "v_ok", "lg_ps", "lg_ok", "cen_ok", "exp_ok", "prob_ok")
        pT_ps, pT_ok, att_ps, att_hi, att_lo = sems("pT_ps", "pT_ok", "att_ps", "att_hi", "att_lo")
        subk_in, subT_ps, subT_ok, hn_ps, hn_ok = sems("subk_in", "subT_ps", "subT_ok", "hn_ps", "hn_ok")
        key_ps, key_ok, top_ok, gcen_ok, gexp_ok, eid_ok = sems(
            "key_ps", "key_ok", "top_ok", "gcen_ok", "gexp_ok", "eid_ok")
        row_in = sems(*[f"row_in{j}" for j in range(RING)])
        row_used, ering_ok, dots_ok, gelu_ok, coef_ok = sems("row_used", "ering_ok", "dots_ok", "gelu_ok", "coef_ok")
        gb_in, var_ok, rt_ok, y_ok, y_out = sems("gb_in", "var_ok", "rt_ok", "y_ok", "y_out")

        class Steps:

            def __init__(self, engine, semaphore):
                self.engine, self.semaphore, self.count = engine, semaphore, 0

            def __call__(self, instruction, hold=True):
                instruction.then_inc(self.semaphore, 1)
                self.count += 1
                if hold:
                    self.engine.wait_ge(self.semaphore, self.count)

        w_conv = a["cc_w_in"][0].rearrange("(k p) (h g n) -> g p k h n", p=P, h=2, n=256)
        w_co = a["cc_w_out"][0].rearrange("(k p) (g n) -> g p k n", p=P, n=512)
        w_1 = a["mlp_w1"][0].rearrange("(k p) (q g n) -> q g p k n", p=P, q=4, n=512)
        w_2 = a["mlp_w2"][0].rearrange("(q k p) (g n) -> q g p k n", p=P, q=4, n=512)
        w_pr = a["w_in_2"][0][:, 0:5120].rearrange("(k p) (g n) -> g p k n", p=P, n=512)
        w_mx = a["w_out_2"][0].rearrange("(k p) (g n) -> g p k n", p=P, n=512)
        w_qr = a["peer_wq"][0].rearrange("(k p) (g n) -> g p k n", p=P, n=512)

        def same_rows(first, n, per):
            for start in range(first, first + n, 2 * per):
                for odd in range(2):
                    yield from range(start + odd, start + 2 * per, 2)

        block = ctx.enter_context(nc.Block())

        @block.sync
        def _(sp):
            def conv_chunk(c, g):
                for half in range(2):
                    sp.dma_start(raw[:, c, :, 256 * half:256 * half + 256],
                                 w_conv[bass.ds(g, 1), :, 4 * c:4 * c + 4, half, :]
                                 .rearrange("o p k n -> (o p) k n")).then_inc(raw_in[c], 16)

            def chunk(c, view, g, G):
                sp.wait_ge(lo_done, G * SUBS + (2 * c + 2 - SUBS))
                sp.dma_start(raw[:, c, :, :], view[bass.ds(g, 1), :, 4 * c:4 * c + 4, :]
                             .rearrange("o p k n -> (o p) k n")).then_inc(raw_in[c], 16)

            sp.dma_start(cst[:, 0:C_CAUSAL], a["table"][:, 0:C_CAUSAL]).then_inc(cst_in, 16)
            for c in range(4):
                cols = slice(c * D // 4, (c + 1) * D // 4)
                sp.dma_start(xnat[:, :, cols], a["x"][0].rearrange("(t p) d -> p t d", p=P)[:, :, cols]
                             ).then_inc(x_in[c], 16)
            for c in range(4):
                conv_chunk(c, 0)
            sp.dma_start(cst[:, C_CAUSAL:C_END], a["table"][:, C_CAUSAL:C_END]).then_inc(cst2_in, 16)
            with sp.Fori(1, G_OUT) as g:
                for c in range(4):
                    sp.wait_ge(lo_done, g * SUBS + (2 * c + 2 - SUBS))
                    conv_chunk(c, g)
            with sp.Fori(0, 4) as g:
                for c in range(4):
                    chunk(c, w_co, g, g + G_OUT)
            with sp.Fori(0, 4) as q:
                for part, view in enumerate((w_1, w_2)):
                    with sp.Fori(0, 4) as g:
                        for c in range(4):
                            chunk(c, view[bass.ds(q, 1)].rearrange("o g p k n -> (o g) p k n"), g,
                                  q * 8 + g + (G_MLP + 4 * part))
            for i, g in enumerate(PROJ_ORDER):
                for c in range(4):
                    chunk(c, w_pr, g, G_PROJ + i)
            for view, G0, n in ((w_mx, G_MIX, 4), (w_qr, G_QRY, 4)):
                with sp.Fori(0, n) as g:
                    for c in range(4):
                        chunk(c, view, g, g + G0)
            sp.wait_ge(bank_done[3], G_END)
            for i, name in enumerate(("ln2_g", "ln2_b")):
                sp.dma_start(gb[:, i, :], a[name].broadcast_to([P, D])).then_inc(gb_in, 16)
            for t in range(NT):
                for half in range(2):
                    cols = slice(half * D // 2, (half + 1) * D // 2)
                    sp.wait_ge(y_ok, 2 * t + half + 1)
                    sp.dma_start(out[0, t * P:(t + 1) * P, cols], y[:, t, cols]).then_inc(y_out, 16)
            sp.wait_ge(y_out, 2 * 16 * NT)

        @block.gpsimd
        def _(pool):
            with pool.Fori(0, G_END) as G:
                for s in range(SUBS):
                    pool.wait_ge(hi_done, G * SUBS + (s + 1))
                    nc.gpsimd.tensor_tensor(w_lo[:, s % 4], raw[:, s // 2, 2 * (s % 2):2 * (s % 2) + 2, :],
                                            w_hi[:, s % 4].bitcast(F32), ALU.subtract).then_inc(lo_done, 1)

            def gather(table, t, first, n):
                with pool.Fori(0, n // (2 * RING)) as r:
                    for half in range(2):
                        nc.gpsimd.tensor_copy(ering[:, half, :],
                                              eid[:, t, bass.ds((2 * r + half) * RING + first % SLOTS, RING)]
                                              ).then_inc(ering_ok, 1)
                        pool.wait_ge(ering_ok, 2 * r + (half + 1 + first // RING))
                        for j in range(RING):
                            pool.wait_ge(row_used, (2 * r + half) * RING + (first + j + 1))
                            pool.sem_inc(pool_pass, 1)
                            pool.indirect_dma_start(rows[:, j, :], None, table,
                                                    bass.IndirectOffsetOnAxis(ering[:, half, j:j + 1], 0)
                                                    ).then_inc(row_in[j], 16)

            pool.wait_ge(bank_done[3], G_END)
            for t in range(NT):
                for g in range(4):
                    pool.wait_ge(eid_ok, 4 * t + g + 1)
                    gather(a["peer_u"][0], t, t * SLOTS + g * SLOTS // 4, SLOTS // 4)
            for t in range(NT):
                gather(a["peer_v"][0], t, (NT + t) * SLOTS, SLOTS)

        @block.tensor
        def _(pe):
            def group(hi, lo, G, ready, base, step, order, hooks):
                for s in range(SUBS):
                    if s in hooks:
                        hooks[s]()
                    pe.wait_ge(ready, base + step * (s + 1))
                    pe.wait_ge(lo_done, G * SUBS + (s + 1))
                    for m in range(4):
                        if s == 0:
                            pe.wait_ge(bank_free[m], G + 1)
                        for k in range(2):
                            wh = w_hi[:, s % 4, k, order[m] * P:(order[m] + 1) * P]
                            wl = w_lo[:, s % 4, k, order[m] * P:(order[m] + 1) * P]
                            dst, kt = bank[m][:, 0:TOK], 2 * s + k
                            nc.tensor.matmul(dst, wh, hi[:, kt, :], start=(kt == 0), stop=False)
                            nc.tensor.matmul(dst, wh, lo[:, kt, :], start=False, stop=False)
                            last = nc.tensor.matmul(dst, wl, hi[:, kt, :], start=False, stop=(kt == KT - 1))
                        if s == SUBS - 1:
                            last.then_inc(bank_done[m], 1)
                    if s < SUBS - 1:
                        last.then_inc(sub_used, 1)

            def groups(hi, lo, G0, n, ready, base=0, step=1, order=(0, 1, 2, 3), hooks={}):
                if n == 1:
                    return group(hi, lo, G0, ready, base, step, order, hooks)
                with pe.Fori(0, n) as g:
                    group(hi, lo, g + G0, ready, base, step, order, hooks)

            def column_means(dst, src, ready, done):
                for k in range(KT):
                    ready(k)
                    last = nc.tensor.matmul(dst[:, 0:TOK], ones, src[:, k, :], start=(k == 0), stop=(k == KT - 1))
                last.then_inc(done, 1)

            def mean_of_sum(ready, value, done):
                pe.wait_ge(ready, value)
                nc.tensor.matmul(misc[0][:, 0:TOK], ones, tile_sum[:], start=True, stop=True).then_inc(done, 1)

            for m in range(4):
                pe.sem_inc(bank_free[m], 1)
            pe.wait_ge(cst_in, 16)
            pe.wait_ge(vec_in, 16 * 11)
            nc.tensor.transpose(bank[0][:, 0:P], vrow[:, 0, :], ident)
            nc.tensor.transpose(bank[0][:, P:V_END], vrow[0:V_END - P, 1, :], ident[0:V_END - P, 0:V_END - P]
                                ).then_inc(vt_ps, 1)
            pe.wait_ge(dw_in, 16)
            pe.wait_ge(pads_ok, 1)
            for k in range(KT):
                last = nc.tensor.transpose(bank[1][:, 32 * k:32 * k + 32], dwn[:, k * P:(k + 1) * P], ident[0:32, 0:32])
            last.then_inc(vt_ps, 1)

            def to_channels(src, done, free, per):
                for r in range(KT // 2):
                    if r >= 4:
                        pe.wait_ge(free, per * (r - 3))
                    for i in range(4):
                        k, t = 2 * r + i // 2, i % 2
                        last = nc.tensor.transpose(misc[r % 4][:, i * P:(i + 1) * P], src[:, t, k * P:(k + 1) * P], ident)
                    last.then_inc(done, 1)

            pe.wait_ge(xsc_ok, 2)
            to_channels(xsc, x_ps, n_out["rms1"], 2)
            pe.wait_ge(vt_ok, 2)
            swap = (2, 3, 0, 1)
            groups(A_hi, A_lo, G_IN, 1, n_op["rms1"], order=swap)
            pe.wait_ge(n_out["rms1"], KT)
            to_channels(xnat, xT_ps, x_ok, 1)
            pe.wait_ge(x_ok, 8)
            pe.wait_ge(cst2_in, 16)
            pe.wait_ge(rbB_ok, 1)
            for h in range(HEADS):
                if h >= 4:
                    pe.wait_ge(brow_ok, h - 3)
                nc.tensor.matmul(misc[h % 4][:, 0:384], rbB[:, h, :], cst[0:BUCKETS, C_HOT:C_HOT + 384],
                                 start=True, stop=True).then_inc(brow_ps, 1)
            groups(A_hi, A_lo, G_IN + 1, 7, n_op["rms1"], order=swap)

            pe.wait_ge(brow_ok, HEADS)
            column_means(misc[0], Z, lambda k: pe.wait_ge(conv_step, 2 * TAPS * (k // 2 + 1)), n_mean["lnc"])
            column_means(misc[1], T, lambda k: pe.wait_ge(n_sq["lnc"], k // 4 + 1), n_var["lnc"])
            groups(B_hi, B_lo, G_OUT, 4, n_op["lnc"])

            groups(A_hi, A_lo, G_MLP, 4, n_op["rms2"], step=2)
            mean_of_sum(ssq_ok, KT, n_mean["rms2"])
            groups(B_hi, B_lo, G_MLP + 4, 4, hid_ok, step=2)
            with pe.Fori(1, 4) as q:
                groups(A_hi, A_lo, q * 8 + G_MLP, 4, n_op["rms2"], step=2)
                groups(B_hi, B_lo, q * 8 + (G_MLP + 4), 4, hid_ok, base=q * KT, step=2)

            def project(i, hooks={}):
                groups(A_hi, A_lo, G_PROJ + i, 1, n_op["rms3"], step=2, hooks=hooks)

            def index_scores(b, heads):
                nk = P * (b + 1)
                per = 512 // nk
                for f in range(len(heads) // per):
                    for i in range(per):
                        h = heads[f * per + i]
                        lo64 = IDX_DIM * (h % 2)
                        last = nc.tensor.matmul(misc[f][:, i * nk:(i + 1) * nk],
                                                proj[lo64:lo64 + IDX_DIM, 32 + h // 2, b * P:(b + 1) * P],
                                                kidx[lo64:lo64 + IDX_DIM, 0:nk], start=True, stop=True)
                    last.then_inc(idx_ps, 1)

            project(0, {5: lambda: mean_of_sum(ssq_ok, 2 * KT, n_mean["rms3"])})
            project(1)
            pe.wait_ge(wt_in, 48)
            pe.wait_ge(n_out["rms3"], 2 * KT)
            for k in range(KT):
                nc.tensor.matmul(misc[0][:, 0:TOK], wt[:, k, 0:P], X[:, k, :], start=(k == 0), stop=(k == KT - 1))
            for t in range(NT):
                for k in range(KT):
                    last = nc.tensor.matmul(misc[1][:, t * 16:t * 16 + 16], X[:, k, t * P:(t + 1) * P],
                                            wt[:, k, P:P + 16], start=(k == 0), stop=(k == KT - 1))
            last.then_inc(tail_ps, 1)
            def first_scores():
                pe.wait_ge(tail_ok, 2)
                pe.wait_ge(proj_ok, 8)
                index_scores(1, list(same_rows(0, 8, 2)))
            project(2, {2: first_scores})
            pe.wait_ge(idx_acc, 8)
            index_scores(1, list(same_rows(8, 8, 2)))
            project(3)
            pe.wait_ge(idx_acc, 16)
            index_scores(0, list(same_rows(0, 16, 4)))
            project(4)
            project(5)
            project(6)
            pe.wait_ge(poolw_in, 16)
            pe.wait_ge(idx_acc, 32)
            for g in range(4):
                pe.wait_ge(pooled_ok, g + 1)
                for o in range(2):
                    for c in range(2):
                        last = nc.tensor.matmul(misc[g][:, o * TOK:(o + 1) * TOK], poolw[:, g, c, o * P:(o + 1) * P],
                                                proj[:, 2 * g + c, :], start=(c == 0), stop=(c == 1))
                last.then_inc(pool_ps, 1)
            project(7)

            def logits(b, at_bank):
                nk = P * (b + 1)
                per = 512 // nk
                for f in range(HEADS // per):
                    for i in range(per):
                        h = f * per + i
                        last = nc.tensor.matmul(misc[at_bank + f][:, i * nk:(i + 1) * nk],
                                                proj[:, 8 + h, b * P:(b + 1) * P], proj[:, 16 + h, 0:nk],
                                                start=True, stop=True)
                    last.then_inc(lg_ps, 1)

            def keys_first(i, at_bank):
                for b in range(NT):
                    for h in range(4 * i, 4 * i + 4):
                        last = nc.tensor.transpose(misc[at_bank + b][:, (h % 4) * P:(h % 4 + 1) * P],
                                                   proj[:, 24 + h, b * P:(b + 1) * P], ident)
                    last.then_inc(v_ps, 1)

            def turn_probs(b):
                for r in range(2 * (b + 1)):
                    for i in range(4):
                        h, kb = divmod(4 * r + i, b + 1)
                        last = nc.tensor.transpose(misc[r][:, i * P:(i + 1) * P], L[b][:, h, kb * P:(kb + 1) * P], ident)
                    last.then_inc(pT_ps, 1)

            def first_logits():
                pe.wait_ge(pm_ok, 8)
                pe.wait_ge(proj_ok, 32)
                logits(1, 0)

            def second_logits():
                pe.wait_ge(lg_ok, HEADS)
                pe.wait_ge(proj_ok, 36)
                logits(0, 0)
                keys_first(0, 2)

            def probs_of_block_1():
                pe.wait_ge(v_ok, 2)
                pe.wait_ge(lg_ok, 2 * HEADS)
                pe.wait_ge(prob_ok, 1)
                turn_probs(1)

            project(8, {2: first_logits})
            project(9, {1: second_logits, 6: probs_of_block_1})
            pe.wait_ge(pT_ok, 4)
            pe.wait_ge(prob_ok, 2)
            turn_probs(0)
            pe.wait_ge(proj_ok, 40)
            keys_first(1, 2)
            for n, (b, i) in enumerate(((1, 0), (0, 0), (1, 1), (0, 1))):
                pe.wait_ge(pT_ok, 5 + n % 2 if n < 2 else 6)
                if n >= 2:
                    pe.wait_ge(v_ok, 4)
                for h in range(4 * i, 4 * i + 4):
                    for kb in range(b + 1):
                        last = nc.tensor.matmul(misc[n][:, (h % 4) * P:(h % 4 + 1) * P],
                                                vnat[:, kb, h * P:(h + 1) * P], pT[b][:, h * (b + 1) + kb, :],
                                                start=(kb == 0), stop=(kb == b))
                last.then_inc(att_ps, 1)
            groups(A_hi, A_lo, G_MIX, 4, mix_op)

            pe.wait_ge(sum_ok, KT)
            nc.tensor.matmul(misc[0][:, 0:TOK], ones, mix_sum[:], start=True, stop=True).then_inc(n_mean["ln1"], 1)
            column_means(misc[1], T, lambda k: pe.wait_ge(n_sq["ln1"], k // 4 + 1), n_var["ln1"])

            def keys_turned():
                pe.wait_ge(subk_in, 16)
                pe.wait_ge(n_op["ln1"], 8)
                for i in range(2):
                    last = nc.tensor.transpose(misc[0][:, i * P:(i + 1) * P], subk[:, i, :], ident)
                last.then_inc(subT_ps, 1)
                pe.wait_ge(subT_ok, 1)
                for r in range(8):
                    if r >= 4:
                        pe.wait_ge(hn_ok, r - 3)
                    for i in range(4):
                        t, k = r // 4, 4 * (r % 4) + i
                        last = nc.tensor.transpose(misc[r % 4][:, i * P:(i + 1) * P], X[:, k, t * P:(t + 1) * P], ident)
                    last.then_inc(hn_ps, 1)

            def key_scores(g):
                def work():
                    pe.wait_ge(bank_free[3], G_QRY + g + 2)
                    pe.wait_ge(hn_ok, 8)
                    if g >= 2:
                        pe.wait_ge(key_ok, 2 * (g - 1))
                    for t in range(NT):
                        for i in range(4):
                            last = nc.tensor.matmul(misc[2 * (g % 2) + t][:, i * P:(i + 1) * P],
                                                    qh[:, 4 * g + i, t * P:(t + 1) * P], subT[:, i % 2, :],
                                                    start=True, stop=True)
                        last.then_inc(key_ps, 1)
                return work

            groups(A_hi, A_lo, G_QRY, 1, n_op["ln1"], hooks={6: keys_turned})
            for g in range(1, 4):
                groups(A_hi, A_lo, G_QRY + g, 1, n_op["ln1"], hooks={2: key_scores(g - 1)})
            key_scores(3)()

        @block.scalar
        def _(act):
            def round_sub(G, s, raw_count):
                act.wait_ge(raw_in[s // 2], raw_count)
                if s >= 4:
                    act.wait_ge(sub_used, G * 7 + (s - 3))
                elif s == 3:
                    if not (isinstance(G, int) and G == 0):
                        act.wait_ge(bank_done[3], G)
                elif not (isinstance(G, int) and G == 0):
                    act.wait_ge(sub_used, G * 7 + (s - 2))
                nc.scalar.copy(w_hi[:, s % 4], raw[:, s // 2, 2 * (s % 2):2 * (s % 2) + 2, :]).then_inc(hi_done, 1)

            def ahead(G, now, then, last=False, middle=None):
                for s in range(3, SUBS):
                    round_sub(G, s, now)
                if middle:
                    middle()
                if not last:
                    for s in range(3):
                        round_sub(G + 1, s, then)

            def landed(G):
                return (G + 9) * 16

            def squares(n, src):
                for p in range(4):
                    act.wait_ge(n_cent[n], p + 1)
                    nc.scalar.activation(T[:, 4 * p:4 * p + 4, :], src[:, 4 * p:4 * p + 4, :], ACT.Square
                                         ).then_inc(n_sq[n], 1)

            def take_root(n):
                act.wait_ge(n_eps[n], 1)
                nc.scalar.activation(root[:], rstd[:], ACT.Sqrt).then_inc(n_root[n], 1)

            def rms_tiles(n, g, base):
                for m in range(4):
                    k = 4 * g + m
                    act.wait_ge(n_out[n], k + 1)
                    nc.scalar.copy(A_hi[:, k, :], T[:, k, :]).then_inc(n_hi[n], 1)
                    if base + k >= 4:
                        act.wait_ge(ssq_ok, base + k - 3)
                    nc.scalar.activation(xsq[:, m, :], X[:, k, :], ACT.Square).then_inc(n_sq[n], 1)

            VEC = (("norm1_g", V_N1), ("norm2_g", V_N2), ("final_g", V_FIN), ("cc_b_in", V_BV), ("cc_dw_b", V_DWB),
                   ("cc_ln_g", V_LNG), ("cc_ln_b", V_LNB), ("cc_b_out", V_BOUT), ("ln1_g", V_L1G),
                   ("ln1_b", V_L1B), ("pool_scale", V_PSC))
            for name, col in VEC:
                v = a[name].rearrange("(r c) -> r c", c=P) if name == "final_g" else a[name][0].rearrange("(r c) -> r c", c=P)
                act.dma_start(vrow[col % P:col % P + v.shape[0], col // P, :], v).then_inc(
                    vec_in, 16)
            act.dma_start(rb[:], a["rel_bias"]).then_inc(rb_in, 16)
            act.wait_ge(pads_ok, 1)
            act.dma_start(dwn[0:TAPS, :], a["cc_dw"][0]).then_inc(dw_in, 16)

            for c in range(4):
                act.wait_ge(x_in[c], 16)
                for t in range(NT):
                    nc.scalar.activation(T[:, 8 * t + 2 * c:8 * t + 2 * c + 2, :],
                                         xnat[:, t, 512 * c:512 * c + 512].rearrange("p (k n) -> p k n", k=2),
                                         ACT.Square, accum_out=xstat[:, t, c:c + 1]).then_inc(xsq_ok, 1)
            act.wait_ge(xeps_ok, 1)
            nc.scalar.activation(xstat[:, :, 6], xstat[:, :, 5], ACT.Sqrt).then_inc(xroot_ok, 1)
            act.wait_ge(vt_ps, 2)
            nc.scalar.copy(VT[:], bank[0][:, 0:V_END]).then_inc(vt_ok, 1)
            nc.scalar.copy(dwT[:], bank[1][:].rearrange("p (k j) -> p k j", j=32)).then_inc(vt_ok, 1)
            for s in range(3):
                round_sub(0, s, 32)
            for r in range(8):
                act.wait_ge(n_out["rms1"], 2 * r + 2)
                nc.scalar.copy(A_hi[:, 2 * r:2 * r + 2, :], T[:, 2 * r:2 * r + 2, :]).then_inc(n_hi["rms1"], 1)

            def gates(g):
                for i in range(2):
                    act.wait_ge(bank_done[i], g + 1)
                    act.wait_ge(bank_free[2 + i], g + 1)
                    act.sem_inc(act_pass, 1)
                    nc.scalar.activation(sig[:, i, :], bank[i][:, 0:TOK], ACT.Sigmoid,
                                         bias=VT[:, bass.ds(V_BG + i + 2 * g, 1)]).then_inc(bank_free[i], 1)

            ahead(0, 32, 64)
            gates(0)
            for r in range(8):
                act.wait_ge(xT_ps, r + 1)
                nc.scalar.copy(X[:, 2 * r:2 * r + 2, :], misc[r % 4][:].rearrange("p (k t) -> p k t", k=2)
                               ).then_inc(x_ok, 1)
            for h in range(HEADS):
                act.wait_ge(brow_ps, h + 1)
                nc.scalar.copy(brow[:, h, :], misc[h % 4][:, 0:384]).then_inc(brow_ok, 1)
            act.wait_ge(brow_ok, HEADS)
            act.dma_start(scratch.rearrange("(h p x) -> p h x", p=P, x=384), brow[:]).then_inc(brow_out, 16)
            with act.Fori(1, 7) as g:
                ahead(g, (g + 1) * 32, (g + 2) * 32)
                gates(g)
            ahead(7, 8 * 32, landed(8))
            gates(7)

            act.wait_ge(n_mean["lnc"], 1)
            nc.scalar.copy(mean_sb[:], misc[0][:, 0:TOK]).then_inc(n_meansb["lnc"], 1)
            squares("lnc", Z)
            take_root("lnc")
            for p in range(4):
                act.wait_ge(n_out["lnc"], p + 1)
                for k in range(4 * p, 4 * p + 4):
                    nc.scalar.activation(T[:, k, :], Z[:, k, :], ACT.Silu, bias=VT[:, V_LNB + k:V_LNB + k + 1],
                                         scale=VT[:, V_LNG + k:V_LNG + k + 1]).then_inc(silu_ok, 1)
                act.wait_ge(silu_ok, 4 * (p + 1))
                nc.scalar.copy(B_hi[:, 4 * p:4 * p + 4, :], T[:, 4 * p:4 * p + 4, :]).then_inc(n_hi["lnc"], 1)
            for g in range(4):
                ahead(G_OUT + g, landed(G_OUT + g), landed(G_OUT + g + 1))
                rms_tiles("rms2", g, 0)

            def mlp_in(q):
                for g in range(4):
                    G = q * 8 + (G_MLP + g)
                    ahead(G, landed(G), landed(G + 1))
                    for m in range(4):
                        act.wait_ge(bank_done[m], G + 1)
                        act.wait_ge(rsq_ok, q * 16 + (4 * g + m + 1))
                        nc.scalar.activation(relu[:, m, :], bank[m][:, 0:TOK], ACT.Relu).then_inc(bank_free[m], 1)
                    for m in range(4):
                        act.wait_ge(bank_free[m], G + 2)
                        nc.scalar.activation(B_hi[:, 4 * g + m, :], relu[:, m, :], ACT.Square).then_inc(hidh_ok, 1)
                    act.wait_ge(hidh_ok, q * 16 + (4 * g + 4))

            def mlp_out(q):
                with act.Fori(0, 4) as g:
                    G = q * 8 + g + (G_MLP + 4)
                    ahead(G, landed(G), landed(G + 1))

            mlp_in(0)
            take_root("rms2")
            mlp_out(0)
            with act.Fori(1, 3) as q:
                mlp_in(q)
                mlp_out(q)
            mlp_in(3)
            for g in range(4):
                G = G_MLP + 28 + g
                ahead(G, landed(G), landed(G + 1))
                rms_tiles("rms3", g, KT)

            def small_weights():
                take_root("rms3")
                act.wait_ge(n_op["rms3"], KT)
                act.wait_ge(n_mean["rms3"], 1)
                act.wait_ge(brow_out, 16)
                w2 = a["w_in_2"][0].rearrange("(k p) n -> p k n", p=P)
                for to, lo, n in ((0, 5120, 64), (64, 5120, 64), (128, 5184, 16)):
                    act.dma_start(wt[:, :, to:to + n], w2[:, :, lo:lo + n]).then_inc(wt_in, 16)
                act.dma_start(poolw[:], a["pool_w"][0].rearrange("g (c p) n -> p g c n", p=P)).then_inc(poolw_in, 16)
                for h in range(HEADS):
                    first = h * P * 384 + P - 1
                    act.dma_start(BT[:, h, :], scratch[first:first + P * 383].rearrange("(p x) -> p x", x=383)[:, 0:TOK]
                                  ).then_inc(BT_in, 16)

            def tail():
                act.wait_ge(tail_ps, 1)
                act.wait_ge(n_op["rms3"], KT)
                nc.scalar.copy(kidx[:], misc[0][:, 0:TOK]).then_inc(tail_ok, 1)
                nc.scalar.mul(widx[:], misc[1][:, 0:32].rearrange("p (t h) -> p t h", t=NT), IDX_SCALE
                              ).then_inc(tail_ok, 1)

            def index_relu(first):
                def work():
                    for n in range(first, first + 4):
                        act.wait_ge(idx_ps, n + 1)
                        nc.scalar.activation(misc[n % 4][:], misc[n % 4][:], ACT.Relu).then_inc(idx_rel, 1)
                return work

            def pool_scaled():
                for g in range(4):
                    act.wait_ge(pool_ps, g + 1)
                    for o in range(2):
                        nc.scalar.mul(proj[:, 2 * g + o, :], misc[g][:, o * TOK:(o + 1) * TOK],
                                      VT[:, V_PSC + 2 * g + o:V_PSC + 2 * g + o + 1]).then_inc(pm_ok, 1)

            def exponent(b):
                act.wait_ge(cen_ok, NT - b)
                nc.scalar.activation(L[b][:], L[b][:], ACT.Exp).then_inc(exp_ok, 1)

            def values(i):
                for kb in range(NT):
                    act.wait_ge(v_ps, 2 * i + kb + 1)
                    nc.scalar.copy(vnat[:, kb, 512 * i:512 * i + 512], misc[2 + kb][:]).then_inc(v_ok, 1)

            def turned(b, before):
                for r in range(2 * (b + 1)):
                    act.wait_ge(pT_ps, before + r + 1)
                    nc.scalar.copy(pT[b][:, 4 * r:4 * r + 4, :], misc[r][:].rearrange("p (i q) -> p i q", i=4)
                                   ).then_inc(pT_ok, 1)

            def values_and_exponent():
                values(0)
                exponent(0)

            middles = {2: index_relu(0), 9: values_and_exponent}
            after = {0: small_weights, 1: tail, 2: index_relu(4), 3: index_relu(8), 6: pool_scaled,
                     8: lambda: exponent(1), 9: lambda: turned(1, 0)}
            for i in range(10):
                G = G_PROJ + i
                ahead(G, landed(G), landed(G + 1), middle=middles.get(i))
                if i in after:
                    after[i]()
            turned(0, 4)
            act.wait_ge(bank_done[3], G_MIX)
            for p in range(2):
                act.wait_ge(pm_ok, 4 * p + 4)
                nc.scalar.copy(A_hi[:, 4 * p:4 * p + 4, :], proj[:, 4 * p:4 * p + 4, :]).then_inc(pm_hi, 1)
            values(1)
            for n, (b, i) in enumerate(((1, 0), (0, 0), (1, 1), (0, 1))):
                act.wait_ge(att_ps, n + 1)
                nc.scalar.copy(A_hi[:, 8 + 4 * i:12 + 4 * i, b * P:(b + 1) * P],
                               misc[n][:].rearrange("p (i q) -> p i q", i=4)).then_inc(att_hi, 1)

            with act.Fori(G_MIX, G_QRY) as G:
                ahead(G, landed(G), landed(G + 1))
            act.wait_ge(n_mean["ln1"], 1)
            nc.scalar.copy(mean_sb[:], misc[0][:, 0:TOK]).then_inc(n_meansb["ln1"], 1)
            act.dma_start(subk[:], a["peer_subkeys"][0].rearrange("i k d -> k i d")).then_inc(subk_in, 16)
            squares("ln1", X)
            take_root("ln1")
            for p in range(4):
                act.wait_ge(n_out["ln1"], 4 * (p + 1))
                nc.scalar.copy(A_hi[:, 4 * p:4 * p + 4, :], X[:, 4 * p:4 * p + 4, :]).then_inc(n_hi["ln1"], 1)

            def subkeys():
                act.wait_ge(subT_ps, 1)
                nc.scalar.copy(subT[:], misc[0][:, 0:2 * P].rearrange("p (i k) -> p i k", i=2)).then_inc(subT_ok, 1)

            def scores(g):
                def work():
                    for t in range(NT):
                        act.wait_ge(key_ps, 2 * g + t + 1)
                        nc.scalar.copy(s_sc[t][:, 4 * g:4 * g + 4, :],
                                       misc[2 * (g % 2) + t][:].rearrange("p (i k) -> p i k", i=4)).then_inc(key_ok, 1)
                return work

            for g in range(4):
                G = G_QRY + g
                ahead(G, landed(G), landed(G + 1), last=g == 3, middle=scores(g - 1) if g else subkeys)
            scores(3)()

            for t in range(NT):
                act.wait_ge(gcen_ok, t + 1)
                nc.scalar.activation(gate[:, t, :], gate[:, t, :], ACT.Exp).then_inc(gexp_ok, 1)
            for t in range(NT):
                act.wait_ge(dots_ok, SLOTS // RING * (t + 1))
                nc.scalar.activation(gelu[:, t, :], dots[:, t, :], ACT.Gelu).then_inc(gelu_ok, 1)
            for t in range(NT):
                act.wait_ge(var_ok, t + 1)
                nc.scalar.activation(fstat[:, t, 3:4], fstat[:, t, 2:3], ACT.Sqrt).then_inc(rt_ok, 1)

        @block.vector
        def _(dve):
            step = Steps(dve, dve_step)
            V = nc.vector

            def over_tiles(tile, n):
                return tile.unsqueeze(1).broadcast_to([P, n, tile.shape[1]])

            def reciprocal_root(n, ps, eps, done):
                dve.wait_ge(done, 1)
                V.tensor_scalar(rstd[:], ps[:, 0:TOK], eps, None, ALU.add).then_inc(n_eps[n], 1)
                dve.wait_ge(n_root[n], 1)
                V.reciprocal(rstd[:], root[:]).then_inc(n_rstd[n], 1)
                dve.wait_ge(n_rstd[n], 1)

            def low_part(n, p, src, hi, lo):
                dve.wait_ge(n_hi[n], p + 1)
                V.tensor_tensor(lo[:, 4 * p:4 * p + 4, :], src[:, 4 * p:4 * p + 4, :],
                                hi[:, 4 * p:4 * p + 4, :].bitcast(F32), ALU.subtract).then_inc(n_op[n], 2)

            def centre(n, src):
                dve.wait_ge(n_meansb[n], 1)
                for p in range(4):
                    V.tensor_tensor(src[:, 4 * p:4 * p + 4, :], src[:, 4 * p:4 * p + 4, :],
                                    over_tiles(mean_sb[:], 4), ALU.subtract).then_inc(n_cent[n], 1)

            def rms_tiles(n, g, gain, base):
                for m in range(4):
                    k = 4 * g + m
                    V.tensor_scalar(T[:, k, :], X[:, k, :], VT[:, gain + k:gain + k + 1], None, ALU.mult
                                    ).then_inc(n_out[n], 1)
                for m in range(4):
                    k = 4 * g + m
                    dve.wait_ge(n_hi[n], k + 1)
                    V.tensor_tensor(A_lo[:, k, :], T[:, k, :], A_hi[:, k, :].bitcast(F32), ALU.subtract
                                    ).then_inc(n_op[n], 1)
                    dve.wait_ge(n_sq[n], k + 1)
                    if k == 0:
                        V.tensor_copy(tile_sum[:], xsq[:, m, :]).then_inc(ssq_ok, 1)
                    else:
                        dve.wait_ge(ssq_ok, base + k)
                        V.tensor_tensor(tile_sum[:], tile_sum[:], xsq[:, m, :], ALU.add).then_inc(ssq_ok, 1)

            dve.sem_inc(rsq_ok, 4)
            dve.sem_inc(row_used, RING)
            V.memset(dwn[:], 0.0).then_inc(pads_ok, 1)
            step(V.memset(upad[:, :, 0:PAD], 0.0), hold=False)

            dve.wait_ge(xsq_ok, 4 * NT)
            step(V.tensor_reduce(xstat[:, :, 4], xstat[:, :, 0:4], AX, ALU.add))
            V.tensor_scalar(xstat[:, :, 5], xstat[:, :, 4], 1.0 / D, RMS_EPS, ALU.mult, ALU.add).then_inc(xeps_ok, 1)
            dve.wait_ge(xroot_ok, 1)
            step(V.reciprocal(xstat[:, :, 7], xstat[:, :, 6]))
            for t in range(NT):
                V.tensor_scalar(xsc[:, t, :], xnat[:, t, :], xstat[:, t, 7:8], None, ALU.mult).then_inc(xsc_ok, 1)
            dve.wait_ge(vt_ok, 2)

            def low_pair(r):
                dve.wait_ge(n_hi["rms1"], r + 1)
                V.tensor_tensor(A_lo[:, 2 * r:2 * r + 2, :], T[:, 2 * r:2 * r + 2, :],
                                A_hi[:, 2 * r:2 * r + 2, :].bitcast(F32), ALU.subtract).then_inc(n_op["rms1"], 1)

            for r in range(8):
                dve.wait_ge(x_ps, r + 1)
                for i in range(2):
                    k = 2 * r + i
                    V.tensor_scalar(T[:, k, :], misc[r % 4][:, i * TOK:(i + 1) * TOK], VT[:, V_N1 + k:V_N1 + k + 1],
                                    None, ALU.mult).then_inc(n_out["rms1"], 1)
                if r:
                    low_pair(r - 1)
            low_pair(7)
            dve.wait_ge(rb_in, 16)
            V.tensor_copy(rbB[:], rb[:].unsqueeze(2).broadcast_to([BUCKETS, HEADS, P])).then_inc(rbB_ok, 1)

            with dve.Fori(0, 8) as g:
                for i in range(2):
                    dve.wait_ge(bank_done[2 + i], g + 1)
                    dve.wait_ge(bank_free[i], g + 2)
                    V.scalar_tensor_tensor(upad[:, i, PAD:PAD + TOK], bank[2 + i][:, 0:TOK],
                                           VT[:, bass.ds(V_BV + i + 2 * g, 1)], sig[:, i, :], ALU.add, ALU.mult
                                           ).then_inc(bank_free[2 + i], 1)
                for n in range(2 * TAPS):
                    j, i = divmod(n, 2)
                    z = Z[:, bass.ds(2 * g + i, 1), :].rearrange("p o t -> p (o t)")
                    w = dwT[:, bass.ds(2 * g + i, 1), j:j + 1].rearrange("p o j -> p (o j)")
                    if n < 2:
                        dve.wait_ge(bank_free[2 + i], g + 2)
                        V.tensor_scalar(z, upad[:, i, 0:TOK], w, VT[:, bass.ds(V_DWB + i + 2 * g, 1)],
                                        ALU.mult, ALU.add).then_inc(conv_step, 1)
                    else:
                        dve.wait_ge(conv_step, g * (2 * TAPS) + (n - 1))
                        V.scalar_tensor_tensor(z, upad[:, i, j:j + TOK], w, z, ALU.mult, ALU.add
                                               ).then_inc(conv_step, 1)
                dve.wait_ge(conv_step, g * (2 * TAPS) + 2 * TAPS)

            centre("lnc", Z)
            reciprocal_root("lnc", misc[1], LN_EPS, n_var["lnc"])
            for p in range(4):
                V.tensor_tensor(Z[:, 4 * p:4 * p + 4, :], Z[:, 4 * p:4 * p + 4, :], over_tiles(rstd[:], 4),
                                ALU.mult).then_inc(n_out["lnc"], 1)
            dve.wait_ge(brow_out, 16)
            for p in range(4):
                low_part("lnc", p, T, B_hi, B_lo)
            for g in range(4):
                for m in range(4):
                    k = 4 * g + m
                    dve.wait_ge(bank_done[m], G_OUT + g + 1)
                    V.scalar_tensor_tensor(X[:, k, :], bank[m][:, 0:TOK], VT[:, V_BOUT + k:V_BOUT + k + 1], X[:, k, :],
                                           ALU.add, ALU.add).then_inc(bank_free[m], 1)
                for m in range(4):
                    dve.wait_ge(bank_free[m], G_OUT + g + 2)
                rms_tiles("rms2", g, V_N2, 0)

            def mlp_in(q):
                for g in range(4):
                    G = q * 8 + (G_MLP + g)
                    for m in range(4):
                        dve.wait_ge(bank_free[m], G + 2)
                        V.tensor_tensor(sq[:, m, :], relu[:, m, :], relu[:, m, :], ALU.mult).then_inc(rsq_ok, 1)
                    for m in range(4):
                        dve.wait_ge(rsq_ok, q * 16 + (4 * g + m + 5))
                        dve.wait_ge(hidh_ok, q * 16 + (4 * g + m + 1))
                        V.tensor_tensor(B_lo[:, 4 * g + m, :], sq[:, m, :], B_hi[:, 4 * g + m, :].bitcast(F32),
                                        ALU.subtract).then_inc(hid_ok, 1)
                    dve.wait_ge(hid_ok, q * 16 + (4 * g + 4))

            def mlp_out(q, last=False):
                for g in range(4):
                    G = q * 8 + (G_MLP + 4 + g)
                    for m in range(4):
                        dve.wait_ge(bank_done[m], G + 1)
                        V.tensor_tensor(sq[:, m, :], bank[m][:, 0:TOK], rstd2[:], ALU.mult).then_inc(bank_free[m], 1)
                    for m in range(4):
                        dve.wait_ge(bank_free[m], G + 2)
                        V.tensor_tensor(X[:, 4 * g + m, :], sq[:, m, :], X[:, 4 * g + m, :], ALU.add
                                        ).then_inc(xadd_ok, 1)
                    dve.wait_ge(xadd_ok, q * 16 + (4 * g + 4))
                    if last:
                        rms_tiles("rms3", g, V_FIN, KT)

            mlp_in(0)
            reciprocal_root("rms2", misc[0], RMS_EPS, n_mean["rms2"])
            step(V.tensor_tensor(rstd2[:], rstd[:], rstd[:], ALU.mult))
            mlp_out(0)
            with dve.Fori(1, 3) as q:
                mlp_in(q)
                mlp_out(q)
            mlp_in(3)
            mlp_out(3, last=True)

            def read_out(i):
                G, first = G_PROJ + i, 4 * PROJ_ORDER[i]
                for m in range(4):
                    dve.wait_ge(bank_done[m], G + 1)
                    V.tensor_tensor(proj[:, first + m, :], bank[m][:, 0:TOK], rstd[:], ALU.mult
                                    ).then_inc(bank_free[m], 1)
                for m in range(4):
                    dve.wait_ge(bank_free[m], G + 2)
                dve.sem_inc(proj_ok, 4)

            def accumulate(b, heads, fill, before=0):
                nk = P * (b + 1)
                per = 512 // nk
                for i, h in enumerate(heads):
                    n = fill + i // per
                    dve.wait_ge(idx_rel, n + 1)
                    if before + i:
                        dve.wait_ge(idx_acc, IDX_HEADS * (1 - b) + before + i)
                    V.scalar_tensor_tensor(score[:, 0:nk], misc[n % 4][:, (i % per) * nk:(i % per + 1) * nk],
                                           widx[:, b, h:h + 1], score[:, 0:nk] if before + i else causal(b),
                                           ALU.mult, ALU.add).then_inc(idx_acc, 1)

            def causal(b):
                return cst[:, C_CAUSAL + b * TOK:C_CAUSAL + b * TOK + P * (b + 1)]

            def keep_best(b):
                nk = P * (b + 1)
                dve.wait_ge(idx_acc, IDX_HEADS * (NT - b))
                src = score
                for _ in range(TOPK // 8):
                    step(V.max(top8[:], src[:, 0:nk]))
                    step(V.match_replace(work[:, 0:nk], top8[:], src[:, 0:nk], TAKEN))
                    src = work
                step(V.tensor_scalar(keep[:, b, 0:nk], work[:, 0:nk], TAKEN / 2, NEG, ALU.is_gt, ALU.mult))
                step(V.tensor_tensor(keep[:, b, 0:nk], keep[:, b, 0:nk], causal(b), ALU.add))

            reciprocal_root("rms3", misc[0], RMS_EPS, n_mean["rms3"])
            read_out(0)
            for k in range(KT):
                V.scalar_tensor_tensor(X[:, k, :], X[:, k, :], VT[:, V_FIN + k:V_FIN + k + 1], rstd[:],
                                       ALU.mult, ALU.mult).then_inc(n_out["rms3"], 1)
            step(V.memset(pbuf[:], 0.0))
            read_out(1)
            dve.wait_ge(tail_ok, 2)
            dve.wait_ge(cst2_in, 16)
            accumulate(1, same_rows(0, 8, 2), 0)
            read_out(2)
            accumulate(1, same_rows(8, 8, 2), 4, 8)
            keep_best(1)
            read_out(3)
            accumulate(0, same_rows(0, IDX_HEADS, 4), 8)
            keep_best(0)
            read_out(4)
            for g, w in enumerate(WINDOWS):
                v = proj[:, 2 * g:2 * g + 2, :]
                src, d = 0, 1
                step(V.tensor_copy(pbuf[:, 0, :, 16:16 + TOK], v))
                while d < w:
                    step(V.tensor_tensor(pbuf[:, 1 - src, :, 16:16 + TOK], pbuf[:, src, :, 16:16 + TOK],
                                         pbuf[:, src, :, 16 - d:16 - d + TOK], ALU.add))
                    src, d = 1 - src, 2 * d
                step(V.tensor_tensor(pbuf[:, src, :, 16:16 + TOK], pbuf[:, src, :, 16:16 + TOK],
                                     over_tiles(cst[:, C_CNT + g * TOK:C_CNT + (g + 1) * TOK], 2), ALU.mult))
                V.tensor_tensor(v, pbuf[:, src, :, 16:16 + TOK], v, ALU.subtract).then_inc(pooled_ok, 1)
                dve.wait_ge(pooled_ok, g + 1)
                if g == 1:
                    read_out(5)
            read_out(6)
            read_out(7)

            def softmax_in(b, fills):
                nk, l = P * (b + 1), L[b][:]
                per = 512 // nk
                for h in range(HEADS):
                    dve.wait_ge(lg_ps, fills + h // per + 1)
                    V.scalar_tensor_tensor(L[b][:, h, :], misc[h // per][:, (h % per) * nk:(h % per + 1) * nk],
                                           P ** -0.5, BT[:, h, TOK - nk:TOK], ALU.mult, ALU.add).then_inc(lg_ok, 1)
                dve.wait_ge(lg_ok, HEADS * (NT - b))
                step(V.tensor_tensor(l, l, over_tiles(keep[:, b, 0:nk], HEADS), ALU.add))
                step(V.tensor_reduce(stat[:, 0, :], l, AX, ALU.max))
                V.tensor_tensor(l, l, stat[:, 0, :].unsqueeze(2).broadcast_to([P, HEADS, nk]), ALU.subtract
                                ).then_inc(cen_ok, 1)

            def softmax_out(b):
                nk, l = P * (b + 1), L[b][:]
                dve.wait_ge(exp_ok, NT - b)
                step(V.tensor_reduce(stat[:, 1, :], l, AX, ALU.add))
                step(V.reciprocal(stat[:, 1, :], stat[:, 1, :]))
                V.tensor_tensor(l, l, stat[:, 1, :].unsqueeze(2).broadcast_to([P, HEADS, nk]), ALU.mult
                                ).then_inc(prob_ok, 1)

            dve.wait_ge(BT_in, 16 * HEADS)
            softmax_in(1, 0)
            read_out(8)
            softmax_out(1)
            softmax_in(0, 4)
            softmax_out(0)
            read_out(9)
            for p in range(2):
                dve.wait_ge(pm_hi, p + 1)
                V.tensor_tensor(A_lo[:, 4 * p:4 * p + 4, :], proj[:, 4 * p:4 * p + 4, :],
                                A_hi[:, 4 * p:4 * p + 4, :].bitcast(F32), ALU.subtract).then_inc(mix_op, 2)
            for n, (b, i) in enumerate(((1, 0), (0, 0), (1, 1), (0, 1))):
                dve.wait_ge(att_hi, n + 1)
                hs = slice(8 + 4 * i, 12 + 4 * i)
                V.tensor_tensor(A_lo[:, hs, b * P:(b + 1) * P], misc[n][:].rearrange("p (i q) -> p i q", i=4),
                                A_hi[:, hs, b * P:(b + 1) * P].bitcast(F32), ALU.subtract).then_inc(att_lo, 1)
                if n % 2:
                    dve.wait_ge(att_lo, n + 1)
                    dve.sem_inc(mix_op, 2)

            step(V.memset(mix_sum[:], 0.0))
            with dve.Fori(0, 4) as g:
                for m in range(4):
                    dve.wait_ge(bank_done[m], g + (G_MIX + 1))
                    xk = X[:, bass.ds(4 * g + m, 1), :].rearrange("p o t -> p (o t)")
                    V.scalar_tensor_tensor(xk, xk, ALPHA, bank[m][:, 0:TOK], ALU.mult, ALU.add
                                           ).then_inc(bank_free[m], 1)
                for m in range(4):
                    xk = X[:, bass.ds(4 * g + m, 1), :].rearrange("p o t -> p (o t)")
                    dve.wait_ge(bank_free[m], g + (G_MIX + 2))
                    if m:
                        dve.wait_ge(sum_ok, 4 * g + m)
                    V.tensor_tensor(mix_sum[:], xk, mix_sum[:], ALU.add).then_inc(sum_ok, 1)
                dve.wait_ge(sum_ok, 4 * g + 4)
            centre("ln1", X)
            reciprocal_root("ln1", misc[1], LN_EPS, n_var["ln1"])
            for p in range(4):
                step(V.tensor_tensor(X[:, 4 * p:4 * p + 4, :], X[:, 4 * p:4 * p + 4, :], over_tiles(rstd[:], 4),
                                     ALU.mult))
                for k in range(4 * p, 4 * p + 4):
                    V.tensor_scalar(X[:, k, :], X[:, k, :], VT[:, V_L1G + k:V_L1G + k + 1],
                                    VT[:, V_L1B + k:V_L1B + k + 1], ALU.mult, ALU.add).then_inc(n_out["ln1"], 1)
                if p:
                    low_part("ln1", p - 1, X, A_hi, A_lo)
            low_part("ln1", 3, X, A_hi, A_lo)
            for r in range(8):
                dve.wait_ge(hn_ps, r + 1)
                V.tensor_copy(hnat[:, r // 4, 512 * (r % 4):512 * (r % 4) + 512], misc[r % 4][:]).then_inc(hn_ok, 1)

            def top16(vals, where, src, wk, n):
                for i in range(n):
                    step(V.max(vals(i)[:, 0:8], src(i)), hold=i == n - 1)
                for i in range(n):
                    step(V.max_index(where(i)[:, 0:8], vals(i)[:, 0:8], src(i)), hold=False)
                    step(V.match_replace(wk(i), vals(i)[:, 0:8], src(i), TAKEN), hold=i == n - 1)
                for i in range(n):
                    step(V.max(vals(i)[:, 8:16], wk(i)), hold=i == n - 1)
                for i in range(n):
                    step(V.max_index(where(i)[:, 8:16], vals(i)[:, 8:16], wk(i)), hold=i == n - 1)

            def choose(t, g):
                dve.wait_ge(key_ok, 2 * g + t + 1)
                top16(lambda i: val16[:, i, :], lambda i: pos16[:, i, :], lambda i: s_sc[t][:, 4 * g + i, :],
                      lambda i: s_wk[:, i, :], 4)
                step(V.tensor_copy(posf[:], pos16[:]), hold=False)
                v = val16[:].rearrange("p (h s) i -> p h s i", s=2)
                four = [P, 2, 16, 16]
                step(V.tensor_tensor(cand[:].rearrange("p h (i j) -> p h i j", i=16),
                                     v[:, :, 0, :].unsqueeze(3).broadcast_to(four),
                                     v[:, :, 1, :].unsqueeze(2).broadcast_to(four), ALU.add))
                top16(lambda h: best[:, 16 * h:16 * h + 16], lambda h: bpos[:, 16 * h:16 * h + 16],
                      lambda h: cand[:, h, :], lambda h: cwork[:, h, :], 2)
                step(V.tensor_scalar(bij[:, 0, :], bpos[:], 4, None, ALU.logical_shift_right), hold=False)
                step(V.tensor_scalar(bij[:, 1, :], bpos[:], 15, None, ALU.bitwise_and))
                step(V.tensor_copy(bijf[:], bij[:]))
                step(V.tensor_tensor(onehot[:], bijf[:].unsqueeze(3).broadcast_to([P, 2, 32, 16]),
                                     cst[:, C_IOTA:C_IOTA + 16].unsqueeze(1).unsqueeze(1).broadcast_to([P, 2, 32, 16]),
                                     ALU.is_equal))
                pf = posf[:].rearrange("p (h s) i -> p h s i", s=2)
                for s in range(2):
                    oh = onehot[:, s].rearrange("p (h k) i -> p h k i", h=2)
                    step(V.tensor_tensor(oh, oh, pf[:, :, s, :].unsqueeze(2).broadcast_to(four), ALU.mult), hold=s)
                step(V.tensor_reduce(eij[:], onehot[:], AX, ALU.add))
                mine = slice(32 * g, 32 * g + 32)
                step(V.scalar_tensor_tensor(eidf[:, t, mine], eij[:, 0, :], float(KEYS), eij[:, 1, :],
                                            ALU.mult, ALU.add))
                V.tensor_copy(eid[:, t, mine], eidf[:, t, mine]).then_inc(eid_ok, 1)
                b3 = best[:].rearrange("p (h k) -> p h k", k=16)
                step(V.tensor_tensor(gate[:, t, mine].rearrange("p (h k) -> p h k", k=16), b3,
                                     b3[:, :, 0:1].broadcast_to([P, 2, 16]), ALU.subtract))

            def gates(t):
                g3 = gate[:, t, :].rearrange("p (h k) -> p h k", k=16)
                dve.wait_ge(gexp_ok, t + 1)
                step(V.tensor_reduce(gsum[:, t, :], g3, AX, ALU.add))
                step(V.reciprocal(gsum[:, t, :], gsum[:, t, :]))
                step(V.tensor_tensor(g3, g3, gsum[:, t, :].unsqueeze(2).broadcast_to([P, PEER_HEADS, 16]), ALU.mult))

            for g in range(4):
                for m in range(4):
                    dve.wait_ge(bank_done[m], G_QRY + g + 1)
                    V.tensor_copy(qh[:, 4 * g + m, :], bank[m][:, 0:TOK]).then_inc(bank_free[m], 1)
                if g:
                    choose(0, g - 1)
            choose(0, 3)
            dve.sem_inc(gcen_ok, 1)

            rounds = SLOTS // RING

            def expert_dots(t, first, n):
                with dve.Fori(first, first + n) as r:
                    N = r + t * rounds
                    for j in range(RING):
                        dve.wait_ge(row_in[j], 16 * N + 16)
                        V.tensor_tensor_reduce(out=rows[:, j, :], in0=rows[:, j, :], in1=hnat[:, t, :], scale=1.0,
                                               scalar=0.0, op0=ALU.mult, op1=ALU.add, accum_out=dring[:, j:j + 1]
                                               ).then_inc(row_used, 1)
                    dve.wait_ge(row_used, N * RING + 2 * RING)
                    V.tensor_scalar(dots[:, t, bass.ds(r * RING, RING)], dring[:], 1.0, None, ALU.mult
                                    ).then_inc(dots_ok, 1)
                    dve.wait_ge(dots_ok, N + 1)

            for g in range(4):
                expert_dots(0, g * rounds // 4, rounds // 4)
                choose(1, g)
            dve.sem_inc(gcen_ok, 1)
            gates(0)
            expert_dots(1, 0, rounds)
            gates(1)
            for t in range(NT):
                step(V.tensor_scalar(mixed[:, t, :], hnat[:, t, :], ALPHA, None, ALU.mult), hold=False)
                dve.wait_ge(gelu_ok, t + 1)
                step(V.tensor_tensor(coef[:, t, :], gelu[:, t, :], gate[:, t, :], ALU.mult))
            dve.wait_ge(gb_in, 32)
            for t in range(NT):
                with dve.Fori(0, rounds) as r:
                    N = r + (NT + t) * rounds
                    for j in range(RING):
                        dve.wait_ge(row_in[j], 16 * N + 16)
                        dve.wait_ge(row_used, N * RING + (RING + j))
                        V.scalar_tensor_tensor(mixed[:, t, :], rows[:, j, :], coef[:, t, bass.ds(r * RING + j, 1)],
                                               mixed[:, t, :], ALU.mult, ALU.add).then_inc(row_used, 1)
                dve.wait_ge(row_used, (NT + t + 1) * rounds * RING + RING)
                f = fstat[:, t, :]
                for c in range(4):
                    step(V.bn_stats(bn[:, t, c, :], mixed[:, t, 512 * c:512 * c + 512]), hold=c == 3)
                step(V.bn_aggr(f[:, 0:2], bn[:, t]))
                V.tensor_scalar(f[:, 2:3], f[:, 1:2], LN_EPS, None, ALU.add).then_inc(var_ok, 1)
                dve.wait_ge(rt_ok, t + 1)
                step(V.reciprocal(f[:, 4:5], f[:, 3:4]))
                for half in range(2):
                    cols = slice(half * D // 2, (half + 1) * D // 2)
                    step(V.tensor_scalar(y[:, t, cols], mixed[:, t, cols], f[:, 0:1], f[:, 4:5],
                                         ALU.subtract, ALU.mult))
                    step(V.tensor_tensor(y[:, t, cols], y[:, t, cols], gb[:, 0, cols], ALU.mult))
                    V.tensor_tensor(y[:, t, cols], y[:, t, cols], gb[:, 1, cols], ALU.add).then_inc(y_ok, 1)


def shape_table():
    import numpy as np

    t = np.zeros((P, C_END), np.float32)
    p, s = np.arange(P)[:, None], np.arange(TOK)[None, :]
    t[:, C_ID:C_ID + P] = np.eye(P)
    t[:, C_ONE:C_ONE + P] = 1.0 / D
    for b in range(NT):
        t[:, C_CAUSAL + b * TOK:C_CAUSAL + (b + 1) * TOK] = np.where(s <= p + b * P, 0.0, NEG)
    for g, w in enumerate(WINDOWS):
        t[:, C_CNT + g * TOK:C_CNT + (g + 1) * TOK] = 1.0 / np.minimum(s + 1, w)
    dist = np.maximum(TOK - 1 - np.arange(384), 0)
    exact = BUCKETS // 2
    far = exact + (np.log(np.maximum(dist, 1) / exact) / np.log(128 / exact) * (BUCKETS - exact)).astype(np.int32)
    bucket = np.where(dist < exact, dist, np.minimum(far, BUCKETS - 1))
    t[0:BUCKETS, C_HOT:C_HOT + 384] = bucket[None, :] == np.arange(BUCKETS)[:, None]
    t[:, C_IOTA:C_IOTA + 16] = np.arange(16)
    return t


_INS = {"x": "x", "norm1_g": "norm1_g", "norm2_g": "norm2_g", "mlp_w1": "mlp_w1", "mlp_w2": "mlp_w2",
        "cc_w_in": "cc_w_in", "cc_b_in": "cc_b_in", "cc_dw": "cc_dw", "cc_dw_b": "cc_dw_b", "cc_ln_g": "cc_ln_g",
        "cc_ln_b": "cc_ln_b", "cc_w_out": "cc_w_out", "cc_b_out": "cc_b_out", "final_g": "final_g",
        "w_in_2": "w_in_2", "pool_w_2": "pool_w", "pool_scale_2": "pool_scale", "rel_bias_2": "rel_bias",
        "w_out_2": "w_out_2", "ln1_g_2": "ln1_g", "ln1_b_2": "ln1_b", "peer_wq_2": "peer_wq",
        "peer_subkeys_2": "peer_subkeys", "peer_u_2": "peer_u", "peer_v_2": "peer_v", "ln2_g_2": "ln2_g",
        "ln2_b_2": "ln2_b"}


def kernel(**inputs):
    import numpy as _np
    import concourse.bacc as _bacc
    from concourse import mybir as _mybir
    from concourse.bass_utils import run_bass_kernel_spmd as _run

    nc = _bacc.Bacc("TRN2", target_bir_lowering=False, num_devices=1)
    arrays, args = {}, {}
    for name, short in _INS.items():
        arr = _np.ascontiguousarray(inputs[name])
        arrays[f"in_{name}"] = arr
        args[short] = nc.dram_tensor(f"in_{name}", arr.shape, _mybir.dt.from_np(arr.dtype), kind="ExternalInput").ap()
    table = shape_table()
    arrays["in_table"] = table
    args["table"] = nc.dram_tensor("in_table", table.shape, F32, kind="ExternalInput").ap()
    out = nc.dram_tensor("out_0", (1, TOK, D), F32, kind="ExternalOutput").ap()
    build(nc, args, out)
    r = _run(nc, [arrays], core_ids=[0])
    return r.results[0]["out_0"]
```

```python
from contextlib import ExitStack

import concourse.bass as bass
from concourse import mybir

F32 = mybir.dt.float32
F32R = mybir.dt.float32r
U32 = mybir.dt.uint32
ACT = mybir.ActivationFunctionType
ALU = mybir.AluOpType
AX = mybir.AxisListType.X

P = 128
TOK = 256
NT = TOK // P
D = 2048
KT = D // P
D_FF = 4 * D
TAPS = 31
PAD = TAPS - 1
LN_EPS, RMS_EPS = 1e-5, 1e-6
ALPHA = 2 ** 0.25
HEADS = 8
IDX_HEADS = 16
IDX_DIM = 64
IDX_SCALE = (IDX_HEADS * IDX_DIM) ** -0.5
TOPK = 64
NEG = -1e30
TAKEN = -3e38
WINDOWS = (2, 4, 8, 16)
BUCKETS = 32
PEER_HEADS = 8
PEER_TOPK = 16
KEYS = 128
SLOTS = PEER_HEADS * PEER_TOPK
RING = 8
DENSE = 1536
PIECE = 512
PIECES = DENSE // PIECE
REST = D - DENSE

G_IN, G_OUT, G_MLP, G_PROJ, G_MIX, G_QRY, G_END = 0, 8, 12, 44, 54, 58, 62
SUBS = 8

C_ID, C_ONE, C_IOTA, C_CAUSAL, C_CNT, C_HOT, C_END = 0, 128, 256, 384, 896, 1920, 2304
V_N1, V_N2, V_FIN, V_BV, V_BG, V_DWB, V_LNG, V_LNB, V_BOUT, V_L1G, V_L1B, V_PSC, V_END = (
    0, 16, 32, 48, 64, 80, 96, 112, 128, 144, 160, 176, 184)

PROJ_ORDER = (8, 9, 0, 1, 4, 5, 2, 3, 6, 7)


def build(nc, a, out):
    with ExitStack() as ctx:
        def sem(name):
            return ctx.enter_context(nc.semaphore(name))

        def at(name, offset, shape, dtype=F32):
            return nc.alloc_sbuf_tensor_at(name, [shape[0], *shape[1:]], dtype, offset=offset)

        KB = 1024
        base = (nc.sbuf_base + 63) // 64 * 64
        o_x, o_t, o_ah, o_al = base, base + 16 * KB, base + 32 * KB, base + 48 * KB
        o_raw, o_hi, o_lo = base + 64 * KB, base + 96 * KB, base + 112 * KB
        o_z = base + 128 * KB
        o_c = o_z + 64 * KB

        X = at("X", o_x, [P, KT, TOK])
        T = at("T", o_t, [P, KT, TOK])
        A_hi = at("A_hi", o_ah, [P, KT, TOK], F32R)
        A_lo = at("A_lo", o_al, [P, KT, TOK], F32R)
        raw = at("raw", o_raw, [P, 4, 4, 512])
        w_hi = at("w_hi", o_hi, [P, 4, 2, 512], F32R)
        w_lo = at("w_lo", o_lo, [P, 4, 2, 512], F32R)

        cst = at("cst", o_c, [P, C_END])
        o = o_c + C_END * 4
        VT = at("VT", o, [P, V_END]); o += V_END * 4
        dwT = at("dwT", o, [P, KT, 32]); o += KT * 32 * 4
        mean_sb = at("mean_sb", o, [P, TOK]); o += TOK * 4
        root = at("root", o, [P, TOK]); o += TOK * 4
        rstd = at("rstd", o, [P, TOK]); o += TOK * 4
        rb = at("rb", o, [BUCKETS, HEADS]); o += 64
        assert o <= nc.sbuf_usable_end, (o, nc.sbuf_usable_end)
        ident = cst[:, C_ID:C_ID + P]
        ones = cst[:, C_ONE:C_ONE + P]

        xnat = at("xnat", o_z + 16 * KB, [P, NT, D])
        xsc = at("xsc", o_z + 32 * KB, [P, NT, D])
        dwn = at("dwn", o_x, [32, D])
        vrow = at("vrow", o_x + 8 * KB, [P, 2, P])
        rbB = at("rbB", o_z + 44 * KB, [BUCKETS, HEADS, P])
        xstat = at("xstat", o_x + 13 * KB, [P, NT, 8])
        brow = at("brow", o_z + 32 * KB, [P, HEADS, 384])
        Z = at("Z", o_z, [P, KT, TOK])
        B_hi = at("B_hi", o_z + 16 * KB, [P, KT, TOK], F32R)
        B_lo = at("B_lo", o_z + 32 * KB, [P, KT, TOK], F32R)
        upad = at("upad", o_z + 48 * KB, [P, 2, PAD + TOK])
        sig = at("sig", o_z + 51 * KB, [P, 2, TOK])
        relu = at("relu", o_z + 48 * KB, [P, 4, TOK])
        sq = at("sq", o_z + 52 * KB, [P, 4, TOK])
        tile_sum = at("tile_sum", o_z + 56 * KB, [P, TOK])
        rstd2 = at("rstd2", o_z + 57 * KB, [P, TOK])
        xsq = at("xsq", o_z + 58 * KB, [P, 4, TOK])
        proj = at("proj", o_z, [P, 40, TOK])
        wt = at("wt", o_z + 48 * KB, [P, KT, 144])
        BT = at("BT", o_z + 40 * KB, [P, HEADS, TOK])
        kidx = at("kidx", o_z + 58 * KB, [P, TOK])
        widx = at("widx", o_z + 59 * KB, [P, NT, IDX_HEADS])
        score = at("score", o_z + 59 * KB + 256, [P, TOK])
        work = at("work", o_z + 60 * KB + 256, [P, TOK])
        keep = at("keep", o_z + 61 * KB + 256, [P, NT, TOK])
        top8 = at("top8", o_z + 63 * KB + 256, [P, 8])
        stat = at("stat", o_z + 63 * KB + 512, [P, 2, HEADS])
        mix_sum = at("mix_sum", o_z + 56 * KB, [P, TOK])
        L = (at("L0", o_z + 32 * KB, [P, HEADS, P]), at("L1", o_z + 48 * KB, [P, HEADS, TOK]))
        pT = (at("pT0", o_z + 36 * KB, [P, HEADS, P]), at("pT1", o_t, [P, 2 * HEADS, P]))
        poolw = at("poolw", o_t, [P, 4, 2, 256])
        pbuf = at("pbuf", o_t + 8 * KB, [P, 2, 2, 16 + TOK])
        vnat = at("vnat", o_t + 8 * KB, [P, NT, HEADS * P])
        qh = at("qh", o_z, [P, KT, TOK])
        hnat = at("hnat", o_z + 16 * KB, [P, NT, D])
        s_sc = (at("s_sc0", o_z + 32 * KB, [P, KT, KEYS]), at("s_sc1", o_z + 40 * KB, [P, KT, KEYS]))
        o = o_z + 48 * KB
        s_wk = at("s_wk", o, [P, 4, KEYS]); o += 2 * KB
        cand = at("cand", o, [P, 2, 256]); o += 2 * KB
        cwork = at("cwork", o, [P, 2, 256]); o += 2 * KB
        onehot = at("onehot", o, [P, 2, 32, PEER_TOPK]); o += 4 * KB
        subk = at("subk", o, [P, 2, P]); o += KB
        subT = at("subT", o, [P, 2, KEYS]); o += KB
        val16 = at("val16", o, [P, 4, 16]); o += 256
        pos16 = at("pos16", o, [P, 4, 16], U32); o += 256
        posf = at("posf", o, [P, 4, 16]); o += 256
        best = at("best", o, [P, 32]); o += 128
        bpos = at("bpos", o, [P, 32], U32); o += 128
        bij = at("bij", o, [P, 2, 32], U32); o += 256
        bijf = at("bijf", o, [P, 2, 32]); o += 256
        assert o <= o_z + 64 * KB
        o = o_c + C_CAUSAL * 4
        eid = at("eid", o, [P, NT, SLOTS], U32); o += KB
        gate = at("gate", o, [P, NT, SLOTS]); o += KB
        dots = at("dots", o, [P, NT, SLOTS]); o += KB
        gelu = at("gelu", o, [P, NT, SLOTS]); o += KB
        coef = at("coef", o, [P, NT, SLOTS]); o += KB
        eijs = at("eijs", o, [P, NT, 2, SLOTS]); o += 2 * KB
        gsum = at("gsum", o, [P, NT, PEER_HEADS]); o += 64
        ering = at("ering", o, [P, 2, RING], U32); o += 64
        vring = at("vring", o, [P, 4, 2], U32); o += 32
        dring = at("dring", o, [P, RING]); o += 32
        bn = at("bn", o, [P, NT, 4, 6]); o += 192
        fstat = at("fstat", o, [P, NT, 8]); o += 64
        assert o <= o_c + C_END * 4
        o = o_c + C_END * 4 + V_END * 4
        keyT = at("keyT", o, [P, NT, 2, P]); o += 2 * KB
        coefT = at("coefT", o, [P, NT, P]); o += KB
        eidf = at("eidf", o, [P, 32]); o += 128
        rows = at("rows", o_raw, [P, RING, D])
        mixed = hnat
        wmat = at("wmat", base, [P, NT, KEYS, P])
        vrows = at("vrows", o_z, [P, RING, REST])
        onej = at("onej", o_z + 32 * KB, [P, 2, 4, KEYS])
        onei = at("onei", o_z + 36 * KB, [P, 2, 4, KEYS])
        v_lo = at("v_lo", o_z + 32 * KB, [P, 4, PIECE], F32R)
        v_raw = at("v_raw", o_z + 40 * KB, [P, 2, PIECES, PIECE])
        v_hi = at("v_hi", o_z + 52 * KB, [P, 4, PIECE], F32R)
        g_hi = at("g_hi", o_z + 60 * KB, [P, 2, NT, P], F32R)
        g_lo = at("g_lo", o_z + 62 * KB, [P, 2, NT, P], F32R)
        gb = at("gb", base, [P, 2, D])
        y = at("y", base + 16 * KB, [P, NT, D])

        def psum(name):
            return ctx.enter_context(nc.psum_tensor(name, [P, 512], F32))

        bank = [psum(f"bank{m}") for m in range(4)]
        misc = [psum(f"misc{m}") for m in range(4)]
        scratch = nc.dram_tensor("bias_rows", [HEADS * P * 384], F32).ap()

        def sems(*names):
            return [sem(n) for n in names]

        raw_in = sems(*[f"raw_in{c}" for c in range(4)])
        hi_done, lo_done = sems("hi_done", "lo_done")
        sub_used = sem("sub_used")
        bank_done = sems(*[f"bank_done{m}" for m in range(4)])
        bank_free = sems(*[f"bank_free{m}" for m in range(4)])
        passed = sem("passed")
        cst_in, cst2_in, vec_in, dw_in, rb_in = sems("cst_in", "cst2_in", "vec_in", "dw_in", "rb_in")
        x_in = sems(*[f"x_in{c}" for c in range(4)])
        xsq_ok, xeps_ok, xroot_ok, xsc_ok, xT_ps = sems("xsq_ok", "xeps_ok", "xroot_ok", "xsc_ok", "xT_ps")
        xadd_ok, ssq_ok, sum_ok, proj_ok = sems("xadd_ok", "ssq_ok", "sum_ok", "proj_ok")
        vt_ps, vt_ok, x_ps, x_ok = sems("vt_ps", "vt_ok", "x_ps", "x_ok")
        rbB_ok, brow_ps, brow_ok, brow_out = sems("rbB_ok", "brow_ps", "brow_ok", "brow_out")
        conv_step, dve_step = sems("conv_step", "dve_step")
        rsq_ok, hidh_ok, hid_ok = sems("rsq_ok", "hidh_ok", "hid_ok")
        NORMS = ("rms1", "lnc", "rms2", "rms3", "ln1")
        n_mean, n_meansb, n_cent, n_sq, n_var, n_eps, n_root, n_out, n_hi, n_op = (
            {n: sem(f"{n}_{what}") for n in NORMS if n[0] == "l" or what in ("out", "hi", "op")
             or n != "rms1" and what in ("mean", "sq", "eps", "root")}
            for what in ("mean", "meansb", "cent", "sq", "var", "eps", "root", "out", "hi", "op"))
        silu_ok, pads_ok = sems("silu_ok", "pads_ok")
        wt_in, wt2_ok, poolw_in, BT_in, tail_ps, tail_ok = sems("wt_in", "wt2_ok", "poolw_in", "BT_in", "tail_ps", "tail_ok")
        pooled_ok, pool_ps, pm_ok, pm_hi, mix_op = sems("pooled_ok", "pool_ps", "pm_ok", "pm_hi", "mix_op")
        idx_ps, idx_rel, idx_acc = sems("idx_ps", "idx_rel", "idx_acc")
        v_ps, v_ok, lg_ps, lg_ok, cen_ok, exp_ok, prob_ok = sems(
            "v_ps", "v_ok", "lg_ps", "lg_ok", "cen_ok", "exp_ok", "prob_ok")
        pT_ps, pT_ok, att_ps, att_hi, att_lo = sems("pT_ps", "pT_ok", "att_ps", "att_hi", "att_lo")
        subk_in, subT_ps, subT_ok, hn_ps, hn_ok = sems("subk_in", "subT_ps", "subT_ok", "hn_ps", "hn_ok")
        key_ps, key_ok, gcen_ok, gexp_ok, eid_ok = sems(
            "key_ps", "key_ok", "gcen_ok", "gexp_ok", "eid_ok")
        row_in = sems(*[f"row_in{j}" for j in range(RING)])
        row_used, ering_ok, dots_ok, gelu_ok, coef_ok = sems("row_used", "ering_ok", "dots_ok", "gelu_ok", "coef_ok")
        keyT_ps, keyT_ok, coefT_ps, coefT_ok, oh_ok, quad_ps, mat_ok = sems(
            "keyT_ps", "keyT_ok", "coefT_ps", "coefT_ok", "oh_ok", "quad_ps", "mat_ok")
        v_in = sems("v_in0", "v_in1")
        vhi_ok, vlo_pool, vlo_dve, ghi_ok, glo_ok, piece_used, vring_ok = sems(
            "vhi_ok", "vlo_pool", "vlo_dve", "ghi_ok", "glo_ok", "piece_used", "vring_ok")
        gb_in, var_ok, rt_ok, y_ok, y_out = sems("gb_in", "var_ok", "rt_ok", "y_ok", "y_out")

        class Steps:

            def __init__(self, engine, semaphore):
                self.engine, self.semaphore, self.count = engine, semaphore, 0

            def __call__(self, instruction, hold=True):
                instruction.then_inc(self.semaphore, 1)
                self.count += 1
                if hold:
                    self.engine.wait_ge(self.semaphore, self.count)

        w_conv = a["cc_w_in"][0].rearrange("(k p) (h g n) -> g p k h n", p=P, h=2, n=256)
        w_co = a["cc_w_out"][0].rearrange("(k p) (g n) -> g p k n", p=P, n=512)
        w_1 = a["mlp_w1"][0].rearrange("(k p) (q g n) -> q g p k n", p=P, q=4, n=512)
        w_2 = a["mlp_w2"][0].rearrange("(q k p) (g n) -> q g p k n", p=P, q=4, n=512)
        w_pr = a["w_in_2"][0][:, 0:5120].rearrange("(k p) (g n) -> g p k n", p=P, n=512)
        w_mx = a["w_out_2"][0].rearrange("(k p) (g n) -> g p k n", p=P, n=512)
        w_v = a["peer_v"][0][:, 0:DENSE].rearrange("(i p) (c n) -> i p c n", p=P, n=PIECE)
        w_qr = a["peer_wq"][0].rearrange("(k p) (g n) -> g p k n", p=P, n=512)

        def same_rows(first, n, per):
            for start in range(first, first + n, 2 * per):
                for odd in range(2):
                    yield from range(start + odd, start + 2 * per, 2)

        block = ctx.enter_context(nc.Block())

        @block.sync
        def _(sp):
            def conv_chunk(c, g):
                for half in range(2):
                    sp.dma_start(raw[:, c, :, 256 * half:256 * half + 256],
                                 w_conv[bass.ds(g, 1), :, 4 * c:4 * c + 4, half, :]
                                 .rearrange("o p k n -> (o p) k n")).then_inc(raw_in[c], 16)

            def chunk(c, view, g, G):
                sp.wait_ge(lo_done, G * SUBS + (2 * c + 2 - SUBS))
                sp.dma_start(raw[:, c, :, :], view[bass.ds(g, 1), :, 4 * c:4 * c + 4, :]
                             .rearrange("o p k n -> (o p) k n")).then_inc(raw_in[c], 16)

            sp.dma_start(cst[:, 0:C_CAUSAL], a["table"][:, 0:C_CAUSAL]).then_inc(cst_in, 16)
            for c in range(4):
                cols = slice(c * D // 4, (c + 1) * D // 4)
                sp.dma_start(xnat[:, :, cols], a["x"][0].rearrange("(t p) d -> p t d", p=P)[:, :, cols]
                             ).then_inc(x_in[c], 16)
            for c in range(4):
                conv_chunk(c, 0)
            sp.dma_start(cst[:, C_CAUSAL:C_END], a["table"][:, C_CAUSAL:C_END]).then_inc(cst2_in, 16)
            with sp.Fori(1, G_OUT) as g:
                for c in range(4):
                    sp.wait_ge(lo_done, g * SUBS + (2 * c + 2 - SUBS))
                    conv_chunk(c, g)
            with sp.Fori(0, 4) as g:
                for c in range(4):
                    chunk(c, w_co, g, g + G_OUT)
            with sp.Fori(0, 4) as q:
                for part, view in enumerate((w_1, w_2)):
                    with sp.Fori(0, 4) as g:
                        for c in range(4):
                            chunk(c, view[bass.ds(q, 1)].rearrange("o g p k n -> (o g) p k n"), g,
                                  q * 8 + g + (G_MLP + 4 * part))
            for i, g in enumerate(PROJ_ORDER):
                for c in range(4):
                    chunk(c, w_pr, g, G_PROJ + i)
            for view, G0, n in ((w_mx, G_MIX, 4), (w_qr, G_QRY, 4)):
                with sp.Fori(0, n) as g:
                    for c in range(4):
                        chunk(c, view, g, g + G0)
            def value_rows(i, slot):
                sp.dma_start(v_raw[:, slot], w_v[bass.ds(i, 1)].rearrange("o p c n -> (o p) c n")
                             ).then_inc(v_in[slot], 16)

            sp.wait_ge(gcen_ok, NT)
            for i in range(2):
                value_rows(i, i)
            with sp.Fori(1, KEYS // 2) as r:
                for slot in range(2):
                    i = 2 * r + slot
                    sp.wait_ge(vlo_pool, 2 * r + (slot - 1))
                    sp.wait_ge(vlo_dve, 4 * r + 2 * (slot - 1))
                    value_rows(i, slot)
            sp.wait_ge(glo_ok, KEYS)
            for i, name in enumerate(("ln2_g", "ln2_b")):
                sp.dma_start(gb[:, i, :], a[name].broadcast_to([P, D])).then_inc(gb_in, 16)
            for t in range(NT):
                for half in range(2):
                    cols = slice(half * D // 2, (half + 1) * D // 2)
                    sp.wait_ge(y_ok, 2 * t + half + 1)
                    sp.dma_start(out[0, t * P:(t + 1) * P, cols], y[:, t, cols]).then_inc(y_out, 16)
            sp.wait_ge(y_out, 2 * 16 * NT)

        @block.gpsimd
        def _(pool):
            with pool.Fori(0, G_END) as G:
                for s in range(SUBS):
                    pool.wait_ge(hi_done, G * SUBS + (s + 1))
                    nc.gpsimd.tensor_tensor(w_lo[:, s % 4], raw[:, s // 2, 2 * (s % 2):2 * (s % 2) + 2, :],
                                            w_hi[:, s % 4].bitcast(F32), ALU.subtract).then_inc(lo_done, 1)

            def gather(table, t, first, n):
                with pool.Fori(0, n // (2 * RING)) as r:
                    for half in range(2):
                        nc.gpsimd.tensor_copy(ering[:, half, :],
                                              eid[:, t, bass.ds((2 * r + half) * RING + first % SLOTS, RING)]
                                              ).then_inc(ering_ok, 1)
                        pool.wait_ge(ering_ok, 2 * r + (half + 1 + first // RING))
                        for j in range(RING):
                            pool.wait_ge(row_used, (2 * r + half) * RING + (first + j + 1))
                            pool.sem_inc(passed, 1)
                            pool.indirect_dma_start(rows[:, j, :], None, table,
                                                    bass.IndirectOffsetOnAxis(ering[:, half, j:j + 1], 0)
                                                    ).then_inc(row_in[j], 16)

            pool.wait_ge(bank_done[3], G_END)
            for t in range(NT):
                for g in range(4):
                    pool.wait_ge(eid_ok, 4 * t + g + 1)
                    gather(a["peer_u"][0], t, t * SLOTS + g * SLOTS // 4, SLOTS // 4)

            def value_gathers(Q, u, t):
                N = Q + NT * SLOTS // RING
                for j in (2 * u, 2 * u + 1):
                    pool.wait_ge(row_used, N * RING + (j + 1))
                    pool.sem_inc(passed, 1)
                nc.gpsimd.tensor_copy(vring[:, u, :],
                                      eid[:, t, bass.ds((Q - t * (SLOTS // RING)) * RING + 2 * u, 2)]
                                      ).then_inc(vring_ok, 1)
                pool.wait_ge(vring_ok, 4 * Q + (u + 1))
                pool.sem_inc(passed, 1)
                for j in (2 * u, 2 * u + 1):
                    pool.indirect_dma_start(vrows[:, j, :], None, a["peer_v"][0],
                                            bass.IndirectOffsetOnAxis(vring[:, u, j % 2:j % 2 + 1], 0),
                                            element_offset=DENSE).then_inc(row_in[j], 16)

            def low_piece(R, u):
                n = 12 * R + 3 * u
                pool.wait_ge(vhi_ok, n + 1)
                pool.wait_ge(piece_used, n + 1)
                nc.gpsimd.tensor_tensor(v_lo[:, (3 * u) % 4], v_raw[:, u % 2, 0], v_hi[:, (3 * u) % 4].bitcast(F32),
                                        ALU.subtract).then_inc(vlo_pool, 1)

            for u in range(4):
                value_gathers(0, u, 0)

            pool.wait_ge(mat_ok, 2 + 2 * SLOTS // 4)

            def row_keys(R, now, following):
                for u in range(4):
                    low_piece(R, u)
                    if u == 0 and now is not None:
                        value_gathers(R, 3, now)
                    if u and following is not None:
                        value_gathers(R + 1, u - 1, following)

            half = SLOTS // RING
            row_keys(0, None, 0)
            with pool.Fori(1, half - 1) as R:
                row_keys(R, 0, 0)
            row_keys(half - 1, 0, 1)
            with pool.Fori(half, 2 * half - 1) as R:
                row_keys(R, 1, 1)
            row_keys(2 * half - 1, 1, None)

        @block.tensor
        def _(pe):
            def group(hi, lo, G, ready, base, step, order, hooks):
                for s in range(SUBS):
                    if s in hooks:
                        hooks[s]()
                    pe.wait_ge(ready, base + step * (s + 1))
                    pe.wait_ge(lo_done, G * SUBS + (s + 1))
                    for m in range(4):
                        if s == 0:
                            pe.wait_ge(bank_free[m], G + 1)
                        for k in range(2):
                            wh = w_hi[:, s % 4, k, order[m] * P:(order[m] + 1) * P]
                            wl = w_lo[:, s % 4, k, order[m] * P:(order[m] + 1) * P]
                            dst, kt = bank[m][:, 0:TOK], 2 * s + k
                            nc.tensor.matmul(dst, wh, hi[:, kt, :], start=(kt == 0), stop=False)
                            nc.tensor.matmul(dst, wh, lo[:, kt, :], start=False, stop=False)
                            last = nc.tensor.matmul(dst, wl, hi[:, kt, :], start=False, stop=(kt == KT - 1))
                        if s == SUBS - 1:
                            last.then_inc(bank_done[m], 1)
                    if s < SUBS - 1:
                        last.then_inc(sub_used, 1)

            def groups(hi, lo, G0, n, ready, base=0, step=1, order=(0, 1, 2, 3), hooks={}):
                if n == 1:
                    return group(hi, lo, G0, ready, base, step, order, hooks)
                with pe.Fori(0, n) as g:
                    group(hi, lo, g + G0, ready, base, step, order, hooks)

            def column_means(dst, src, ready, done):
                for k in range(KT):
                    ready(k)
                    last = nc.tensor.matmul(dst[:, 0:TOK], ones, src[:, k, :], start=(k == 0), stop=(k == KT - 1))
                last.then_inc(done, 1)

            def mean_of_sum(ready, value, done):
                pe.wait_ge(ready, value)
                nc.tensor.matmul(misc[0][:, 0:TOK], ones, tile_sum[:], start=True, stop=True).then_inc(done, 1)

            for m in range(4):
                pe.sem_inc(bank_free[m], 1)
            pe.wait_ge(cst_in, 16)
            pe.wait_ge(vec_in, 16 * 11)
            nc.tensor.transpose(bank[0][:, 0:P], vrow[:, 0, :], ident)
            nc.tensor.transpose(bank[0][:, P:V_END], vrow[0:V_END - P, 1, :], ident[0:V_END - P, 0:V_END - P]
                                ).then_inc(vt_ps, 1)
            pe.wait_ge(dw_in, 16)
            pe.wait_ge(pads_ok, 1)
            for k in range(KT):
                last = nc.tensor.transpose(bank[1][:, 32 * k:32 * k + 32], dwn[:, k * P:(k + 1) * P], ident[0:32, 0:32])
            last.then_inc(vt_ps, 1)

            def to_channels(src, done, free, per):
                for r in range(KT // 2):
                    if r >= 4:
                        pe.wait_ge(free, per * (r - 3))
                    for i in range(4):
                        k, t = 2 * r + i // 2, i % 2
                        last = nc.tensor.transpose(misc[r % 4][:, i * P:(i + 1) * P], src[:, t, k * P:(k + 1) * P], ident)
                    last.then_inc(done, 1)

            pe.wait_ge(xsc_ok, 2)
            to_channels(xsc, x_ps, n_out["rms1"], 2)
            pe.wait_ge(vt_ok, 2)
            swap = (2, 3, 0, 1)
            groups(A_hi, A_lo, G_IN, 1, n_op["rms1"], order=swap)
            pe.wait_ge(n_out["rms1"], KT)
            to_channels(xnat, xT_ps, x_ok, 1)
            pe.wait_ge(x_ok, 8)
            pe.wait_ge(cst2_in, 16)
            pe.wait_ge(rbB_ok, 1)
            for h in range(HEADS):
                if h >= 4:
                    pe.wait_ge(brow_ok, h - 3)
                nc.tensor.matmul(misc[h % 4][:, 0:384], rbB[:, h, :], cst[0:BUCKETS, C_HOT:C_HOT + 384],
                                 start=True, stop=True).then_inc(brow_ps, 1)
            groups(A_hi, A_lo, G_IN + 1, 7, n_op["rms1"], order=swap)

            pe.wait_ge(brow_ok, HEADS)
            column_means(misc[0], Z, lambda k: pe.wait_ge(conv_step, 2 * TAPS * (k // 2 + 1)), n_mean["lnc"])
            column_means(misc[1], T, lambda k: pe.wait_ge(n_sq["lnc"], k // 4 + 1), n_var["lnc"])
            groups(B_hi, B_lo, G_OUT, 4, n_op["lnc"])

            groups(A_hi, A_lo, G_MLP, 4, n_op["rms2"], step=2)
            mean_of_sum(ssq_ok, KT, n_mean["rms2"])
            groups(B_hi, B_lo, G_MLP + 4, 4, hid_ok, step=2)
            with pe.Fori(1, 4) as q:
                groups(A_hi, A_lo, q * 8 + G_MLP, 4, n_op["rms2"], step=2)
                groups(B_hi, B_lo, q * 8 + (G_MLP + 4), 4, hid_ok, base=q * KT, step=2)

            def project(i, hooks={}):
                groups(A_hi, A_lo, G_PROJ + i, 1, n_op["rms3"], step=2, hooks=hooks)

            def index_scores(b, heads):
                nk = P * (b + 1)
                per = 512 // nk
                for f in range(len(heads) // per):
                    for i in range(per):
                        h = heads[f * per + i]
                        lo64 = IDX_DIM * (h % 2)
                        last = nc.tensor.matmul(misc[f][:, i * nk:(i + 1) * nk],
                                                proj[lo64:lo64 + IDX_DIM, 32 + h // 2, b * P:(b + 1) * P],
                                                kidx[lo64:lo64 + IDX_DIM, 0:nk], start=True, stop=True)
                    last.then_inc(idx_ps, 1)

            project(0, {5: lambda: mean_of_sum(ssq_ok, 2 * KT, n_mean["rms3"])})
            project(1)
            pe.wait_ge(wt2_ok, 1)
            pe.wait_ge(n_out["rms3"], 2 * KT)
            for k in range(KT):
                nc.tensor.matmul(misc[0][:, 0:TOK], wt[:, k, 0:P], X[:, k, :], start=(k == 0), stop=(k == KT - 1))
            for t in range(NT):
                for k in range(KT):
                    last = nc.tensor.matmul(misc[1][:, t * 16:t * 16 + 16], X[:, k, t * P:(t + 1) * P],
                                            wt[:, k, P:P + 16], start=(k == 0), stop=(k == KT - 1))
            last.then_inc(tail_ps, 1)
            def first_scores():
                pe.wait_ge(tail_ok, 2)
                pe.wait_ge(proj_ok, 8)
                index_scores(1, list(same_rows(0, 8, 2)))
            project(2, {2: first_scores})
            pe.wait_ge(idx_acc, 8)
            index_scores(1, list(same_rows(8, 8, 2)))
            project(3)
            pe.wait_ge(idx_acc, 16)
            index_scores(0, list(same_rows(0, 16, 4)))
            project(4)
            project(5)
            project(6)
            pe.wait_ge(poolw_in, 16)
            pe.wait_ge(idx_acc, 32)
            for g in range(4):
                pe.wait_ge(pooled_ok, g + 1)
                for o in range(2):
                    for c in range(2):
                        last = nc.tensor.matmul(misc[g][:, o * TOK:(o + 1) * TOK], poolw[:, g, c, o * P:(o + 1) * P],
                                                proj[:, 2 * g + c, :], start=(c == 0), stop=(c == 1))
                last.then_inc(pool_ps, 1)
            project(7)

            def logits(b, at_bank):
                nk = P * (b + 1)
                per = 512 // nk
                for f in range(HEADS // per):
                    for i in range(per):
                        h = f * per + i
                        last = nc.tensor.matmul(misc[at_bank + f][:, i * nk:(i + 1) * nk],
                                                proj[:, 8 + h, b * P:(b + 1) * P], proj[:, 16 + h, 0:nk],
                                                start=True, stop=True)
                    last.then_inc(lg_ps, 1)

            def keys_first(i, at_bank):
                for b in range(NT):
                    for h in range(4 * i, 4 * i + 4):
                        last = nc.tensor.transpose(misc[at_bank + b][:, (h % 4) * P:(h % 4 + 1) * P],
                                                   proj[:, 24 + h, b * P:(b + 1) * P], ident)
                    last.then_inc(v_ps, 1)

            def turn_probs(b):
                for r in range(2 * (b + 1)):
                    for i in range(4):
                        h, kb = divmod(4 * r + i, b + 1)
                        last = nc.tensor.transpose(misc[r][:, i * P:(i + 1) * P], L[b][:, h, kb * P:(kb + 1) * P], ident)
                    last.then_inc(pT_ps, 1)

            def first_logits():
                pe.wait_ge(pm_ok, 8)
                pe.wait_ge(proj_ok, 32)
                logits(1, 0)

            def second_logits():
                pe.wait_ge(lg_ok, HEADS)
                pe.wait_ge(proj_ok, 36)
                logits(0, 0)
                keys_first(0, 2)

            def probs_of_block_1():
                pe.wait_ge(v_ok, 2)
                pe.wait_ge(lg_ok, 2 * HEADS)
                pe.wait_ge(prob_ok, 1)
                turn_probs(1)

            project(8, {2: first_logits})
            project(9, {1: second_logits, 6: probs_of_block_1})
            pe.wait_ge(pT_ok, 4)
            pe.wait_ge(prob_ok, 2)
            turn_probs(0)
            pe.wait_ge(proj_ok, 40)
            keys_first(1, 2)
            for n, (b, i) in enumerate(((1, 0), (0, 0), (1, 1), (0, 1))):
                pe.wait_ge(pT_ok, 5 + n % 2 if n < 2 else 6)
                if n >= 2:
                    pe.wait_ge(v_ok, 4)
                for h in range(4 * i, 4 * i + 4):
                    for kb in range(b + 1):
                        last = nc.tensor.matmul(misc[n][:, (h % 4) * P:(h % 4 + 1) * P],
                                                vnat[:, kb, h * P:(h + 1) * P], pT[b][:, h * (b + 1) + kb, :],
                                                start=(kb == 0), stop=(kb == b))
                last.then_inc(att_ps, 1)
            groups(A_hi, A_lo, G_MIX, 4, mix_op)

            pe.wait_ge(sum_ok, KT)
            nc.tensor.matmul(misc[0][:, 0:TOK], ones, mix_sum[:], start=True, stop=True).then_inc(n_mean["ln1"], 1)
            column_means(misc[1], T, lambda k: pe.wait_ge(n_sq["ln1"], k // 4 + 1), n_var["ln1"])

            def keys_turned():
                pe.wait_ge(subk_in, 16)
                pe.wait_ge(n_op["ln1"], 8)
                for i in range(2):
                    last = nc.tensor.transpose(misc[0][:, i * P:(i + 1) * P], subk[:, i, :], ident)
                last.then_inc(subT_ps, 1)
                pe.wait_ge(subT_ok, 1)
                for r in range(8):
                    if r >= 4:
                        pe.wait_ge(hn_ok, r - 3)
                    for i in range(4):
                        t, k = r // 4, 4 * (r % 4) + i
                        last = nc.tensor.transpose(misc[r % 4][:, i * P:(i + 1) * P], X[:, k, t * P:(t + 1) * P], ident)
                    last.then_inc(hn_ps, 1)

            def key_scores(g):
                def work():
                    pe.wait_ge(bank_free[3], G_QRY + g + 2)
                    pe.wait_ge(hn_ok, 8)
                    if g >= 2:
                        pe.wait_ge(key_ok, 2 * (g - 1))
                    for t in range(NT):
                        for i in range(4):
                            last = nc.tensor.matmul(misc[2 * (g % 2) + t][:, i * P:(i + 1) * P],
                                                    qh[:, 4 * g + i, t * P:(t + 1) * P], subT[:, i % 2, :],
                                                    start=True, stop=True)
                        last.then_inc(key_ps, 1)
                return work

            groups(A_hi, A_lo, G_QRY, 1, n_op["ln1"], hooks={6: keys_turned})
            for g in range(1, 4):
                groups(A_hi, A_lo, G_QRY + g, 1, n_op["ln1"], hooks={2: key_scores(g - 1)})
            key_scores(3)()

            pe.sem_inc(quad_ps, 2)
            pe.sem_inc(piece_used, 4)

            def turn_keys(t):
                pe.wait_ge(eid_ok, 4 * t + 4)
                if t:
                    pe.wait_ge(keyT_ok, t)
                for s in range(2):
                    last = nc.tensor.transpose(misc[0][:, s * P:(s + 1) * P], eijs[:, t, s, :], ident)
                last.then_inc(keyT_ps, 1)
                pe.wait_ge(coef_ok, t + 1)
                nc.tensor.transpose(misc[1][:, 0:P], coef[:, t, :], ident).then_inc(coefT_ps, 1)

            def quads(t):
                with pe.Fori(0, SLOTS // RING) as r:
                    for h in range(2):
                        q = 2 * r + (h + 32 * t)
                        pe.wait_ge(oh_ok, 5 * q + 5)
                        pe.wait_ge(mat_ok, q + 1)
                        for i in range(4):
                            last = nc.tensor.matmul(misc[2 + h][:, i * P:(i + 1) * P], onej[:, h, i, :],
                                                    onei[:, h, i, :], start=True, stop=True)
                        last.then_inc(quad_ps, 1)

            for t in range(NT):
                turn_keys(t)
                quads(t)

            acc = ((bank[0], bank[1], misc[0]), (bank[2], bank[3], misc[1]))
            pe.wait_ge(coefT_ok, NT)

            def value_products(R, first=False, final=False):
                for u in range(4):
                    for c in range(PIECES):
                        n = 3 * u + c
                        if c == 0:
                            pe.wait_ge(glo_ok, 4 * R + (u + 1))
                            pe.wait_ge(vlo_pool, 4 * R + (u + 1))
                        else:
                            pe.wait_ge(vlo_dve, 8 * R + (2 * u + c))
                        for t in range(NT):
                            dst = acc[t][c][:, 0:PIECE]
                            gh, gl = g_hi[:, u % 2, t, :], g_lo[:, u % 2, t, :]
                            vh, vl = v_hi[:, n % 4, :], v_lo[:, n % 4, :]
                            nc.tensor.matmul(dst, gh, vh, start=first and u == 0, stop=False)
                            nc.tensor.matmul(dst, gh, vl, start=False, stop=False)
                            last = nc.tensor.matmul(dst, gl, vh, start=False, stop=final and u == 3)
                        last.then_inc(piece_used, 1)

            value_products(0, first=True)
            with pe.Fori(1, KEYS // 4 - 1) as R:
                value_products(R)
            value_products(KEYS // 4 - 1, final=True)

        @block.scalar
        def _(act):
            def round_sub(G, s, raw_count):
                act.wait_ge(raw_in[s // 2], raw_count)
                if s >= 4:
                    act.wait_ge(sub_used, G * 7 + (s - 3))
                elif s == 3:
                    if not (isinstance(G, int) and G == 0):
                        act.wait_ge(bank_done[3], G)
                elif not (isinstance(G, int) and G == 0):
                    act.wait_ge(sub_used, G * 7 + (s - 2))
                nc.scalar.copy(w_hi[:, s % 4], raw[:, s // 2, 2 * (s % 2):2 * (s % 2) + 2, :]).then_inc(hi_done, 1)

            def ahead(G, now, then, last=False, middle=None):
                for s in range(3, SUBS):
                    round_sub(G, s, now)
                if middle:
                    middle()
                if not last:
                    for s in range(3):
                        round_sub(G + 1, s, then)

            def landed(G):
                return (G + 9) * 16

            def squares(n, src):
                for p in range(4):
                    act.wait_ge(n_cent[n], p + 1)
                    nc.scalar.activation(T[:, 4 * p:4 * p + 4, :], src[:, 4 * p:4 * p + 4, :], ACT.Square
                                         ).then_inc(n_sq[n], 1)

            def take_root(n):
                act.wait_ge(n_eps[n], 1)
                nc.scalar.activation(root[:], rstd[:], ACT.Sqrt).then_inc(n_root[n], 1)

            def rms_tiles(n, g, base):
                for m in range(4):
                    k = 4 * g + m
                    act.wait_ge(n_out[n], k + 1)
                    nc.scalar.copy(A_hi[:, k, :], T[:, k, :]).then_inc(n_hi[n], 1)
                    if base + k >= 4:
                        act.wait_ge(ssq_ok, base + k - 3)
                    nc.scalar.activation(xsq[:, m, :], X[:, k, :], ACT.Square).then_inc(n_sq[n], 1)

            VEC = (("norm1_g", V_N1), ("norm2_g", V_N2), ("final_g", V_FIN), ("cc_b_in", V_BV), ("cc_dw_b", V_DWB),
                   ("cc_ln_g", V_LNG), ("cc_ln_b", V_LNB), ("cc_b_out", V_BOUT), ("ln1_g", V_L1G),
                   ("ln1_b", V_L1B), ("pool_scale", V_PSC))
            for name, col in VEC:
                v = a[name].rearrange("(r c) -> r c", c=P) if name == "final_g" else a[name][0].rearrange("(r c) -> r c", c=P)
                act.dma_start(vrow[col % P:col % P + v.shape[0], col // P, :], v).then_inc(
                    vec_in, 16)
            act.dma_start(rb[:], a["rel_bias"]).then_inc(rb_in, 16)
            act.wait_ge(pads_ok, 1)
            act.dma_start(dwn[0:TAPS, :], a["cc_dw"][0]).then_inc(dw_in, 16)

            for c in range(4):
                act.wait_ge(x_in[c], 16)
                for t in range(NT):
                    nc.scalar.activation(T[:, 8 * t + 2 * c:8 * t + 2 * c + 2, :],
                                         xnat[:, t, 512 * c:512 * c + 512].rearrange("p (k n) -> p k n", k=2),
                                         ACT.Square, accum_out=xstat[:, t, c:c + 1]).then_inc(xsq_ok, 1)
            act.wait_ge(xeps_ok, 1)
            nc.scalar.activation(xstat[:, :, 6], xstat[:, :, 5], ACT.Sqrt).then_inc(xroot_ok, 1)
            act.wait_ge(vt_ps, 2)
            nc.scalar.copy(VT[:], bank[0][:, 0:V_END]).then_inc(vt_ok, 1)
            nc.scalar.copy(dwT[:], bank[1][:].rearrange("p (k j) -> p k j", j=32)).then_inc(vt_ok, 1)
            for s in range(3):
                round_sub(0, s, 32)
            for r in range(8):
                act.wait_ge(n_out["rms1"], 2 * r + 2)
                nc.scalar.copy(A_hi[:, 2 * r:2 * r + 2, :], T[:, 2 * r:2 * r + 2, :]).then_inc(n_hi["rms1"], 1)

            def gates(g):
                for i in range(2):
                    act.wait_ge(bank_done[i], g + 1)
                    act.wait_ge(bank_free[2 + i], g + 1)
                    act.sem_inc(passed, 1)
                    nc.scalar.activation(sig[:, i, :], bank[i][:, 0:TOK], ACT.Sigmoid,
                                         bias=VT[:, bass.ds(V_BG + i + 2 * g, 1)]).then_inc(bank_free[i], 1)

            ahead(0, 32, 64)
            gates(0)
            for r in range(8):
                act.wait_ge(xT_ps, r + 1)
                nc.scalar.copy(X[:, 2 * r:2 * r + 2, :], misc[r % 4][:].rearrange("p (k t) -> p k t", k=2)
                               ).then_inc(x_ok, 1)
            for h in range(HEADS):
                act.wait_ge(brow_ps, h + 1)
                nc.scalar.copy(brow[:, h, :], misc[h % 4][:, 0:384]).then_inc(brow_ok, 1)
            act.wait_ge(brow_ok, HEADS)
            act.dma_start(scratch.rearrange("(h p x) -> p h x", p=P, x=384), brow[:]).then_inc(brow_out, 16)
            with act.Fori(1, 7) as g:
                ahead(g, (g + 1) * 32, (g + 2) * 32)
                gates(g)
            ahead(7, 8 * 32, landed(8))
            gates(7)

            act.wait_ge(n_mean["lnc"], 1)
            nc.scalar.copy(mean_sb[:], misc[0][:, 0:TOK]).then_inc(n_meansb["lnc"], 1)
            squares("lnc", Z)
            take_root("lnc")
            for p in range(4):
                act.wait_ge(n_out["lnc"], p + 1)
                for k in range(4 * p, 4 * p + 4):
                    nc.scalar.activation(T[:, k, :], Z[:, k, :], ACT.Silu, bias=VT[:, V_LNB + k:V_LNB + k + 1],
                                         scale=VT[:, V_LNG + k:V_LNG + k + 1]).then_inc(silu_ok, 1)
                act.wait_ge(silu_ok, 4 * (p + 1))
                nc.scalar.copy(B_hi[:, 4 * p:4 * p + 4, :], T[:, 4 * p:4 * p + 4, :]).then_inc(n_hi["lnc"], 1)
            for g in range(4):
                ahead(G_OUT + g, landed(G_OUT + g), landed(G_OUT + g + 1))
                rms_tiles("rms2", g, 0)

            def mlp_in(q):
                for g in range(4):
                    G = q * 8 + (G_MLP + g)
                    ahead(G, landed(G), landed(G + 1))
                    for m in range(4):
                        act.wait_ge(bank_done[m], G + 1)
                        act.wait_ge(rsq_ok, q * 16 + (4 * g + m + 1))
                        nc.scalar.activation(relu[:, m, :], bank[m][:, 0:TOK], ACT.Relu).then_inc(bank_free[m], 1)
                    for m in range(4):
                        act.wait_ge(bank_free[m], G + 2)
                        nc.scalar.activation(B_hi[:, 4 * g + m, :], relu[:, m, :], ACT.Square).then_inc(hidh_ok, 1)
                    act.wait_ge(hidh_ok, q * 16 + (4 * g + 4))

            def mlp_out(q):
                with act.Fori(0, 4) as g:
                    G = q * 8 + g + (G_MLP + 4)
                    ahead(G, landed(G), landed(G + 1))

            mlp_in(0)
            take_root("rms2")
            mlp_out(0)
            with act.Fori(1, 3) as q:
                mlp_in(q)
                mlp_out(q)
            mlp_in(3)
            for g in range(4):
                G = G_MLP + 28 + g
                ahead(G, landed(G), landed(G + 1))
                rms_tiles("rms3", g, KT)

            def small_weights():
                take_root("rms3")
                act.wait_ge(n_op["rms3"], KT)
                act.wait_ge(n_mean["rms3"], 1)
                act.wait_ge(brow_out, 16)
                w2 = a["w_in_2"][0].rearrange("(k p) n -> p k n", p=P)
                for p in range(4):
                    act.dma_start(wt[:, 4 * p:4 * p + 4, 64:144], w2[:, 4 * p:4 * p + 4, 5120:5200]).then_inc(wt_in, 16)

            def mixer_tables():
                act.dma_start(poolw[:], a["pool_w"][0].rearrange("g (c p) n -> p g c n", p=P)).then_inc(poolw_in, 16)
                for h in range(HEADS):
                    first = h * P * 384 + P - 1
                    act.dma_start(BT[:, h, :], scratch[first:first + P * 383].rearrange("(p x) -> p x", x=383)[:, 0:TOK]
                                  ).then_inc(BT_in, 16)

            def keys_twice():
                act.wait_ge(wt_in, 64)
                nc.scalar.copy(wt[:, :, 0:64], wt[:, :, 64:128]).then_inc(wt2_ok, 1)

            def tail():
                act.wait_ge(tail_ps, 1)
                act.wait_ge(n_op["rms3"], KT)
                nc.scalar.copy(kidx[:], misc[0][:, 0:TOK]).then_inc(tail_ok, 1)
                nc.scalar.mul(widx[:], misc[1][:, 0:32].rearrange("p (t h) -> p t h", t=NT), IDX_SCALE
                              ).then_inc(tail_ok, 1)

            def index_relu(first):
                def work():
                    for n in range(first, first + 4):
                        act.wait_ge(idx_ps, n + 1)
                        nc.scalar.activation(misc[n % 4][:], misc[n % 4][:], ACT.Relu).then_inc(idx_rel, 1)
                return work

            def pool_scaled():
                for g in range(4):
                    act.wait_ge(pool_ps, g + 1)
                    for o in range(2):
                        nc.scalar.mul(proj[:, 2 * g + o, :], misc[g][:, o * TOK:(o + 1) * TOK],
                                      VT[:, V_PSC + 2 * g + o:V_PSC + 2 * g + o + 1]).then_inc(pm_ok, 1)

            def exponent(b):
                act.wait_ge(cen_ok, NT - b)
                nc.scalar.activation(L[b][:], L[b][:], ACT.Exp).then_inc(exp_ok, 1)

            def values(i):
                for kb in range(NT):
                    act.wait_ge(v_ps, 2 * i + kb + 1)
                    nc.scalar.copy(vnat[:, kb, 512 * i:512 * i + 512], misc[2 + kb][:]).then_inc(v_ok, 1)

            def turned(b, before):
                for r in range(2 * (b + 1)):
                    act.wait_ge(pT_ps, before + r + 1)
                    nc.scalar.copy(pT[b][:, 4 * r:4 * r + 4, :], misc[r][:].rearrange("p (i q) -> p i q", i=4)
                                   ).then_inc(pT_ok, 1)

            def values_and_exponent():
                values(0)
                exponent(0)

            middles = {1: keys_twice, 2: index_relu(0), 4: mixer_tables, 9: values_and_exponent}
            after = {0: small_weights, 1: tail, 2: index_relu(4), 3: index_relu(8), 6: pool_scaled,
                     8: lambda: exponent(1), 9: lambda: turned(1, 0)}
            for i in range(10):
                G = G_PROJ + i
                ahead(G, landed(G), landed(G + 1), middle=middles.get(i))
                if i in after:
                    after[i]()
            turned(0, 4)
            act.wait_ge(bank_done[3], G_MIX)
            for p in range(2):
                act.wait_ge(pm_ok, 4 * p + 4)
                nc.scalar.copy(A_hi[:, 4 * p:4 * p + 4, :], proj[:, 4 * p:4 * p + 4, :]).then_inc(pm_hi, 1)
            values(1)
            for n, (b, i) in enumerate(((1, 0), (0, 0), (1, 1), (0, 1))):
                act.wait_ge(att_ps, n + 1)
                nc.scalar.copy(A_hi[:, 8 + 4 * i:12 + 4 * i, b * P:(b + 1) * P],
                               misc[n][:].rearrange("p (i q) -> p i q", i=4)).then_inc(att_hi, 1)

            with act.Fori(G_MIX, G_QRY) as G:
                ahead(G, landed(G), landed(G + 1))
            act.wait_ge(n_mean["ln1"], 1)
            nc.scalar.copy(mean_sb[:], misc[0][:, 0:TOK]).then_inc(n_meansb["ln1"], 1)
            act.dma_start(subk[:], a["peer_subkeys"][0].rearrange("i k d -> k i d")).then_inc(subk_in, 16)
            squares("ln1", X)
            take_root("ln1")
            for p in range(4):
                act.wait_ge(n_out["ln1"], 4 * (p + 1))
                nc.scalar.copy(A_hi[:, 4 * p:4 * p + 4, :], X[:, 4 * p:4 * p + 4, :]).then_inc(n_hi["ln1"], 1)

            def subkeys():
                act.wait_ge(subT_ps, 1)
                nc.scalar.copy(subT[:], misc[0][:, 0:2 * P].rearrange("p (i k) -> p i k", i=2)).then_inc(subT_ok, 1)

            def scores(g):
                def work():
                    for t in range(NT):
                        act.wait_ge(key_ps, 2 * g + t + 1)
                        nc.scalar.copy(s_sc[t][:, 4 * g:4 * g + 4, :],
                                       misc[2 * (g % 2) + t][:].rearrange("p (i k) -> p i k", i=4)).then_inc(key_ok, 1)
                return work

            for g in range(4):
                G = G_QRY + g
                ahead(G, landed(G), landed(G + 1), last=g == 3, middle=scores(g - 1) if g else subkeys)
            scores(3)()

            for t in range(NT):
                act.wait_ge(gcen_ok, t + 1)
                nc.scalar.activation(gate[:, t, :], gate[:, t, :], ACT.Exp).then_inc(gexp_ok, 1)
                act.wait_ge(keyT_ps, t + 1)
                nc.scalar.copy(keyT[:, t], misc[0][:, 0:2 * P].rearrange("p (s n) -> p s n", s=2)).then_inc(keyT_ok, 1)
                act.wait_ge(dots_ok, SLOTS // RING * (t + 1))
                nc.scalar.activation(gelu[:, t, :], dots[:, t, :], ACT.Gelu).then_inc(gelu_ok, 1)
                act.wait_ge(coefT_ps, t + 1)
                nc.scalar.copy(coefT[:, t, :], misc[1][:, 0:P]).then_inc(coefT_ok, 1)
                if t == 0:
                    act.sem_inc(mat_ok, 2)
                with act.Fori(0, SLOTS // RING) as r:
                    for h in range(2):
                        q = 2 * r + (h + 32 * t)
                        act.wait_ge(quad_ps, q + 3)
                        act.sem_inc(passed, 1)
                        nc.scalar.copy(wmat[:, t, :, bass.ds(8 * r + 4 * h, 4)].rearrange("p i n -> p n i"),
                                       misc[2 + h][:].rearrange("p (n i) -> p n i", n=4)).then_inc(mat_ok, 1)

            act.wait_ge(mat_ok, 2 + 2 * SLOTS // 4)

            with act.Fori(0, KEYS // 4) as R:
                for u in range(4):
                    act.wait_ge(piece_used, 12 * R + (3 * u + 1))
                    act.sem_inc(passed, 1)
                    nc.scalar.copy(g_hi[:, u % 2], wmat[:, :, bass.ds(4 * R + u, 1), :]
                                   .rearrange("p t o n -> p t (o n)")).then_inc(ghi_ok, 1)
                    for c in range(PIECES):
                        n = 3 * u + c
                        act.wait_ge(v_in[u % 2], 32 * R + 16 * (u // 2 + 1))
                        act.wait_ge(piece_used, 12 * R + (n + 1))
                        nc.scalar.copy(v_hi[:, n % 4], v_raw[:, u % 2, c]).then_inc(vhi_ok, 1)
            for t in range(NT):
                act.wait_ge(var_ok, t + 1)
                nc.scalar.activation(fstat[:, t, 3:4], fstat[:, t, 2:3], ACT.Sqrt).then_inc(rt_ok, 1)

        @block.vector
        def _(dve):
            step = Steps(dve, dve_step)
            V = nc.vector

            def over_tiles(tile, n):
                return tile.unsqueeze(1).broadcast_to([P, n, tile.shape[1]])

            def reciprocal_root(n, ps, eps, done):
                dve.wait_ge(done, 1)
                V.tensor_scalar(rstd[:], ps[:, 0:TOK], eps, None, ALU.add).then_inc(n_eps[n], 1)
                dve.wait_ge(n_root[n], 1)
                step(V.reciprocal(rstd[:], root[:]))

            def low_part(n, p, src, hi, lo):
                dve.wait_ge(n_hi[n], p + 1)
                V.tensor_tensor(lo[:, 4 * p:4 * p + 4, :], src[:, 4 * p:4 * p + 4, :],
                                hi[:, 4 * p:4 * p + 4, :].bitcast(F32), ALU.subtract).then_inc(n_op[n], 2)

            def centre(n, src):
                dve.wait_ge(n_meansb[n], 1)
                for p in range(4):
                    V.tensor_tensor(src[:, 4 * p:4 * p + 4, :], src[:, 4 * p:4 * p + 4, :],
                                    over_tiles(mean_sb[:], 4), ALU.subtract).then_inc(n_cent[n], 1)

            def rms_tiles(n, g, gain, base):
                for m in range(4):
                    k = 4 * g + m
                    V.tensor_scalar(T[:, k, :], X[:, k, :], VT[:, gain + k:gain + k + 1], None, ALU.mult
                                    ).then_inc(n_out[n], 1)
                for m in range(4):
                    k = 4 * g + m
                    dve.wait_ge(n_hi[n], k + 1)
                    V.tensor_tensor(A_lo[:, k, :], T[:, k, :], A_hi[:, k, :].bitcast(F32), ALU.subtract
                                    ).then_inc(n_op[n], 1)
                    dve.wait_ge(n_sq[n], k + 1)
                    if k == 0:
                        V.tensor_copy(tile_sum[:], xsq[:, m, :]).then_inc(ssq_ok, 1)
                    else:
                        dve.wait_ge(ssq_ok, base + k)
                        V.tensor_tensor(tile_sum[:], tile_sum[:], xsq[:, m, :], ALU.add).then_inc(ssq_ok, 1)

            dve.sem_inc(rsq_ok, 4)
            dve.sem_inc(row_used, RING)
            V.memset(dwn[:], 0.0).then_inc(pads_ok, 1)
            step(V.memset(upad[:, :, 0:PAD], 0.0), hold=False)

            dve.wait_ge(xsq_ok, 4 * NT)
            step(V.tensor_reduce(xstat[:, :, 4], xstat[:, :, 0:4], AX, ALU.add))
            V.tensor_scalar(xstat[:, :, 5], xstat[:, :, 4], 1.0 / D, RMS_EPS, ALU.mult, ALU.add).then_inc(xeps_ok, 1)
            dve.wait_ge(xroot_ok, 1)
            step(V.reciprocal(xstat[:, :, 7], xstat[:, :, 6]))
            for t in range(NT):
                V.tensor_scalar(xsc[:, t, :], xnat[:, t, :], xstat[:, t, 7:8], None, ALU.mult).then_inc(xsc_ok, 1)
            dve.wait_ge(vt_ok, 2)

            def low_pair(r):
                dve.wait_ge(n_hi["rms1"], r + 1)
                V.tensor_tensor(A_lo[:, 2 * r:2 * r + 2, :], T[:, 2 * r:2 * r + 2, :],
                                A_hi[:, 2 * r:2 * r + 2, :].bitcast(F32), ALU.subtract).then_inc(n_op["rms1"], 1)

            for r in range(8):
                dve.wait_ge(x_ps, r + 1)
                for i in range(2):
                    k = 2 * r + i
                    V.tensor_scalar(T[:, k, :], misc[r % 4][:, i * TOK:(i + 1) * TOK], VT[:, V_N1 + k:V_N1 + k + 1],
                                    None, ALU.mult).then_inc(n_out["rms1"], 1)
                if r:
                    low_pair(r - 1)
            low_pair(7)
            dve.wait_ge(rb_in, 16)
            V.tensor_copy(rbB[:], rb[:].unsqueeze(2).broadcast_to([BUCKETS, HEADS, P])).then_inc(rbB_ok, 1)

            with dve.Fori(0, 8) as g:
                for i in range(2):
                    dve.wait_ge(bank_done[2 + i], g + 1)
                    dve.wait_ge(bank_free[i], g + 2)
                    V.scalar_tensor_tensor(upad[:, i, PAD:PAD + TOK], bank[2 + i][:, 0:TOK],
                                           VT[:, bass.ds(V_BV + i + 2 * g, 1)], sig[:, i, :], ALU.add, ALU.mult
                                           ).then_inc(bank_free[2 + i], 1)
                for n in range(2 * TAPS):
                    j, i = divmod(n, 2)
                    z = Z[:, bass.ds(2 * g + i, 1), :].rearrange("p o t -> p (o t)")
                    w = dwT[:, bass.ds(2 * g + i, 1), j:j + 1].rearrange("p o j -> p (o j)")
                    if n < 2:
                        dve.wait_ge(bank_free[2 + i], g + 2)
                        V.tensor_scalar(z, upad[:, i, 0:TOK], w, VT[:, bass.ds(V_DWB + i + 2 * g, 1)],
                                        ALU.mult, ALU.add).then_inc(conv_step, 1)
                    else:
                        dve.wait_ge(conv_step, g * (2 * TAPS) + (n - 1))
                        V.scalar_tensor_tensor(z, upad[:, i, j:j + TOK], w, z, ALU.mult, ALU.add
                                               ).then_inc(conv_step, 1)
                dve.wait_ge(conv_step, g * (2 * TAPS) + 2 * TAPS)

            centre("lnc", Z)
            reciprocal_root("lnc", misc[1], LN_EPS, n_var["lnc"])
            for p in range(4):
                V.tensor_tensor(Z[:, 4 * p:4 * p + 4, :], Z[:, 4 * p:4 * p + 4, :], over_tiles(rstd[:], 4),
                                ALU.mult).then_inc(n_out["lnc"], 1)
            dve.wait_ge(brow_out, 16)
            for p in range(4):
                low_part("lnc", p, T, B_hi, B_lo)
            for g in range(4):
                for m in range(4):
                    k = 4 * g + m
                    dve.wait_ge(bank_done[m], G_OUT + g + 1)
                    V.scalar_tensor_tensor(X[:, k, :], bank[m][:, 0:TOK], VT[:, V_BOUT + k:V_BOUT + k + 1], X[:, k, :],
                                           ALU.add, ALU.add).then_inc(bank_free[m], 1)
                for m in range(4):
                    dve.wait_ge(bank_free[m], G_OUT + g + 2)
                rms_tiles("rms2", g, V_N2, 0)

            def mlp_in(q):
                for g in range(4):
                    G = q * 8 + (G_MLP + g)
                    for m in range(4):
                        dve.wait_ge(bank_free[m], G + 2)
                        V.tensor_tensor(sq[:, m, :], relu[:, m, :], relu[:, m, :], ALU.mult).then_inc(rsq_ok, 1)
                    for m in range(4):
                        dve.wait_ge(rsq_ok, q * 16 + (4 * g + m + 5))
                        dve.wait_ge(hidh_ok, q * 16 + (4 * g + m + 1))
                        V.tensor_tensor(B_lo[:, 4 * g + m, :], sq[:, m, :], B_hi[:, 4 * g + m, :].bitcast(F32),
                                        ALU.subtract).then_inc(hid_ok, 1)
                    dve.wait_ge(hid_ok, q * 16 + (4 * g + 4))

            def mlp_out(q, last=False):
                for g in range(4):
                    G = q * 8 + (G_MLP + 4 + g)
                    for m in range(4):
                        dve.wait_ge(bank_done[m], G + 1)
                        V.tensor_tensor(sq[:, m, :], bank[m][:, 0:TOK], rstd2[:], ALU.mult).then_inc(bank_free[m], 1)
                    for m in range(4):
                        dve.wait_ge(bank_free[m], G + 2)
                        V.tensor_tensor(X[:, 4 * g + m, :], sq[:, m, :], X[:, 4 * g + m, :], ALU.add
                                        ).then_inc(xadd_ok, 1)
                    dve.wait_ge(xadd_ok, q * 16 + (4 * g + 4))
                    if last:
                        rms_tiles("rms3", g, V_FIN, KT)

            mlp_in(0)
            reciprocal_root("rms2", misc[0], RMS_EPS, n_mean["rms2"])
            step(V.tensor_tensor(rstd2[:], rstd[:], rstd[:], ALU.mult))
            mlp_out(0)
            with dve.Fori(1, 3) as q:
                mlp_in(q)
                mlp_out(q)
            mlp_in(3)
            mlp_out(3, last=True)

            def read_out(i):
                G, first = G_PROJ + i, 4 * PROJ_ORDER[i]
                for m in range(4):
                    dve.wait_ge(bank_done[m], G + 1)
                    V.tensor_tensor(proj[:, first + m, :], bank[m][:, 0:TOK], rstd[:], ALU.mult
                                    ).then_inc(bank_free[m], 1)
                for m in range(4):
                    dve.wait_ge(bank_free[m], G + 2)
                dve.sem_inc(proj_ok, 4)

            def accumulate(b, heads, fill, before=0):
                nk = P * (b + 1)
                per = 512 // nk
                for i, h in enumerate(heads):
                    n = fill + i // per
                    dve.wait_ge(idx_rel, n + 1)
                    if before + i:
                        dve.wait_ge(idx_acc, IDX_HEADS * (1 - b) + before + i)
                    V.scalar_tensor_tensor(score[:, 0:nk], misc[n % 4][:, (i % per) * nk:(i % per + 1) * nk],
                                           widx[:, b, h:h + 1], score[:, 0:nk] if before + i else causal(b),
                                           ALU.mult, ALU.add).then_inc(idx_acc, 1)

            def causal(b):
                return cst[:, C_CAUSAL + b * TOK:C_CAUSAL + b * TOK + P * (b + 1)]

            def keep_best(b):
                nk = P * (b + 1)
                dve.wait_ge(idx_acc, IDX_HEADS * (NT - b))
                src = score
                for _ in range(TOPK // 8):
                    step(V.max(top8[:], src[:, 0:nk]))
                    step(V.match_replace(work[:, 0:nk], top8[:], src[:, 0:nk], TAKEN))
                    src = work
                step(V.tensor_scalar(keep[:, b, 0:nk], work[:, 0:nk], TAKEN / 2, NEG, ALU.is_gt, ALU.mult))
                step(V.tensor_tensor(keep[:, b, 0:nk], keep[:, b, 0:nk], causal(b), ALU.add))

            reciprocal_root("rms3", misc[0], RMS_EPS, n_mean["rms3"])
            read_out(0)
            for k in range(KT):
                V.scalar_tensor_tensor(X[:, k, :], X[:, k, :], VT[:, V_FIN + k:V_FIN + k + 1], rstd[:],
                                       ALU.mult, ALU.mult).then_inc(n_out["rms3"], 1)
            step(V.memset(pbuf[:], 0.0))
            read_out(1)
            dve.wait_ge(tail_ok, 2)
            dve.wait_ge(cst2_in, 16)
            accumulate(1, same_rows(0, 8, 2), 0)
            read_out(2)
            accumulate(1, same_rows(8, 8, 2), 4, 8)
            keep_best(1)
            read_out(3)
            accumulate(0, same_rows(0, IDX_HEADS, 4), 8)
            keep_best(0)
            read_out(4)
            for g, w in enumerate(WINDOWS):
                v = proj[:, 2 * g:2 * g + 2, :]
                src, d = 0, 1
                step(V.tensor_copy(pbuf[:, 0, :, 16:16 + TOK], v))
                while d < w:
                    step(V.tensor_tensor(pbuf[:, 1 - src, :, 16:16 + TOK], pbuf[:, src, :, 16:16 + TOK],
                                         pbuf[:, src, :, 16 - d:16 - d + TOK], ALU.add))
                    src, d = 1 - src, 2 * d
                step(V.tensor_tensor(pbuf[:, src, :, 16:16 + TOK], pbuf[:, src, :, 16:16 + TOK],
                                     over_tiles(cst[:, C_CNT + g * TOK:C_CNT + (g + 1) * TOK], 2), ALU.mult))
                V.tensor_tensor(v, pbuf[:, src, :, 16:16 + TOK], v, ALU.subtract).then_inc(pooled_ok, 1)
                dve.wait_ge(pooled_ok, g + 1)
                if g == 1:
                    read_out(5)
            read_out(6)
            read_out(7)

            def softmax_in(b, fills):
                nk, l = P * (b + 1), L[b][:]
                per = 512 // nk
                for h in range(HEADS):
                    dve.wait_ge(lg_ps, fills + h // per + 1)
                    V.scalar_tensor_tensor(L[b][:, h, :], misc[h // per][:, (h % per) * nk:(h % per + 1) * nk],
                                           P ** -0.5, BT[:, h, TOK - nk:TOK], ALU.mult, ALU.add).then_inc(lg_ok, 1)
                dve.wait_ge(lg_ok, HEADS * (NT - b))
                step(V.tensor_tensor(l, l, over_tiles(keep[:, b, 0:nk], HEADS), ALU.add))
                step(V.tensor_reduce(stat[:, 0, :], l, AX, ALU.max))
                V.tensor_tensor(l, l, stat[:, 0, :].unsqueeze(2).broadcast_to([P, HEADS, nk]), ALU.subtract
                                ).then_inc(cen_ok, 1)

            def softmax_out(b):
                nk, l = P * (b + 1), L[b][:]
                dve.wait_ge(exp_ok, NT - b)
                step(V.tensor_reduce(stat[:, 1, :], l, AX, ALU.add))
                step(V.reciprocal(stat[:, 1, :], stat[:, 1, :]))
                V.tensor_tensor(l, l, stat[:, 1, :].unsqueeze(2).broadcast_to([P, HEADS, nk]), ALU.mult
                                ).then_inc(prob_ok, 1)

            dve.wait_ge(BT_in, 16 * HEADS)
            softmax_in(1, 0)
            read_out(8)
            softmax_out(1)
            softmax_in(0, 4)
            softmax_out(0)
            read_out(9)
            for p in range(2):
                dve.wait_ge(pm_hi, p + 1)
                V.tensor_tensor(A_lo[:, 4 * p:4 * p + 4, :], proj[:, 4 * p:4 * p + 4, :],
                                A_hi[:, 4 * p:4 * p + 4, :].bitcast(F32), ALU.subtract).then_inc(mix_op, 2)
            for n, (b, i) in enumerate(((1, 0), (0, 0), (1, 1), (0, 1))):
                dve.wait_ge(att_hi, n + 1)
                hs = slice(8 + 4 * i, 12 + 4 * i)
                V.tensor_tensor(A_lo[:, hs, b * P:(b + 1) * P], misc[n][:].rearrange("p (i q) -> p i q", i=4),
                                A_hi[:, hs, b * P:(b + 1) * P].bitcast(F32), ALU.subtract).then_inc(att_lo, 1)
                if n % 2:
                    dve.wait_ge(att_lo, n + 1)
                    dve.sem_inc(mix_op, 2)

            step(V.memset(mix_sum[:], 0.0))
            with dve.Fori(0, 4) as g:
                for m in range(4):
                    dve.wait_ge(bank_done[m], g + (G_MIX + 1))
                    xk = X[:, bass.ds(4 * g + m, 1), :].rearrange("p o t -> p (o t)")
                    V.scalar_tensor_tensor(xk, xk, ALPHA, bank[m][:, 0:TOK], ALU.mult, ALU.add
                                           ).then_inc(bank_free[m], 1)
                for m in range(4):
                    xk = X[:, bass.ds(4 * g + m, 1), :].rearrange("p o t -> p (o t)")
                    dve.wait_ge(bank_free[m], g + (G_MIX + 2))
                    if m:
                        dve.wait_ge(sum_ok, 4 * g + m)
                    V.tensor_tensor(mix_sum[:], xk, mix_sum[:], ALU.add).then_inc(sum_ok, 1)
                dve.wait_ge(sum_ok, 4 * g + 4)
            centre("ln1", X)
            reciprocal_root("ln1", misc[1], LN_EPS, n_var["ln1"])
            for p in range(4):
                step(V.tensor_tensor(X[:, 4 * p:4 * p + 4, :], X[:, 4 * p:4 * p + 4, :], over_tiles(rstd[:], 4),
                                     ALU.mult))
                for k in range(4 * p, 4 * p + 4):
                    V.tensor_scalar(X[:, k, :], X[:, k, :], VT[:, V_L1G + k:V_L1G + k + 1],
                                    VT[:, V_L1B + k:V_L1B + k + 1], ALU.mult, ALU.add).then_inc(n_out["ln1"], 1)
                if p:
                    low_part("ln1", p - 1, X, A_hi, A_lo)
            low_part("ln1", 3, X, A_hi, A_lo)
            for r in range(8):
                dve.wait_ge(hn_ps, r + 1)
                V.tensor_copy(hnat[:, r // 4, 512 * (r % 4):512 * (r % 4) + 512], misc[r % 4][:]).then_inc(hn_ok, 1)

            def top16(vals, where, src, wk, n):
                for i in range(n):
                    step(V.max(vals(i)[:, 0:8], src(i)), hold=i == n - 1)
                for i in range(n):
                    step(V.max_index(where(i)[:, 0:8], vals(i)[:, 0:8], src(i)), hold=False)
                    step(V.match_replace(wk(i), vals(i)[:, 0:8], src(i), TAKEN), hold=i == n - 1)
                for i in range(n):
                    step(V.max(vals(i)[:, 8:16], wk(i)), hold=i == n - 1)
                for i in range(n):
                    step(V.max_index(where(i)[:, 8:16], vals(i)[:, 8:16], wk(i)), hold=i == n - 1)

            def choose(t, g):
                dve.wait_ge(key_ok, 2 * g + t + 1)
                top16(lambda i: val16[:, i, :], lambda i: pos16[:, i, :], lambda i: s_sc[t][:, 4 * g + i, :],
                      lambda i: s_wk[:, i, :], 4)
                step(V.tensor_copy(posf[:], pos16[:]), hold=False)
                v = val16[:].rearrange("p (h s) i -> p h s i", s=2)
                four = [P, 2, 16, 16]
                step(V.tensor_tensor(cand[:].rearrange("p h (i j) -> p h i j", i=16),
                                     v[:, :, 0, :].unsqueeze(3).broadcast_to(four),
                                     v[:, :, 1, :].unsqueeze(2).broadcast_to(four), ALU.add))
                top16(lambda h: best[:, 16 * h:16 * h + 16], lambda h: bpos[:, 16 * h:16 * h + 16],
                      lambda h: cand[:, h, :], lambda h: cwork[:, h, :], 2)
                step(V.tensor_scalar(bij[:, 0, :], bpos[:], 4, None, ALU.logical_shift_right), hold=False)
                step(V.tensor_scalar(bij[:, 1, :], bpos[:], 15, None, ALU.bitwise_and))
                step(V.tensor_copy(bijf[:], bij[:]))
                step(V.tensor_tensor(onehot[:], bijf[:].unsqueeze(3).broadcast_to([P, 2, 32, 16]),
                                     cst[:, C_IOTA:C_IOTA + 16].unsqueeze(1).unsqueeze(1).broadcast_to([P, 2, 32, 16]),
                                     ALU.is_equal))
                pf = posf[:].rearrange("p (h s) i -> p h s i", s=2)
                for s in range(2):
                    oh = onehot[:, s].rearrange("p (h k) i -> p h k i", h=2)
                    step(V.tensor_tensor(oh, oh, pf[:, :, s, :].unsqueeze(2).broadcast_to(four), ALU.mult), hold=s)
                mine = slice(32 * g, 32 * g + 32)
                step(V.tensor_reduce(eijs[:, t, :, mine], onehot[:], AX, ALU.add))
                step(V.scalar_tensor_tensor(eidf[:], eijs[:, t, 0, mine], float(KEYS), eijs[:, t, 1, mine],
                                            ALU.mult, ALU.add))
                V.tensor_copy(eid[:, t, mine], eidf[:]).then_inc(eid_ok, 1)
                b3 = best[:].rearrange("p (h k) -> p h k", k=16)
                step(V.tensor_tensor(gate[:, t, mine].rearrange("p (h k) -> p h k", k=16), b3,
                                     b3[:, :, 0:1].broadcast_to([P, 2, 16]), ALU.subtract))

            def gates(t):
                g3 = gate[:, t, :].rearrange("p (h k) -> p h k", k=16)
                dve.wait_ge(gexp_ok, t + 1)
                step(V.tensor_reduce(gsum[:, t, :], g3, AX, ALU.add))
                step(V.reciprocal(gsum[:, t, :], gsum[:, t, :]))
                step(V.tensor_tensor(g3, g3, gsum[:, t, :].unsqueeze(2).broadcast_to([P, PEER_HEADS, 16]), ALU.mult))

            for g in range(4):
                for m in range(4):
                    dve.wait_ge(bank_done[m], G_QRY + g + 1)
                    V.tensor_copy(qh[:, 4 * g + m, :], bank[m][:, 0:TOK]).then_inc(bank_free[m], 1)
                if g:
                    choose(0, g - 1)
            choose(0, 3)
            dve.sem_inc(gcen_ok, 1)

            rounds = SLOTS // RING

            def expert_dots(t, first, n, also=None):
                with dve.Fori(first, first + n) as r:
                    N = r + t * rounds
                    for j in range(RING):
                        dve.wait_ge(row_in[j], 16 * N + 16)
                        V.tensor_tensor_reduce(out=rows[:, j, :], in0=rows[:, j, :], in1=hnat[:, t, :], scale=1.0,
                                               scalar=0.0, op0=ALU.mult, op1=ALU.add, accum_out=dring[:, j:j + 1]
                                               ).then_inc(row_used, 1)
                    dve.wait_ge(row_used, N * RING + 2 * RING)
                    V.tensor_scalar(dots[:, t, bass.ds(r * RING, RING)], dring[:], 1.0, None, ALU.mult
                                    ).then_inc(dots_ok, 1)
                    dve.wait_ge(dots_ok, N + 1)
                    if also:
                        also(r)

            iota = cst[:, C_IOTA:C_IOTA + KEYS]

            def one_hots(t):
                def work(r):
                    for h in range(2):
                        q = 2 * r + (h + 32 * t)
                        dve.wait_ge(quad_ps, q + 1)
                        V.tensor_tensor(onej[:, h], iota.unsqueeze(1).broadcast_to([P, 4, KEYS]),
                                        keyT[:, t, 1, bass.ds(8 * r + 4 * h, 4)].unsqueeze(2)
                                        .broadcast_to([P, 4, KEYS]), ALU.is_equal).then_inc(oh_ok, 1)
                        for i in range(4):
                            V.tensor_scalar(onei[:, h, i, :], iota,
                                            keyT[:, t, 0, bass.ds(8 * r + (4 * h + i), 1)],
                                            coefT[:, t, bass.ds(8 * r + (4 * h + i), 1)],
                                            ALU.is_equal, ALU.mult).then_inc(oh_ok, 1)
                return work

            def coefficients(t):
                dve.wait_ge(gelu_ok, t + 1)
                V.tensor_tensor(coef[:, t, :], gelu[:, t, :], gate[:, t, :], ALU.mult).then_inc(coef_ok, 1)
                dve.wait_ge(coef_ok, t + 1)
                dve.wait_ge(coefT_ok, t + 1)

            for g in range(4):
                expert_dots(0, g * rounds // 4, rounds // 4)
                choose(1, g)
            gates(0)
            dve.sem_inc(gcen_ok, 1)
            coefficients(0)
            expert_dots(1, 0, rounds, also=one_hots(0))
            gates(1)
            coefficients(1)
            with dve.Fori(0, rounds) as r:
                one_hots(1)(r)
            step(V.tensor_scalar(mixed[:], hnat[:], ALPHA, None, ALU.mult))

            for t in range(NT):
                with dve.Fori(t * rounds, (t + 1) * rounds) as R:
                    N = R + NT * rounds
                    for u in range(4):
                        dve.wait_ge(ghi_ok, 4 * R + (u + 1))
                        V.tensor_tensor(g_lo[:, u % 2], wmat[:, :, bass.ds(4 * R + u, 1), :]
                                        .rearrange("p t o n -> p t (o n)"), g_hi[:, u % 2].bitcast(F32),
                                        ALU.subtract).then_inc(glo_ok, 1)
                        for c in (1, 2):
                            n = 3 * u + c
                            dve.wait_ge(vhi_ok, 12 * R + (n + 1))
                            V.tensor_tensor(v_lo[:, n % 4], v_raw[:, u % 2, c], v_hi[:, n % 4].bitcast(F32),
                                            ALU.subtract).then_inc(vlo_dve, 1)
                        for j in (2 * u, 2 * u + 1):
                            dve.wait_ge(row_in[j], 16 * N + 16)
                            dve.wait_ge(row_used, N * RING + (RING + j))
                            V.scalar_tensor_tensor(mixed[:, t, DENSE:D], vrows[:, j, :],
                                                   coef[:, t, bass.ds((R - t * rounds) * RING + j, 1)],
                                                   mixed[:, t, DENSE:D], ALU.mult, ALU.add).then_inc(row_used, 1)

            dve.wait_ge(row_used, (NT + 2) * rounds * RING + RING)
            dve.wait_ge(piece_used, 4 + KEYS * PIECES)
            dve.wait_ge(gb_in, 32)
            for t in range(NT):
                for c, b in enumerate(((bank[0], bank[1], misc[0]), (bank[2], bank[3], misc[1]))[t]):
                    cols = slice(c * PIECE, (c + 1) * PIECE)
                    step(V.tensor_tensor(mixed[:, t, cols], mixed[:, t, cols], b[:], ALU.add), hold=c == PIECES - 1)
                f = fstat[:, t, :]
                for c in range(4):
                    step(V.bn_stats(bn[:, t, c, :], mixed[:, t, 512 * c:512 * c + 512]), hold=c == 3)
                step(V.bn_aggr(f[:, 0:2], bn[:, t]))
                V.tensor_scalar(f[:, 2:3], f[:, 1:2], LN_EPS, None, ALU.add).then_inc(var_ok, 1)
                dve.wait_ge(rt_ok, t + 1)
                step(V.reciprocal(f[:, 4:5], f[:, 3:4]))
                for half in range(2):
                    cols = slice(half * D // 2, (half + 1) * D // 2)
                    step(V.tensor_scalar(y[:, t, cols], mixed[:, t, cols], f[:, 0:1], f[:, 4:5],
                                         ALU.subtract, ALU.mult))
                    step(V.tensor_tensor(y[:, t, cols], y[:, t, cols], gb[:, 0, cols], ALU.mult))
                    V.tensor_tensor(y[:, t, cols], y[:, t, cols], gb[:, 1, cols], ALU.add).then_inc(y_ok, 1)


def shape_table():
    import numpy as np

    t = np.zeros((P, C_END), np.float32)
    p, s = np.arange(P)[:, None], np.arange(TOK)[None, :]
    t[:, C_ID:C_ID + P] = np.eye(P)
    t[:, C_ONE:C_ONE + P] = 1.0 / D
    for b in range(NT):
        t[:, C_CAUSAL + b * TOK:C_CAUSAL + (b + 1) * TOK] = np.where(s <= p + b * P, 0.0, NEG)
    for g, w in enumerate(WINDOWS):
        t[:, C_CNT + g * TOK:C_CNT + (g + 1) * TOK] = 1.0 / np.minimum(s + 1, w)
    dist = np.maximum(TOK - 1 - np.arange(384), 0)
    exact = BUCKETS // 2
    far = exact + (np.log(np.maximum(dist, 1) / exact) / np.log(128 / exact) * (BUCKETS - exact)).astype(np.int32)
    bucket = np.where(dist < exact, dist, np.minimum(far, BUCKETS - 1))
    t[0:BUCKETS, C_HOT:C_HOT + 384] = bucket[None, :] == np.arange(BUCKETS)[:, None]
    t[:, C_IOTA:C_IOTA + KEYS] = np.arange(KEYS)
    return t


_INS = {"x": "x", "norm1_g": "norm1_g", "norm2_g": "norm2_g", "mlp_w1": "mlp_w1", "mlp_w2": "mlp_w2",
        "cc_w_in": "cc_w_in", "cc_b_in": "cc_b_in", "cc_dw": "cc_dw", "cc_dw_b": "cc_dw_b", "cc_ln_g": "cc_ln_g",
        "cc_ln_b": "cc_ln_b", "cc_w_out": "cc_w_out", "cc_b_out": "cc_b_out", "final_g": "final_g",
        "w_in_2": "w_in_2", "pool_w_2": "pool_w", "pool_scale_2": "pool_scale", "rel_bias_2": "rel_bias",
        "w_out_2": "w_out_2", "ln1_g_2": "ln1_g", "ln1_b_2": "ln1_b", "peer_wq_2": "peer_wq",
        "peer_subkeys_2": "peer_subkeys", "peer_u_2": "peer_u", "peer_v_2": "peer_v", "ln2_g_2": "ln2_g",
        "ln2_b_2": "ln2_b"}


def kernel(**inputs):
    import numpy as _np
    import concourse.bacc as _bacc
    from concourse import mybir as _mybir
    from concourse.bass_utils import run_bass_kernel_spmd as _run

    nc = _bacc.Bacc("TRN2", target_bir_lowering=False, num_devices=1)
    arrays, args = {}, {}
    for name, short in _INS.items():
        arr = _np.ascontiguousarray(inputs[name])
        arrays[f"in_{name}"] = arr
        args[short] = nc.dram_tensor(f"in_{name}", arr.shape, _mybir.dt.from_np(arr.dtype), kind="ExternalInput").ap()
    table = shape_table()
    arrays["in_table"] = table
    args["table"] = nc.dram_tensor("in_table", table.shape, F32, kind="ExternalInput").ap()
    out = nc.dram_tensor("out_0", (1, TOK, D), F32, kind="ExternalOutput").ap()
    build(nc, args, out)
    r = _run(nc, [arrays], core_ids=[0])
    return r.results[0]["out_0"]
```
